# Optimizing a Trainium2 kernel written in Bass

```python
import math
import jax, jax.numpy as jnp
from jax import lax
import numpy as np

D_MODEL = 1024
BATCH = 1
SEQ = 512
DEPTH = 2

MLA_HEADS = 8
Q_LORA = 384
KV_LORA = 256
QK_NOPE = 64
QK_ROPE = 32
QK_HEAD = QK_NOPE + QK_ROPE
V_HEAD = 64
MLA_WIDTH = MLA_HEADS * V_HEAD
ROPE_BASE = 10000.0
Q_BLOCK = 128
POOL_WINDOWS = (2, 4, 8, 16)
POOL_GROUPS = len(POOL_WINDOWS)
POOL_WIDTH = 512
POOL_GC = POOL_WIDTH // POOL_GROUPS
N_BRANCHES = 2
IN_SPLITS = (Q_LORA, KV_LORA, QK_ROPE, POOL_WIDTH, N_BRANCHES * D_MODEL)
IN_WIDTH = sum(IN_SPLITS)
PEER_HEADS = 8
N_KEYS = 128
N_EXPERTS = N_KEYS * N_KEYS
PEER_KEY_DIM = 256
PEER_HALF = PEER_KEY_DIM // 2
PEER_TOPK = 16
PEER_CHUNK = 128
RMS_EPS = 1e-6

kernel_name = "hybrid_mla_pool_peer_encoder"

def rms_norm(x, g):
    xf = x.astype(jnp.float32)
    y = xf * lax.rsqrt(jnp.mean(xf * xf, axis=-1, keepdims=True) + RMS_EPS)
    return (y * g.astype(jnp.float32)).astype(x.dtype)

def rope_cos_sin(positions):
    inv = ROPE_BASE ** (-jnp.arange(0, QK_ROPE, 2, dtype=jnp.float32) / QK_ROPE)
    ang = positions.astype(jnp.float32)[..., None] * inv
    return jnp.cos(ang), jnp.sin(ang)

def apply_rope(x, cos, sin):
    cos = cos.astype(x.dtype)
    sin = sin.astype(x.dtype)
    x1, x2 = jnp.split(x, 2, axis=-1)
    return jnp.concatenate([x1 * cos - x2 * sin, x1 * sin + x2 * cos], axis=-1)

def block_attention(q, k, v):
    B, S, H, Dh = q.shape
    nb = S // Q_BLOCK
    scale = 1.0 / math.sqrt(Dh)
    qb = q.reshape(B, nb, Q_BLOCK, H, Dh).transpose(1, 0, 2, 3, 4)

    def one(qblk):
        s = jnp.einsum('bqhd,bkhd->bhqk', qblk, k).astype(jnp.float32) * scale
        p = jax.nn.softmax(s, axis=-1).astype(v.dtype)
        return jnp.einsum('bhqk,bkhd->bqhd', p, v)

    o = lax.map(one, qb)
    return o.transpose(1, 0, 2, 3, 4).reshape(B, S, H * V_HEAD)

def mla_branch(c_q, c_kv, k_pe, cos, sin, q_lora_g, kv_lora_g, w_uq, w_ukv, q_head_g, k_head_g, w_o):
    B, S, _ = c_q.shape
    q = (rms_norm(c_q, q_lora_g) @ w_uq).reshape(B, S, MLA_HEADS, QK_HEAD)
    q_nope, q_pe = q[..., :QK_NOPE], q[..., QK_NOPE:]
    q_pe = apply_rope(q_pe, cos[:, :, None, :], sin[:, :, None, :])
    kv = (rms_norm(c_kv, kv_lora_g) @ w_ukv).reshape(B, S, MLA_HEADS, QK_NOPE + V_HEAD)
    k_nope, v = kv[..., :QK_NOPE], kv[..., QK_NOPE:]
    k_pe = apply_rope(k_pe, cos, sin)
    k_pe = jnp.broadcast_to(k_pe[:, :, None, :], (B, S, MLA_HEADS, QK_ROPE))
    q = rms_norm(jnp.concatenate([q_nope, q_pe], axis=-1), q_head_g)
    k = rms_norm(jnp.concatenate([k_nope, k_pe], axis=-1), k_head_g)
    o = block_attention(q, k, v)
    return o @ w_o

def pool_branch(p, pool_w, pool_scale, w_pool_out):
    B, S, _ = p.shape
    pf = p.reshape(B, S, POOL_GROUPS, POOL_GC).astype(jnp.float32)
    cs = jnp.concatenate([jnp.zeros((B, 1, POOL_GROUPS, POOL_GC), jnp.float32),
                          jnp.cumsum(pf, axis=1)], axis=1)
    half = jnp.array(POOL_WINDOWS, dtype=jnp.int32) // 2
    t = jnp.arange(S, dtype=jnp.int32)[:, None]
    lo = jnp.clip(t - half[None, :], 0, S)
    hi = jnp.clip(t + half[None, :], 0, S)
    gidx = jnp.arange(POOL_GROUPS, dtype=jnp.int32)[None, :]
    win_sum = cs[:, hi, gidx] - cs[:, lo, gidx]
    count = (hi - lo).astype(jnp.float32)[None, :, :, None]
    mixed = (win_sum / count - pf).astype(p.dtype)
    y = jnp.einsum('bsgc,gcd->bsgd', mixed, pool_w).reshape(B, S, POOL_WIDTH) * pool_scale
    return y @ w_pool_out

def peer_ffn(xn, wq, sub_keys, expert_u, expert_v):
    B, S, D = xn.shape
    xc = xn.reshape((B * S) // PEER_CHUNK, PEER_CHUNK, D)
    K = PEER_TOPK

    def one(x):
        C = x.shape[0]
        q = (x @ wq).reshape(C, PEER_HEADS, 2, PEER_HALF)
        s = jnp.einsum('chpk,hpnk->chpn', q, sub_keys).astype(jnp.float32)
        top_s, top_i = lax.top_k(s, K)
        cand = top_s[:, :, 0, :, None] + top_s[:, :, 1, None, :]
        best_s, best_j = lax.top_k(cand.reshape(C, PEER_HEADS, K * K), K)
        i1 = jnp.take_along_axis(top_i[:, :, 0], best_j // K, axis=-1)
        i2 = jnp.take_along_axis(top_i[:, :, 1], best_j % K, axis=-1)
        e = i1 * N_KEYS + i2
        g = jax.nn.softmax(best_s, axis=-1).astype(x.dtype)
        u = jnp.take(expert_u, e, axis=0)
        h = jax.nn.gelu(jnp.einsum('cd,chkd->chk', x, u))
        v = jnp.take(expert_v, e, axis=0)
        return jnp.einsum('chk,chkd->cd', g * h, v)

    return lax.map(one, xc).reshape(B, S, D)

def setup_inputs(seed: int = 0) -> dict:
    key = jax.random.key(seed)
    ks = jax.random.split(key, 24)
    f32 = jnp.float32

    def nrm(k, shape, scale):
        return jax.random.normal(k, shape, f32) * scale

    def gain(k, shape):
        return 1.0 + 0.1 * jax.random.normal(k, shape, f32)

    L = DEPTH
    x = jax.random.normal(ks[0], (BATCH, SEQ, D_MODEL), f32)
    offsets = jax.random.randint(ks[1], (BATCH, 1), 0, 4096, dtype=jnp.int32)
    positions = jnp.arange(SEQ, dtype=jnp.int32)[None, :] + offsets
    return {
        "x": x,
        "positions": positions,
        "norm1_g": gain(ks[2], (L, D_MODEL)),
        "w_in": nrm(ks[3], (L, D_MODEL, IN_WIDTH), D_MODEL ** -0.5),
        "q_lora_g": gain(ks[4], (L, Q_LORA)),
        "kv_lora_g": gain(ks[5], (L, KV_LORA)),
        "w_uq": nrm(ks[6], (L, Q_LORA, MLA_HEADS * QK_HEAD), Q_LORA ** -0.5),
        "w_ukv": nrm(ks[7], (L, KV_LORA, MLA_HEADS * (QK_NOPE + V_HEAD)), KV_LORA ** -0.5),
        "q_head_g": gain(ks[8], (L, QK_HEAD)),
        "k_head_g": gain(ks[9], (L, QK_HEAD)),
        "w_o_mla": nrm(ks[10], (L, MLA_WIDTH, D_MODEL), MLA_WIDTH ** -0.5),
        "pool_w": nrm(ks[11], (L, POOL_GROUPS, POOL_GC, POOL_GC), POOL_GC ** -0.5),
        "pool_scale": gain(ks[12], (L, POOL_WIDTH)),
        "w_pool_out": nrm(ks[13], (L, POOL_WIDTH, D_MODEL), POOL_WIDTH ** -0.5),
        "gate_bias": nrm(ks[14], (L, N_BRANCHES, D_MODEL), 0.1),
        "w_out": nrm(ks[15], (L, D_MODEL, D_MODEL), D_MODEL ** -0.5),
        "norm2_g": gain(ks[16], (L, D_MODEL)),
        "peer_wq": nrm(ks[17], (L, D_MODEL, PEER_HEADS * PEER_KEY_DIM), D_MODEL ** -0.5),
        "peer_keys": nrm(ks[18], (L, PEER_HEADS, 2, N_KEYS, PEER_HALF), PEER_HALF ** -0.5),
        "peer_u": nrm(ks[19], (L, N_EXPERTS, D_MODEL), D_MODEL ** -0.5),
        "peer_v": nrm(ks[20], (L, N_EXPERTS, D_MODEL), PEER_HEADS ** -0.5),
    }

def reference(x, positions, norm1_g, w_in, q_lora_g, kv_lora_g, w_uq, w_ukv, q_head_g, k_head_g,
              w_o_mla, pool_w, pool_scale, w_pool_out, gate_bias, w_out, norm2_g,
              peer_wq, peer_keys, peer_u, peer_v):
    B, S, D = x.shape
    cos, sin = rope_cos_sin(positions)
    cuts = list(np.cumsum(IN_SPLITS)[:-1])
    for l in range(DEPTH):
        xn = rms_norm(x, norm1_g[l])
        c_q, c_kv, k_pe, p, g_logits = jnp.split(xn @ w_in[l], cuts, axis=-1)
        a = mla_branch(c_q, c_kv, k_pe, cos, sin, q_lora_g[l], kv_lora_g[l], w_uq[l], w_ukv[l],
                       q_head_g[l], k_head_g[l], w_o_mla[l])
        b = pool_branch(p, pool_w[l], pool_scale[l], w_pool_out[l])
        gates = jax.nn.sigmoid((g_logits.reshape(B, S, N_BRANCHES, D) + gate_bias[l]).astype(jnp.float32)).astype(x.dtype)
        mix = gates[:, :, 0] * a + gates[:, :, 1] * b
        x = x + mix @ w_out[l]
        x = x + peer_ffn(rms_norm(x, norm2_g[l]), peer_wq[l], peer_keys[l], peer_u[l], peer_v[l])
    return x


_drawn_inputs = setup_inputs


def setup_inputs(seed=0):
    import zlib

    import numpy as np

    out = dict(_drawn_inputs(seed))
    spreads = {}
    factors = {}
    for name, (base, spread) in spreads.items():
        noise = np.random.default_rng([zlib.crc32(name.encode()), seed]).standard_normal(out[name].shape)
        drawn = base * np.exp(spread * noise) if base else spread * noise
        out[name] = __import__('jax').numpy.asarray(drawn.astype(out[name].dtype))
    for name, factor in factors.items():
        out[name] = (out[name] * factor).astype(out[name].dtype)
    return out
```

```python
from contextlib import ExitStack

import numpy as np

import concourse.bass as bass
from concourse import mybir

ACT = mybir.ActivationFunctionType
ALU = mybir.AluOpType
AX = mybir.AxisListType.X
F32 = mybir.dt.float32
F32R = mybir.dt.float32r
U32 = mybir.dt.uint32
I32 = mybir.dt.int32

P = 128
LAYERS = 2
SEQ = 512
D = 1024
TT = SEQ // P
KD = D // P
HEADS, NOPE, ROPE, VH = 8, 64, 32, 64
QK = NOPE + ROPE
HALF = ROPE // 2
Q_LORA, KV_LORA = 384, 256
QT_, KVT = Q_LORA // P, KV_LORA // P
GROUPS = 4
PAD = 8
NK = 128
TOPK = 16
PH = 8
EPS = 1e-6

J_C, J_P, J_KPE, J_POOL, J_GATE = 0, 5, 9, 10, 11
J_WPO, J_UQ, J_UKV, J_WO, J_WOUT, J_WQ, J_U = 27, 31, 34, 36, 40, 48, 64
JOBS = J_U + NK

V_N1, V_N2, V_QG, V_KVG, V_PS, V_GB, V_QH, V_KH, V_ALL = 0, 8, 16, 19, 21, 25, 41, 42, 43

TB = 64
NTB = SEQ // TB

PER = dict(
    vectors_loaded=16, keys_loaded=16, block_loaded0=16 * JOBS // 2, block_loaded1=16 * JOBS // 2,
    high_part=JOBS, low_part=JOBS, block_used=JOBS, squares_summed=2, variance_inverted=2, rms_ready=2,
    rows_normed=2, norm_transposed=2 * KD, norm_high=2 * KD, norm_low=2 * KD, taken_by_act=36,
    taken_by_dve=14, latent_squared=5, latent_summed=1, latent_variance=1, latent_rms=1, window_means=1,
    pool_high=4, pool_low=4, qkv_product=8, qkv_taken=8, heads_variance=1, heads_rms=1, head_sliced=8,
    head_transposed=8, head_ready=8, head_scores=32, head_max=32, head_exp=32, probs_transposed=32,
    probs_taken=32, head_output=8, head_stored=8, attn_transposed=4, attn_high=4, attn_low=4, mix_full=8,
    mix_high=8, key_scores=16, key_scores_taken=16, best_shifted=1, best_exp=1, choice_ready=1,
    choice_transposed=3, onehots_ready=128, routed=128, routing_taken=128, routing_stored0=64,
    routing_stored1=64, v_loaded0=1024, v_loaded1=1024, v_high=128, v_low=128, gelu_done=128, weighted=128,
    weighted_high=128, weighted_low=128, routing_loaded0=512, routing_loaded1=512, output_product=512,
    residual_added=8 + 512,
)

FROM_ONE = ("low_part", "block_used", "residual_added", "weighted", "v_low", "head_stored", "key_scores", "routing_stored0", "routing_stored1", "output_product")


def program(nc, x, pos, inv_freq, ident, edge, vecs, stream, peer_keys, peer_u, peer_v, out):
    route = nc.dram_tensor("route_dram", [NTB, P, NK, TB], F32, kind="Internal").ap()
    ctx = ExitStack()
    with ctx:
        def sb(name, shape, dt=F32):
            return ctx.enter_context(nc.sbuf_tensor(name, shape, dt))

        X = sb("X", [P, TT, D])
        XH = sb("XH", [P, KD, SEQ], F32R)
        XL = sb("XL", [P, KD, SEQ], F32R)
        RAW = sb("RAW", [P, 2, 1024])
        RH = sb("RH", [P, 4, 1024], F32R)
        RL = sb("RL", [P, 4, 1024], F32R)
        IDN = sb("IDN", [P, P])
        IOTA = sb("IOTA", [P, P])
        ONES = sb("ONES", [P, 1])
        EDGE = sb("EDGE", [P, GROUPS, 2, PAD])
        VEC = sb("VEC", [P, V_ALL])
        COS = sb("COS", [P, TT, HALF])
        SIN = sb("SIN", [P, TT, HALF])
        NRM = sb("NRM", [P, 3, TT])
        CN = sb("CN", [P, 3, 8])
        GQS = sb("GQS", [P, 1])

        size = 117 * 1024
        sb("arena", [P, size // 4])
        start = nc.sbuf_base - size

        def at(name, offset, shape, dt=F32):
            n = 4
            for s in shape[1:]:
                n *= s
            assert offset + n <= size, name
            return nc.alloc_sbuf_tensor_at(name, shape, dt, offset=start + offset)

        K = 1024
        CH = at("CH", 0, [P, 5, SEQ], F32R)
        CL = at("CL", 10 * K, [P, 5, SEQ], F32R)
        SQT = at("SQT", 0, [P, TT * HEADS, QK])
        ROT = at("ROT", 12 * K, [P, 4, TT * HEADS * HALF])
        PR = at("PR", 0, [P, TT, SEQ])
        PT = at("PT", 8 * K, [P, TT, SEQ])
        XS = at("XS", 20 * K, [P, TT, D])
        MIXH = at("MIXH", 20 * K, [P, GROUPS, SEQ], F32R)
        MIXL = at("MIXL", 28 * K, [P, GROUPS, SEQ], F32R)
        O = at("O", 20 * K, [P, TT, SEQ])
        QTR = at("QTR", 28 * K, [P, SEQ])
        KTR = at("KTR", 30 * K, [P, SEQ])
        QSL = at("QSL", 32 * K, [P, TT, QK])
        KSL = at("KSL", 32 * K + 1536, [P, TT, QK])
        SMALL = at("SMALL", 35 * K, [P, 256])
        RQ = SMALL[:, 0:32].rearrange("p (t h) -> p t h", t=TT)
        RK = SMALL[:, 32:64].rearrange("p (t h) -> p t h", t=TT)
        NMX = SMALL[:, 64:68]
        RSM = SMALL[:, 68:72]
        RIN = SMALL[:, 72:76]
        KPS = SMALL[:, 76:80]
        ROTC = at("ROTC", 52 * K, [P, 4, TT, HALF])
        PADDED = at("PADDED", 36 * K, [P, GROUPS, SEQ + 2 * PAD])
        WA = at("WA", 36 * K + 8448, [P, SEQ + 2 * PAD])
        WB = at("WB", 36 * K + 10560, [P, SEQ + 2 * PAD])
        KV = at("KV", 36 * K, [P, TT, D])
        YH = at("YH", 52 * K, [P, GROUPS, SEQ], F32R)
        YL = at("YL", 60 * K, [P, GROUPS, SEQ], F32R)
        OH = at("OH", 52 * K, [P, GROUPS, SEQ], F32R)
        OL = at("OL", 60 * K, [P, GROUPS, SEQ], F32R)
        SQC = at("SQC", 68 * K, [P, 5, SEQ])
        GAB = at("GAB", 68 * K, [P, 2 * KD, SEQ])
        Q = at("Q", 100 * K, [P, TT, HEADS, QK])
        T2 = at("T2", 100 * K, [P, 2, SEQ])
        KPE = at("KPE", 112 * K, [P, TT, ROPE])
        KEYS = at("KEYS", 0, [P, 2 * PH * NK])
        QF = at("QF", 8 * K, [P, 2, SEQ])
        SW = at("SW", 12 * K, [P, TT, NK])
        CAND = at("CAND", 14 * K, [P, TT, 256])
        CW = at("CW", 18 * K, [P, TT, 256])
        EQ = at("EQ", 22 * K, [P, TT, TOPK, TOPK])
        EQ2 = at("EQ2", 26 * K, [P, TT, TOPK, TOPK])
        V16 = at("V16", 30 * K, [P, TT, 2, TOPK])
        I16 = at("I16", 30 * K + 512, [P, TT, 2, TOPK], U32)
        F16 = at("F16", 31 * K, [P, TT, 2, TOPK])
        B16 = at("B16", 31 * K + 512, [P, TT, TOPK])
        J16 = at("J16", 31 * K + 768, [P, TT, TOPK], U32)
        JHL = at("JHL", 32 * K, [P, 2, TT, TOPK], U32)
        JF = at("JF", 32 * K + 512, [P, 2, TT, TOPK])
        BV = at("BV", 33 * K, [P, TT, P])
        GW = at("GW", 35 * K, [P, TT, P])
        BS = at("BS", 37 * K, [P, 2, TT * PH])
        I1 = at("I1", 38 * K, [P, TT, P])
        I2 = at("I2", 40 * K, [P, TT, P])
        STAGE = [at(f"STAGE{s}", 32 * K * s, [P, NK, TB]) for s in range(2)]
        IT = at("IT", 64 * K, [P, 3, SEQ])
        OA = at("OA", 70 * K, [P, 2, 4, P])
        OB = at("OB", 74 * K, [P, 2, 4, P])
        VRAW = at("VRAW", 0, [P, 2, D])
        VHI = at("VHI", 8 * K, [P, 4, D], F32R)
        VLO = at("VLO", 24 * K, [P, 4, D], F32R)
        GC = at("GC", 40 * K, [P, 2, NTB, 2, TB])
        GEL = at("GEL", 48 * K, [P, 2, SEQ])
        WF = at("WF", 52 * K, [P, 2, SEQ])
        WHI = at("WHI", 56 * K, [P, 4, SEQ], F32R)
        WLO = at("WLO", 64 * K, [P, 4, SEQ], F32R)

        PS = ctx.enter_context(nc.psum_tensor("PS", [P, 8, 512], F32))

        sems = {n: ctx.enter_context(nc.semaphore(n)) for n in PER}
        passed = ctx.enter_context(nc.semaphore("passed"))
        mix_low = ctx.enter_context(nc.semaphore("mix_low"))
        const_in = ctx.enter_context(nc.semaphore("const_in"))
        iota_made = ctx.enter_context(nc.semaphore("iota_made"))
        trig_arg = ctx.enter_context(nc.semaphore("trig_arg"))
        trig_made = ctx.enter_context(nc.semaphore("trig_made"))
        stored = ctx.enter_context(nc.semaphore("stored"))
        S = type("Sems", (), sems)

        def count(layer, name, n):
            return layer * PER[name] + n + (name in FROM_ONE)

        def apart(engine):
            engine.sem_inc(passed, 1)

        block = ctx.enter_context(nc.Block())

        @block.sync
        def _(sp):
            sp.dma_start(X[:], x.rearrange("b (t p) d -> p (b t) d", p=P)).then_inc(const_in, 16)
            sp.dma_start(PADDED[:, 0, 0:TT].bitcast(I32), pos).then_inc(const_in, 16)
            sp.dma_start(COS[:, 0, :], inv_freq).then_inc(const_in, 16)
            sp.dma_start(IDN[:], ident).then_inc(const_in, 16)
            sp.dma_start(EDGE[:].rearrange("p g e c -> p (g e c)"), edge).then_inc(const_in, 16)
            with sp.Fori(0, LAYERS) as l:

                def load_block(src, slot):
                    sp.dma_start(RAW[:, slot, :], src).then_inc(sems[f"block_loaded{slot}"], 16)

                sp.wait_ge(S.residual_added, count(l, "residual_added", 0))
                sp.dma_start(VEC[:], vecs[l]).then_inc(S.vectors_loaded, 16)
                for j in range(4):
                    sp.wait_ge(S.low_part, count(l, "low_part", max(j - 1, 0)))
                    load_block(stream[l, j], j % 2)
                with sp.Fori(1, 12) as i:
                    for k in range(4):
                        sp.wait_ge(S.low_part, count(l, "low_part", 4 * i + k - 1))
                        load_block(stream[l, 4 * i + k], k % 2)
                for j in range(J_WQ, J_WQ + 4):
                    if j == J_WQ + 2:
                        sp.wait_ge(S.residual_added, count(l, "residual_added", 8))
                        sp.dma_start(KEYS[:], peer_keys[l]).then_inc(S.keys_loaded, 16)
                    sp.wait_ge(S.low_part, count(l, "low_part", j - 1))
                    load_block(stream[l, j], j % 2)
                with sp.Fori(13, 16) as i:
                    for k in range(4):
                        sp.wait_ge(S.low_part, count(l, "low_part", 4 * i + k - 1))
                        load_block(stream[l, 4 * i + k], k % 2)
                for c in range(2):
                    sp.wait_ge(S.low_part, count(l, "low_part", J_U + c - 1))
                    load_block(peer_u[l, c], c)
                with sp.Fori(0, NTB // 2) as i:
                    for s in range(2):
                        sp.wait_ge(S.routing_taken, count(l, "routing_taken", 32 * i + 16 * s + 16))
                        sp.dma_start(route[2 * i + s], STAGE[s][:]).then_inc(sems[f"routing_stored{s}"], 16)
                sp.wait_ge(S.routing_stored0, count(l, "routing_stored0", 64))
                apart(sp)
                sp.wait_ge(S.routing_stored1, count(l, "routing_stored1", 64))
                apart(sp)

                def chunk(it, k, last=False):
                    if k % 2 == 0:
                        g = 2 * it + k // 2
                        sp.wait_ge(S.weighted, count(l, "weighted", max(2 * g - 2, 0) if isinstance(g, int) else 2 * g - 2))
                        sp.dma_start(
                            GC[:, k // 2, :, :, :].rearrange("p b i t -> p b (i t)"),
                            route.rearrange("b p (g i) t -> p g b (i t)", i=2)[:, g],
                        ).then_inc(sems[f"routing_loaded{k // 2}"], 16)
                    if not (last and k >= 2):
                        sp.wait_ge(S.low_part, count(l, "low_part", J_U + 4 * it + k + 1))
                        load_block(peer_u[l, 4 * it + k + 2], k % 2)
                    c = 4 * it + k
                    sp.wait_ge(S.v_low, count(l, "v_low", max(c - 1, 0) if isinstance(c, int) else c - 1))
                    sp.dma_start(VRAW[:, k % 2, :], peer_v[l, :, c, :]).then_inc(sems[f"v_loaded{k % 2}"], 16)

                for k in range(4):
                    chunk(0, k)
                with sp.Fori(1, 31) as it:
                    for k in range(4):
                        chunk(it, k)
                for k in range(4):
                    chunk(31, k, last=True)
            sp.wait_ge(S.residual_added, count(LAYERS, "residual_added", 0))
            sp.dma_start(out.rearrange("b (t p) d -> p (b t) d", p=P), X[:]).then_inc(stored, 16)
            sp.wait_ge(stored, 16)

        @block.tensor
        def _(pe):
            pe.wait_ge(iota_made, 1)
            pe.wait_ge(const_in, 80)
            with pe.Fori(0, LAYERS) as l:

                def passes(acc, sh, sl, mh, ml, first, last):
                    pe.matmul(acc, sh, mh, start=first, stop=False)
                    pe.matmul(acc, sh, ml, start=False, stop=False)
                    return pe.matmul(acc, sl, mh, start=False, stop=last)

                def by_columns(bank, slot):
                    for k in range(KD):
                        w = slice(k * P, (k + 1) * P)
                        m = passes(PS[:, bank, :], RH[:, slot, w], RL[:, slot, w], XH[:, k, :], XL[:, k, :],
                                   k == 0, k == KD - 1)
                    return m

                def transpose_norm(n):
                    pe.wait_ge(S.rows_normed, count(l, "rows_normed", n + 1))
                    for k in range(KD):
                        if k >= 2:
                            pe.wait_ge(S.norm_low, count(l, "norm_low", KD * n + k - 1))
                        for t in range(TT):
                            m = pe.transpose(PS[:, k % 2, t * P:(t + 1) * P], XS[:, t, k * P:(k + 1) * P], IDN[:])
                        m.then_inc(S.norm_transposed, 1)
                    pe.wait_ge(S.norm_low, count(l, "norm_low", KD * (n + 1)))

                transpose_norm(0)
                for j in range(J_C, J_P):
                    if j >= 2:
                        pe.wait_ge(S.taken_by_dve, count(l, "taken_by_dve", j - 1))
                    pe.wait_ge(S.low_part, count(l, "low_part", j + 1))
                    by_columns(2 * (j % 2), j % 4).then_inc(S.block_used, 1)
                for j in range(J_P, J_KPE):
                    pe.wait_ge(S.taken_by_dve, count(l, "taken_by_dve", min(j - 1, 5)))
                    if j >= 7:
                        pe.wait_ge(S.taken_by_act, count(l, "taken_by_act", j - 6))
                    pe.wait_ge(S.low_part, count(l, "low_part", j + 1))
                    by_columns(2 * (j % 2), j % 4).then_inc(S.block_used, 1)
                pe.wait_ge(S.taken_by_act, count(l, "taken_by_act", 3))
                pe.wait_ge(S.low_part, count(l, "low_part", J_KPE + 1))
                for t in range(TT):
                    for k in range(KD):
                        s, tok, w = J_KPE % 4, slice(t * P, (t + 1) * P), slice(k * ROPE, (k + 1) * ROPE)
                        m = passes(PS[:, 2, t * ROPE:(t + 1) * ROPE], XH[:, k, tok], XL[:, k, tok],
                                   RH[:, s, w], RL[:, s, w], k == 0, k == KD - 1)
                m.then_inc(S.block_used, 1)
                pe.wait_ge(S.latent_squared, count(l, "latent_squared", 5))
                for t in range(TT):
                    for col, js in ((t, range(QT_)), (4 + t, range(QT_, QT_ + KVT))):
                        for j in js:
                            m = pe.matmul(PS[:, 7, col:col + 1], SQC[:, j, t * P:(t + 1) * P], ONES[:],
                                          start=j == js[0], stop=j == js[-1])
                m.then_inc(S.latent_summed, 1)
                pe.wait_ge(S.latent_summed, count(l, "latent_summed", 1))
                pe.wait_ge(S.latent_variance, count(l, "latent_variance", 1))
                pe.wait_ge(S.window_means, count(l, "window_means", 1))
                pe.wait_ge(S.low_part, count(l, "low_part", J_POOL + 1))
                for g in range(GROUPS):
                    w = slice(g * P, (g + 1) * P)
                    m = passes(PS[:, 4 + g, :], RH[:, J_POOL % 4, w], RL[:, J_POOL % 4, w],
                               MIXH[:, g, :], MIXL[:, g, :], True, True)
                m.then_inc(S.block_used, 1)
                pe.wait_ge(S.taken_by_dve, count(l, "taken_by_dve", 6))
                pe.wait_ge(S.low_part, count(l, "low_part", J_GATE + 1))
                by_columns(2, J_GATE % 4).then_inc(S.block_used, 1)
                pe.wait_ge(S.taken_by_act, count(l, "taken_by_act", 4))
                pe.wait_ge(S.low_part, count(l, "low_part", J_GATE + 2))
                by_columns(0, (J_GATE + 1) % 4).then_inc(S.block_used, 1)
                for j in range(J_GATE + 2, J_GATE + 4):
                    pe.wait_ge(S.taken_by_act, count(l, "taken_by_act", j - 8))
                    pe.wait_ge(S.low_part, count(l, "low_part", j + 1))
                    by_columns(2 * (j % 2), j % 4).then_inc(S.block_used, 1)
                with pe.Fori(0, 3) as i:
                    for k in range(4):
                        j = J_GATE + 4 + k
                        pe.wait_ge(S.taken_by_act, count(l, "taken_by_act", 4 * i + j - 8))
                        pe.wait_ge(S.low_part, count(l, "low_part", 4 * i + j + 1))
                        by_columns(2 * (j % 2), j % 4).then_inc(S.block_used, 1)
                pe.wait_ge(S.pool_low, count(l, "pool_low", 4))

                def two_tiles(j, mh, ml):
                    for h in range(2):
                        for k in range(4):
                            w = slice((h * 4 + k) * P, (h * 4 + k + 1) * P)
                            m = passes(PS[:, 2 * (j % 2) + h, :], RH[:, j % 4, w], RL[:, j % 4, w],
                                       mh[:, k, :], ml[:, k, :], k == 0, k == 3)
                    m.then_inc(S.block_used, 1)

                for j in range(J_WPO, J_UQ):
                    if j < J_WPO + 2:
                        pe.wait_ge(S.taken_by_act, count(l, "taken_by_act", 4 + 15 + j - J_WPO))
                    else:
                        pe.wait_ge(S.taken_by_dve, count(l, "taken_by_dve", j - 22))
                    pe.wait_ge(S.low_part, count(l, "low_part", j + 1))
                    two_tiles(j, YH, YL)
                pe.wait_ge(S.taken_by_dve, count(l, "taken_by_dve", 10))
                pe.wait_ge(S.low_part, count(l, "low_part", J_UKV))
                for t in range(TT):
                    if t >= 2:
                        pe.wait_ge(S.qkv_taken, count(l, "qkv_taken", t - 1))
                    tok = slice(t * P, (t + 1) * P)
                    for h in range(2):
                        for k in range(QT_):
                            w = slice(h * 384, (h + 1) * 384)
                            m = passes(PS[:, 2 * (t % 2) + h, 0:384], CH[:, k, tok], CL[:, k, tok],
                                       RH[:, (J_UQ + k) % 4, w], RL[:, (J_UQ + k) % 4, w], k == 0, k == QT_ - 1)
                    m.then_inc(S.qkv_product, 1)
                pe.wait_ge(S.qkv_product, count(l, "qkv_product", 4))
                pe.sem_inc(S.block_used, 3)
                pe.wait_ge(S.low_part, count(l, "low_part", J_UKV + 2))
                for t in range(TT):
                    pe.wait_ge(S.qkv_taken, count(l, "qkv_taken", t + 3))
                    tok = slice(t * P, (t + 1) * P)
                    for h in range(2):
                        for k in range(KVT):
                            w = slice(h * 512, (h + 1) * 512)
                            m = passes(PS[:, 2 * (t % 2) + h, :], CH[:, QT_ + k, tok], CL[:, QT_ + k, tok],
                                       RH[:, (J_UKV + k) % 4, w], RL[:, (J_UKV + k) % 4, w], k == 0, k == KVT - 1)
                    m.then_inc(S.qkv_product, 1)
                pe.wait_ge(S.qkv_product, count(l, "qkv_product", 8))
                pe.sem_inc(S.block_used, 2)
                pe.wait_ge(S.qkv_taken, count(l, "qkv_taken", 8))
                apart(pe)

                with pe.Fori(0, HEADS) as h:
                    pe.wait_ge(S.head_sliced, count(l, "head_sliced", h + 1))
                    pe.wait_ge(S.head_stored, count(l, "head_stored", h))
                    for t in range(TT):
                        pe.transpose(PS[0:QK, 0, t * P:(t + 1) * P], QSL[:, t, :], IDN[:])
                    for t in range(TT):
                        m = pe.transpose(PS[0:QK, 1, t * P:(t + 1) * P], KSL[:, t, :], IDN[:])
                    m.then_inc(S.head_transposed, 1)
                    pe.wait_ge(S.head_ready, count(l, "head_ready", h + 1))
                    for t in range(TT):
                        pe.matmul(PS[:, 2 + t, :], QTR[0:QK, t * P:(t + 1) * P], KTR[0:QK, :],
                                  start=True, stop=True).then_inc(S.head_scores, 1)
                    for t in range(TT):
                        pe.wait_ge(S.head_exp, count(l, "head_exp", 4 * h + t + 1))
                        if t >= 2:
                            pe.wait_ge(S.probs_taken, count(l, "probs_taken", 4 * h + t - 1))
                        for k in range(TT):
                            m = pe.transpose(PS[:, 6 + t % 2, k * P:(k + 1) * P], PR[:, t, k * P:(k + 1) * P], IDN[:])
                        m.then_inc(S.probs_transposed, 1)
                    pe.wait_ge(S.probs_taken, count(l, "probs_taken", 4 * h + 4))
                    for t in range(TT):
                        for k in range(TT):
                            m = pe.matmul(PS[:, 0, t * VH:(t + 1) * VH], PT[:, k, t * P:(t + 1) * P],
                                          KV[:, k, bass.ds(h * P + NOPE, VH)], start=k == 0, stop=k == TT - 1)
                    m.then_inc(S.head_output, 1)
                pe.wait_ge(S.head_stored, count(l, "head_stored", HEADS))
                for w in range(4):
                    for t in range(TT):
                        m = pe.transpose(PS[:, 4 + w, t * P:(t + 1) * P], O[:, t, w * P:(w + 1) * P], IDN[:])
                    m.then_inc(S.attn_transposed, 1)
                pe.wait_ge(S.attn_low, count(l, "attn_low", 4))
                for j in range(J_WO, J_WOUT):
                    if j >= J_WO + 2:
                        pe.wait_ge(S.taken_by_dve, count(l, "taken_by_dve", 11 + j - J_WO - 2))
                    pe.wait_ge(S.low_part, count(l, "low_part", j + 1))
                    two_tiles(j, OH, OL)
                pe.wait_ge(S.taken_by_dve, count(l, "taken_by_dve", 14))
                pe.wait_ge(S.norm_low, count(l, "norm_low", KD + 0))
                pe.wait_ge(S.mix_high, count(l, "mix_high", 8))
                pe.wait_ge(S.mix_full, count(l, "mix_full", 8))
                pe.wait_ge(mix_low, l * 8 + 8)
                for j in range(J_WOUT, J_WQ):
                    pe.wait_ge(S.low_part, count(l, "low_part", j + 1))
                    h, kk = divmod(j - J_WOUT, 4)
                    for t in range(TT):
                        for i in range(2):
                            k, w, tok = 2 * kk + i, slice(i * 512, (i + 1) * 512), slice(t * P, (t + 1) * P)
                            m = passes(PS[:, 4 * h + t, :], XH[:, k, tok], XL[:, k, tok],
                                       RH[:, j % 4, w], RL[:, j % 4, w], k == 0, k == KD - 1)
                    m.then_inc(S.block_used, 1)

                pe.wait_ge(S.residual_added, count(l, "residual_added", 8))
                transpose_norm(1)
                pe.wait_ge(S.keys_loaded, count(l, "keys_loaded", 16))

                def query(i, k):
                    j = J_WQ + k
                    pe.wait_ge(S.low_part, count(l, "low_part", 4 * i + j + 1))
                    by_columns(2 * (k % 2), k).then_inc(S.block_used, 1)
                    pe.wait_ge(S.taken_by_act, count(l, "taken_by_act", 20 + 4 * i + k + 1))
                    n = 4 * i + k
                    if isinstance(n, int):
                        if n >= 2:
                            pe.wait_ge(S.key_scores_taken, count(l, "key_scores_taken", n - 1))
                    else:
                        pe.wait_ge(S.key_scores_taken, count(l, "key_scores_taken", n - 1))
                    for t in range(TT):
                        m = pe.matmul(PS[:, 4 + k % 2, t * P:(t + 1) * P], QF[:, k % 2, t * P:(t + 1) * P],
                                      KEYS[:, bass.ds(n * NK, NK)], start=True, stop=True)
                    m.then_inc(S.key_scores, 1)

                for k in range(4):
                    query(0, k)
                with pe.Fori(1, 4) as i:
                    for k in range(4):
                        query(i, k)
                pe.wait_ge(S.choice_ready, count(l, "choice_ready", 1))
                for n, src in enumerate((I1, I2, GW)):
                    for t in range(TT):
                        m = pe.transpose(PS[:, n, t * P:(t + 1) * P], src[:, t, :], IDN[:])
                    m.then_inc(S.choice_transposed, 1)
                def route_tokens(n, s):
                    pe.wait_ge(S.onehots_ready, count(l, "onehots_ready", n + 1))
                    for t in range(4):
                        m = pe.matmul(PS[:, 4 + s, t * P:(t + 1) * P], OA[:, s, t, :], OB[:, s, t, :],
                                      start=True, stop=True)
                    m.then_inc(S.routed, 1)

                route_tokens(0, 0)
                route_tokens(1, 1)
                with pe.Fori(1, 64) as i:
                    for s in range(2):
                        pe.wait_ge(S.routing_taken, count(l, "routing_taken", 2 * i + s - 1))
                        route_tokens(2 * i + s, s)

                def hidden(it, k):
                    c = 4 * it + k
                    if not isinstance(c, int) or c >= 4:
                        pe.wait_ge(S.gelu_done, count(l, "gelu_done", c - 3))
                    pe.wait_ge(S.low_part, count(l, "low_part", J_U + c + 1))
                    by_columns(k % 4, k % 4).then_inc(S.block_used, 1)

                def output(it, pair):
                    g = 2 * it + pair
                    pe.wait_ge(S.weighted_low, count(l, "weighted_low", 2 * g + 2))
                    pe.wait_ge(S.v_low, count(l, "v_low", 2 * g + 2))
                    for o in range(8):
                        t, h = divmod(o, 2)
                        n = 8 * g + o
                        pe.wait_ge(S.residual_added, count(l, "residual_added", 8 + (max(n - 3, 0) if isinstance(n, int) else n - 3)))
                        for i in range(2):
                            s, tok, w = 2 * pair + i, slice(t * P, (t + 1) * P), slice(h * 512, (h + 1) * 512)
                            m = passes(PS[:, 4 + o % 4, :], WHI[:, s, tok], WLO[:, s, tok],
                                       VHI[:, s, w], VLO[:, s, w], i == 0, i == 1)
                        m.then_inc(S.output_product, 1)

                hidden(0, 0)
                hidden(0, 1)
                hidden(0, 2)
                hidden(0, 3)
                pe.wait_ge(S.routing_taken, count(l, "routing_taken", 128))
                output(0, 0)
                hidden(1, 0)
                hidden(1, 1)
                output(0, 1)
                with pe.Fori(1, 31) as it:
                    hidden(it, 2)
                    hidden(it, 3)
                    output(it, 0)
                    hidden(it + 1, 0)
                    hidden(it + 1, 1)
                    output(it, 1)
                hidden(31, 2)
                hidden(31, 3)
                output(31, 0)
                output(31, 1)

        @block.scalar
        def _(act):
            act.wait_ge(const_in, 80)
            act.wait_ge(trig_arg, 1)
            act.activation(SIN[:], ROTC[:, 0], ACT.Sin)
            act.activation(COS[:], ROTC[:, 1], ACT.Sin).then_inc(trig_made, 1)
            with act.Fori(0, LAYERS) as l:

                def hi(i, j):
                    n = 4 * i + j
                    act.wait_ge(sems[f"block_loaded{j % 2}"], 16 * (l * (JOBS // 2) + 2 * i + j // 2 + 1))
                    act.wait_ge(S.block_used, count(l, "block_used", max(n - 3, 0) if isinstance(n, int) else n - 3))
                    act.activation(RH[:, j % 4, :], RAW[:, j % 2, :], ACT.Copy).then_inc(S.high_part, 1)

                def norm(n):
                    for t in range(TT):
                        m = act.activation(XS[:, t, :], X[:, t, :], ACT.Square, accum_out=NRM[:, 0, t:t + 1])
                    m.then_inc(S.squares_summed, 1)
                    act.wait_ge(S.variance_inverted, count(l, "variance_inverted", n + 1))
                    act.activation(NRM[:, 2, :], NRM[:, 1, :], ACT.Sqrt).then_inc(S.rms_ready, 1)

                def split_norm(n, gain):
                    for k in range(KD):
                        act.wait_ge(S.norm_transposed, count(l, "norm_transposed", KD * n + k + 1))
                        act.activation(XH[:, k, :], PS[:, k % 2, :], ACT.Copy,
                                       scale=VEC[:, gain + k:gain + k + 1]).then_inc(S.norm_high, 1)

                act.wait_ge(S.vectors_loaded, count(l, "vectors_loaded", 16))
                act.wait_ge(S.residual_added, count(l, "residual_added", 0))
                norm(0)
                hi(0, 0)
                hi(0, 1)
                split_norm(0, V_N1)
                for j in range(J_C, J_P):
                    hi(0, j + 2)
                    act.wait_ge(S.block_used, count(l, "block_used", j + 1))
                    act.activation(CH[:, j, :], PS[:, 2 * (j % 2), :], ACT.Copy,
                                   scale=VEC[:, V_QG + j:V_QG + j + 1])
                    act.activation(SQC[:, j, :], PS[:, 2 * (j % 2), :], ACT.Square).then_inc(S.latent_squared, 1)
                for j in range(J_P, J_KPE):
                    hi(0, j + 2)
                    act.wait_ge(S.block_used, count(l, "block_used", j + 1))
                    act.activation(PADDED[:, j - J_P, PAD:PAD + SEQ], PS[:, 2 * (j % 2), :],
                                   ACT.Copy).then_inc(S.taken_by_act, 1)
                hi(0, J_KPE + 2)
                act.wait_ge(S.latent_variance, count(l, "latent_variance", 1))
                act.activation(CN[:, 2, :], CN[:, 1, :], ACT.Sqrt).then_inc(S.latent_rms, 1)
                hi(0, J_POOL + 2)
                act.wait_ge(S.block_used, count(l, "block_used", J_POOL + 1))
                for g in range(GROUPS):
                    act.activation(YH[:, g, :], PS[:, 4 + g, :], ACT.Copy,
                                   scale=VEC[:, V_PS + g:V_PS + g + 1]).then_inc(S.pool_high, 1)
                with act.Fori(0, 4) as i:
                    for k in range(4):
                        j = J_GATE + k
                        hi(i, j + 2)
                        act.wait_ge(S.block_used, count(l, "block_used", 4 * i + j + 1))
                        act.activation(GAB[:, 4 * i + k, :], PS[:, 2 * (j % 2), :], ACT.Sigmoid,
                                       bias=VEC[:, bass.ds(V_GB + 4 * i + k, 1)]).then_inc(S.taken_by_act, 1)
                for j in range(J_WPO, J_UQ):
                    hi(0, j + 2)
                hi(0, J_UQ + 2)
                hi(0, J_UQ + 3)
                for t in range(TT):
                    act.wait_ge(S.qkv_product, count(l, "qkv_product", t + 1))
                    act.activation(Q[:, t].rearrange("p (x h) e -> p x (h e)", x=2),
                                   PS[:, 2 * (t % 2):2 * (t % 2) + 2, 0:384], ACT.Copy,
                                   scale=CN[:, 2, t:t + 1]).then_inc(S.qkv_taken, 1)
                hi(0, J_UQ + 4)
                for t in range(TT):
                    act.wait_ge(S.qkv_product, count(l, "qkv_product", t + 5))
                    act.activation(KV[:, t, :].rearrange("p (x e) -> p x e", x=2),
                                   PS[:, 2 * (t % 2):2 * (t % 2) + 2, :], ACT.Copy,
                                   scale=CN[:, 2, 4 + t:5 + t]).then_inc(S.qkv_taken, 1)
                hi(0, J_WO)
                hi(0, J_WO + 1)
                act.wait_ge(S.heads_variance, count(l, "heads_variance", 1))
                act.activation(SMALL[:, 0:64], SMALL[:, 128:192], ACT.Sqrt).then_inc(S.heads_rms, 1)
                with act.Fori(0, HEADS) as h:
                    act.wait_ge(S.head_transposed, count(l, "head_transposed", h + 1))
                    act.activation(QTR[0:QK, :], PS[0:QK, 0, :], ACT.Copy, scale=GQS[0:QK, :])
                    act.activation(KTR[0:QK, :], PS[0:QK, 1, :], ACT.Copy,
                                   scale=VEC[0:QK, V_KH:V_KH + 1]).then_inc(S.head_ready, 1)
                    for t in range(TT):
                        act.wait_ge(S.head_max, count(l, "head_max", 4 * h + t + 1))
                        act.activation(PR[:, t, :], PS[:, 2 + t, :], ACT.Exp, bias=NMX[:, t:t + 1],
                                       accum_out=RSM[:, t:t + 1]).then_inc(S.head_exp, 1)
                for w in range(4):
                    act.wait_ge(S.attn_transposed, count(l, "attn_transposed", w + 1))
                    act.activation(OH[:, w, :], PS[:, 4 + w, :], ACT.Copy).then_inc(S.attn_high, 1)
                for j in range(J_WO, J_WOUT):
                    hi(0, j + 2)
                    for m in range(2):
                        n = 2 * (j - J_WO) + m
                        act.wait_ge(S.mix_full, count(l, "mix_full", n + 1))
                        act.activation(XH[:, n, :], T2[:, n % 2, :], ACT.Copy).then_inc(S.mix_high, 1)
                for j in range(J_WOUT, J_WQ):
                    hi(0, j + 2)
                act.wait_ge(S.residual_added, count(l, "residual_added", 8))
                norm(1)
                split_norm(1, V_N2)
                with act.Fori(0, 4) as i:
                    for k in range(4):
                        j = J_WQ + k
                        hi(i, j + 2)
                        act.wait_ge(S.block_used, count(l, "block_used", 4 * i + j + 1))
                        act.wait_ge(S.key_scores, count(l, "key_scores", 4 * i + max(k - 1, 0)))
                        act.activation(QF[:, k % 2, :], PS[:, 2 * (k % 2), :], ACT.Copy).then_inc(S.taken_by_act, 1)
                act.wait_ge(S.best_shifted, count(l, "best_shifted", 1))
                act.activation(GW[:], BV[:], ACT.Exp).then_inc(S.best_exp, 1)
                with act.Fori(0, NTB // 2) as b:
                    for s in range(2):
                        act.wait_ge(sems[f"routing_stored{s}"], count(l, f"routing_stored{s}", 16 * b))
                        with act.Fori(0, TB // 8) as i:
                            for k in range(2):
                                act.wait_ge(S.routed, count(l, "routed", 32 * b + 16 * s + 2 * i + k + 1))
                                act.activation(STAGE[s][:, :, bass.ds(8 * i + 4 * k, 4)],
                                               PS[:, 4 + k, :].rearrange("p (t i) -> p i t", t=4),
                                               ACT.Copy).then_inc(S.routing_taken, 1)

                def chunk(it, k, last=False):
                    c = 4 * it + k
                    static = isinstance(c, int)
                    if not (last and k >= 2):
                        hi(it, J_U + k + 2)
                    act.wait_ge(sems[f"v_loaded{k % 2}"], 16 * (l * 64 + 2 * it + k // 2 + 1))
                    g = 2 * it + k // 2
                    act.wait_ge(S.output_product, count(l, "output_product", max(8 * g - 8, 0) if static else 8 * g - 8))
                    act.activation(VHI[:, k, :], VRAW[:, k % 2, :], ACT.Copy).then_inc(S.v_high, 1)
                    act.wait_ge(S.block_used, count(l, "block_used", J_U + c + 1))
                    act.wait_ge(S.weighted, count(l, "weighted", max(c - 1, 0) if static else c - 1))
                    act.activation(GEL[:, k % 2, :], PS[:, k, :], ACT.Gelu_apprx_tanh).then_inc(S.gelu_done, 1)
                    act.wait_ge(S.weighted, count(l, "weighted", c + 1))
                    act.activation(WHI[:, k, :], WF[:, k % 2, :], ACT.Copy).then_inc(S.weighted_high, 1)

                for k in range(4):
                    chunk(0, k)
                with act.Fori(1, 31) as it:
                    for k in range(4):
                        chunk(it, k)
                for k in range(4):
                    chunk(31, k, last=True)

        @block.vector
        def _(dve):
            dve.memset(ONES[:], 1.0)
            dve.wait_ge(iota_made, 1)
            dve.wait_ge(const_in, 80)
            POSF, ANG, TURN = WA[:, 0:TT], ROTC[:, 2], ROTC[:, 3]
            dve.tensor_copy(POSF, PADDED[:, 0, 0:TT].bitcast(I32))
            dve.drain()
            dve.tensor_tensor(ANG, COS[:, 0, :].unsqueeze(1).to_broadcast([P, TT, HALF]),
                              POSF.unsqueeze(2).to_broadcast([P, TT, HALF]), ALU.mult)
            dve.drain()
            magic = 1.5 * 2.0 ** 23
            dve.tensor_scalar(TURN, ANG, 1 / (2 * np.pi), magic, ALU.mult, ALU.add)
            dve.drain()
            dve.tensor_scalar(TURN, TURN, -magic, None, ALU.add)
            dve.drain()
            c1 = 6.28125
            c2 = float(np.float32(np.round((2 * np.pi - c1) * 2.0 ** 21) / 2.0 ** 21))
            c3 = 2 * np.pi - c1 - c2
            for c in (c1, c2, c3):
                dve.scalar_tensor_tensor(ANG, TURN, -c, ANG, ALU.mult, ALU.add)
                dve.drain()
            top = float(np.float32(3.1415925))
            dve.tensor_scalar(ROTC[:, 0], ANG, top, -top, ALU.min, ALU.max)
            dve.tensor_scalar(ROTC[:, 1], ANG, np.pi / 2, None, ALU.add)
            dve.drain()
            dve.tensor_scalar(TURN, ROTC[:, 1], top, -2 * np.pi, ALU.is_gt, ALU.mult)
            dve.drain()
            dve.tensor_tensor(ROTC[:, 1], ROTC[:, 1], TURN, ALU.add)
            dve.drain()
            dve.tensor_scalar(ROTC[:, 1], ROTC[:, 1], top, -top, ALU.min, ALU.max).then_inc(trig_arg, 1)
            dve.wait_ge(trig_made, 1)
            dve.drain()
            with dve.Fori(0, LAYERS) as l:

                def lo(i, j):
                    dve.wait_ge(S.high_part, count(l, "high_part", 4 * i + j + 1))
                    dve.tensor_tensor(RL[:, j % 4, :], RAW[:, j % 2, :], RH[:, j % 4, :].bitcast(F32),
                                      ALU.subtract).then_inc(S.low_part, 1)

                def norm(n):
                    dve.wait_ge(S.squares_summed, count(l, "squares_summed", n + 1))
                    dve.tensor_scalar(NRM[:, 0, :], NRM[:, 0, :], 1.0 / D, EPS, ALU.mult, ALU.add)
                    dve.drain()
                    dve.reciprocal(NRM[:, 1, :], NRM[:, 0, :]).then_inc(S.variance_inverted, 1)
                    dve.wait_ge(S.rms_ready, count(l, "rms_ready", n + 1))
                    for t in range(TT):
                        m = dve.tensor_scalar(XS[:, t, :], X[:, t, :], NRM[:, 2, t:t + 1], None, ALU.mult)
                    m.then_inc(S.rows_normed, 1)

                def split_norm(n, gain):
                    for k in range(KD):
                        dve.wait_ge(S.norm_high, count(l, "norm_high", KD * n + k + 1))
                        dve.scalar_tensor_tensor(XL[:, k, :], PS[:, k % 2, :], VEC[:, gain + k:gain + k + 1],
                                                 XH[:, k, :].bitcast(F32), ALU.mult, ALU.subtract).then_inc(S.norm_low, 1)

                dve.wait_ge(S.vectors_loaded, count(l, "vectors_loaded", 16))
                dve.tensor_scalar(GQS[:], VEC[:, V_QH:V_QH + 1], QK ** -0.5, None, ALU.mult)
                norm(0)
                lo(0, 0)
                lo(0, 1)
                split_norm(0, V_N1)
                for g in range(GROUPS):
                    dve.memset(PADDED[:, g, 0:PAD], 0.0)
                    m = dve.memset(PADDED[:, g, PAD + SEQ:], 0.0)
                dve.drain()
                for j in range(J_C, J_P):
                    lo(0, j + 2)
                    dve.wait_ge(S.latent_squared, count(l, "latent_squared", j + 1))
                    dve.scalar_tensor_tensor(CL[:, j, :], PS[:, 2 * (j % 2), :], VEC[:, V_QG + j:V_QG + j + 1],
                                             CH[:, j, :].bitcast(F32), ALU.mult, ALU.subtract).then_inc(S.taken_by_dve, 1)
                for j in range(J_P, J_KPE):
                    lo(0, j + 2)
                dve.wait_ge(S.taken_by_act, count(l, "taken_by_act", 4))
                for g in range(GROUPS):
                    src = PADDED[:, g, :]
                    bufs = (WA, WB)
                    dve.tensor_tensor(WA[:, 1:528], src[:, 1:528], src[:, 0:527], ALU.add)
                    dve.drain()
                    have = 0
                    lo_i, hi_i = 1, 528
                    for step in range(g):
                        d = 2 ** step
                        lo_i, hi_i = lo_i + d, hi_i - d
                        a, b = bufs[have], bufs[1 - have]
                        dve.tensor_tensor(b[:, lo_i:hi_i], a[:, lo_i - d:hi_i - d], a[:, lo_i + d:hi_i + d], ALU.add)
                        dve.drain()
                        have = 1 - have
                    win = bufs[have]
                    dve.tensor_tensor(win[:, PAD:2 * PAD], win[:, PAD:2 * PAD], EDGE[:, g, 0, :], ALU.mult)
                    dve.tensor_tensor(win[:, SEQ:SEQ + PAD], win[:, SEQ:SEQ + PAD], EDGE[:, g, 1, :], ALU.mult)
                    dve.drain()
                    other = bufs[1 - have]
                    dve.scalar_tensor_tensor(other[:, 0:SEQ], win[:, PAD:PAD + SEQ], 0.5 ** (g + 1),
                                             src[:, PAD:PAD + SEQ], ALU.mult, ALU.subtract)
                    dve.drain()
                    dve.tensor_copy(MIXH[:, g, :], other[:, 0:SEQ])
                    dve.drain()
                    m = dve.tensor_tensor(MIXL[:, g, :], other[:, 0:SEQ], MIXH[:, g, :].bitcast(F32), ALU.subtract)
                    if g == GROUPS - 1:
                        m.then_inc(S.window_means, 1)
                    dve.drain()
                lo(0, J_KPE + 2)
                dve.wait_ge(S.block_used, count(l, "block_used", J_KPE + 1))
                dve.tensor_copy(KPE[:].rearrange("p t e -> p (t e)"), PS[:, 2, 0:TT * ROPE]).then_inc(S.taken_by_dve, 1)
                dve.wait_ge(S.latent_summed, count(l, "latent_summed", 1))
                dve.tensor_scalar(CN[:, 0, 0:4], PS[:, 7, 0:4], 1.0 / Q_LORA, EPS, ALU.mult, ALU.add)
                dve.tensor_scalar(CN[:, 0, 4:8], PS[:, 7, 4:8], 1.0 / KV_LORA, EPS, ALU.mult, ALU.add)
                dve.drain()
                dve.reciprocal(CN[:, 1, :], CN[:, 0, :]).then_inc(S.latent_variance, 1)
                lo(0, J_POOL + 2)
                for g in range(GROUPS):
                    dve.wait_ge(S.pool_high, count(l, "pool_high", g + 1))
                    dve.scalar_tensor_tensor(YL[:, g, :], PS[:, 4 + g, :], VEC[:, V_PS + g:V_PS + g + 1],
                                             YH[:, g, :].bitcast(F32), ALU.mult, ALU.subtract).then_inc(S.pool_low, 1)
                with dve.Fori(0, 4) as i:
                    for k in range(4):
                        lo(i, J_GATE + k + 2)
                dve.wait_ge(S.taken_by_act, count(l, "taken_by_act", 20))
                for j in range(J_WPO, J_UQ):
                    lo(0, j + 2)
                    dve.wait_ge(S.block_used, count(l, "block_used", j + 1))
                    for m in range(2):
                        n = KD + 2 * (j - J_WPO) + m
                        ins = dve.tensor_tensor(GAB[:, n, :], PS[:, 2 * (j % 2) + m, :], GAB[:, n, :], ALU.mult)
                    ins.then_inc(S.taken_by_dve, 1)
                lo(0, J_UQ + 2)
                lo(0, J_UQ + 3)
                lo(0, J_UQ + 4)
                lo(0, J_WO)
                lo(0, J_WO + 1)
                dve.wait_ge(S.qkv_taken, count(l, "qkv_taken", 8))
                cosq = COS[:].unsqueeze(2).to_broadcast([P, TT, HEADS, HALF])
                sinq = SIN[:].unsqueeze(2).to_broadcast([P, TT, HEADS, HALF])

                def rotate(x1, x2, cos, sin, r):
                    dve.tensor_tensor(r[0], x1, cos, ALU.mult)
                    dve.tensor_tensor(r[1], x2, sin, ALU.mult)
                    dve.tensor_tensor(r[2], x1, sin, ALU.mult)
                    dve.tensor_tensor(r[3], x2, cos, ALU.mult)
                    dve.drain()
                    dve.tensor_tensor(x1, r[0], r[1], ALU.subtract)
                    dve.tensor_tensor(x2, r[2], r[3], ALU.add)
                    dve.drain()

                rotate(Q[:, :, :, NOPE:NOPE + HALF], Q[:, :, :, NOPE + HALF:QK], cosq, sinq,
                       [ROT[:, n, :].rearrange("p (t h e) -> p t h e", t=TT, h=HEADS) for n in range(4)])
                rotate(KPE[:, :, 0:HALF], KPE[:, :, HALF:ROPE], COS[:], SIN[:],
                       [ROT[:, n, 0:TT * HALF].rearrange("p (t e) -> p t e", t=TT) for n in range(4)])
                qv = Q[:].rearrange("p t h e -> p (t h) e")
                kn = KV[:].rearrange("p t (h e) -> p (t h) e", h=HEADS)[:, :, 0:NOPE]
                dve.tensor_tensor(SQT[:], qv, qv, ALU.mult)
                dve.drain()
                dve.tensor_reduce(SMALL[:, 128:160], SQT[:], AX, ALU.add)
                dve.drain()
                dve.tensor_tensor(SQT[:, :, 0:NOPE], kn, kn, ALU.mult)
                dve.tensor_tensor(ROT[:, 0, 0:TT * ROPE].rearrange("p (t e) -> p t e", t=TT), KPE[:], KPE[:], ALU.mult)
                dve.drain()
                dve.tensor_reduce(SMALL[:, 160:192], SQT[:, :, 0:NOPE], AX, ALU.add)
                dve.tensor_reduce(KPS, ROT[:, 0, 0:TT * ROPE].rearrange("p (t e) -> p t e", t=TT), AX, ALU.add)
                dve.drain()
                sk = SMALL[:, 160:192].rearrange("p (t h) -> p t h", t=TT)
                dve.tensor_tensor(sk, sk, KPS.unsqueeze(2).to_broadcast([P, TT, HEADS]), ALU.add)
                dve.drain()
                dve.tensor_scalar(SMALL[:, 128:192], SMALL[:, 128:192], 1.0 / QK, EPS, ALU.mult, ALU.add)
                dve.drain()
                dve.reciprocal(SMALL[:, 128:192], SMALL[:, 128:192]).then_inc(S.heads_variance, 1)
                dve.wait_ge(S.heads_rms, count(l, "heads_rms", 1))
                apart(dve)
                with dve.Fori(0, HEADS) as h:
                    def head_scale(r, n):
                        return r[:, :, bass.ds(h, 1)].to_broadcast([P, TT, n])

                    dve.tensor_tensor(QSL[:], Q[:, :, bass.ds(h, 1), :].rearrange("p t o e -> p (t o) e"),
                                      head_scale(RQ, QK), ALU.mult)
                    dve.tensor_tensor(KSL[:, :, 0:NOPE], KV[:, :, bass.ds(h * P, NOPE)], head_scale(RK, NOPE), ALU.mult)
                    dve.tensor_tensor(KSL[:, :, NOPE:QK], KPE[:], head_scale(RK, ROPE), ALU.mult).then_inc(S.head_sliced, 1)
                    for t in range(TT):
                        dve.wait_ge(S.head_scores, count(l, "head_scores", 4 * h + t + 1))
                        dve.tensor_reduce(NMX[:, t:t + 1], PS[:, 2 + t, :], AX, ALU.max, negate=True).then_inc(S.head_max, 1)
                    for t in range(TT):
                        dve.wait_ge(S.probs_transposed, count(l, "probs_transposed", 4 * h + t + 1))
                        dve.tensor_copy(PT[:, :, t * P:(t + 1) * P],
                                        PS[:, 6 + t % 2, :].rearrange("p (k q) -> p k q", k=TT)).then_inc(S.probs_taken, 1)
                    dve.wait_ge(S.head_exp, count(l, "head_exp", 4 * h + 4))
                    dve.reciprocal(RIN, RSM)
                    dve.drain()
                    dve.wait_ge(S.head_output, count(l, "head_output", h + 1))
                    dve.tensor_tensor(O[:, :, bass.ds(h * VH, VH)],
                                      PS[:, 0, 0:TT * VH].rearrange("p (t e) -> p t e", t=TT),
                                      RIN.unsqueeze(2).to_broadcast([P, TT, VH]), ALU.mult).then_inc(S.head_stored, 1)
                    dve.drain()
                for w in range(4):
                    dve.wait_ge(S.attn_high, count(l, "attn_high", w + 1))
                    dve.tensor_tensor(OL[:, w, :], PS[:, 4 + w, :], OH[:, w, :].bitcast(F32), ALU.subtract).then_inc(S.attn_low, 1)
                for j in range(J_WO, J_WOUT):
                    lo(0, j + 2)
                    dve.wait_ge(S.block_used, count(l, "block_used", j + 1))
                    for m in range(2):
                        n = 2 * (j - J_WO) + m
                        dve.tensor_tensor(T2[:, m, :], PS[:, 2 * (j % 2) + m, :], GAB[:, n, :], ALU.mult)
                        dve.drain()
                        dve.tensor_tensor(T2[:, m, :], T2[:, m, :], GAB[:, KD + n, :], ALU.add).then_inc(S.mix_full, 1)
                        dve.wait_ge(S.mix_high, count(l, "mix_high", n + 1))
                        dve.tensor_tensor(XL[:, n, :], T2[:, m, :], XH[:, n, :].bitcast(F32), ALU.subtract).then_inc(mix_low, 1)
                    dve.drain()
                    dve.engine_nop().then_inc(S.taken_by_dve, 1)
                for j in range(J_WOUT, J_WQ):
                    lo(0, j + 2)
                    h, kk = divmod(j - J_WOUT, 4)
                    if kk == 3:
                        dve.wait_ge(S.block_used, count(l, "block_used", j + 1))
                        for t in range(TT):
                            w = slice(h * 512, (h + 1) * 512)
                            dve.tensor_tensor(X[:, t, w], PS[:, 4 * h + t, :], X[:, t, w], ALU.add).then_inc(S.residual_added, 1)
                norm(1)
                split_norm(1, V_N2)

                def best16(n, vals, idx, src, work):
                    for t in range(TT):
                        dve.max(vals(t)[:, 0:8], src(t))
                    dve.drain()
                    for t in range(TT):
                        dve.max_index(idx(t)[:, 0:8], vals(t)[:, 0:8], src(t))
                        m = dve.match_replace(work(t), vals(t)[:, 0:8], src(t), -3.0e38)
                    dve.drain()
                    for t in range(TT):
                        dve.max(vals(t)[:, 8:16], work(t))
                    dve.drain()
                    for t in range(TT):
                        dve.max_index(idx(t)[:, 8:16], vals(t)[:, 8:16], work(t))
                    return m

                with dve.Fori(0, 4) as i:
                    for head in range(2):
                        for half in range(2):
                            k = 2 * head + half
                            lo(i, J_WQ + k + 2)
                            dve.wait_ge(S.key_scores, count(l, "key_scores", 4 * i + k + 1))
                            apart(dve)
                            best16(0, lambda t: V16[:, t, half, :], lambda t: I16[:, t, half, :],
                                   lambda t: PS[:, 4 + k % 2, t * P:(t + 1) * P], lambda t: SW[:, t, :])
                            dve.drain()
                            dve.engine_nop().then_inc(S.key_scores_taken, 1)
                        dve.tensor_tensor(CAND[:].rearrange("p t (a b) -> p t a b", a=TOPK),
                                          V16[:, :, 0, :].unsqueeze(3).to_broadcast([P, TT, TOPK, TOPK]),
                                          V16[:, :, 1, :].unsqueeze(2).to_broadcast([P, TT, TOPK, TOPK]), ALU.add)
                        dve.tensor_copy(F16[:], I16[:])
                        dve.drain()
                        best16(0, lambda t: B16[:, t, :], lambda t: J16[:, t, :], lambda t: CAND[:, t, :],
                               lambda t: CW[:, t, :])
                        dve.drain()
                        dve.tensor_scalar(JHL[:, 0], J16[:], 4, None, ALU.logical_shift_right)
                        dve.tensor_scalar(JHL[:, 1], J16[:], 15, None, ALU.bitwise_and)
                        dve.drain()
                        dve.tensor_copy(JF[:], JHL[:])
                        dve.tensor_copy(BV[:, :, bass.ds((2 * i + head) * TOPK, TOPK)], B16[:])
                        dve.drain()
                        ramp = IOTA[:, 0:TOPK].unsqueeze(1).to_broadcast([P, TOPK, TOPK])
                        for half, (e, dst) in enumerate(((EQ, I1), (EQ2, I2))):
                            for t in range(TT):
                                dve.tensor_tensor(e[:, t], JF[:, half, t, :].unsqueeze(2).to_broadcast([P, TOPK, TOPK]),
                                                  ramp, ALU.is_equal)
                        dve.drain()
                        for half, e in enumerate((EQ, EQ2)):
                            dve.tensor_tensor(e[:], e[:], F16[:, :, half, :].unsqueeze(2).to_broadcast([P, TT, TOPK, TOPK]),
                                              ALU.mult)
                        dve.drain()
                        for e, dst in ((EQ, I1), (EQ2, I2)):
                            dve.tensor_reduce(dst[:, :, bass.ds((2 * i + head) * TOPK, TOPK)], e[:], AX, ALU.add)
                        dve.drain()
                bv = BV[:].rearrange("p t (h k) -> p (t h) k", k=TOPK)
                gw = GW[:].rearrange("p t (h k) -> p (t h) k", k=TOPK)
                dve.tensor_copy(BS[:, 0, :].unsqueeze(2), bv[:, :, 0:1])
                dve.drain()
                dve.tensor_tensor(bv, bv, BS[:, 0, :].unsqueeze(2).to_broadcast([P, TT * PH, TOPK]),
                                  ALU.subtract).then_inc(S.best_shifted, 1)
                dve.wait_ge(S.best_exp, count(l, "best_exp", 1))
                dve.tensor_reduce(BS[:, 1, :], gw, AX, ALU.add)
                dve.drain()
                dve.reciprocal(BS[:, 1, :], BS[:, 1, :])
                dve.drain()
                dve.tensor_tensor(gw, gw, BS[:, 1, :].unsqueeze(2).to_broadcast([P, TT * PH, TOPK]),
                                  ALU.mult).then_inc(S.choice_ready, 1)
                for n in range(3):
                    dve.wait_ge(S.choice_transposed, count(l, "choice_transposed", n + 1))
                    dve.tensor_copy(IT[:, n, :], PS[:, n, :])
                dve.drain()

                def one_hots(i, k, s):
                    for t in range(4):
                        tok = 8 * i + 4 * s + t
                        dve.tensor_scalar(OA[:, s, t, :], IOTA[:], IT[:, 0, bass.ds(tok, 1)], None, ALU.is_equal)
                        m = dve.tensor_scalar(OB[:, s, t, :], IOTA[:], IT[:, 1, bass.ds(tok, 1)],
                                              IT[:, 2, bass.ds(tok, 1)], ALU.is_equal, ALU.mult)
                    m.then_inc(S.onehots_ready, 1)

                one_hots(0, 0, 0)
                one_hots(0, 0, 1)
                with dve.Fori(1, 64) as i:
                    for s in range(2):
                        dve.wait_ge(S.routed, count(l, "routed", 2 * i + s - 1))
                        one_hots(i, 0, s)

                def add_outputs(g, first):
                    for o in range(first, first + 4):
                        t, h = divmod(o, 2)
                        w = slice(h * 512, (h + 1) * 512)
                        dve.wait_ge(S.output_product, count(l, "output_product", 8 * g + o + 1))
                        dve.tensor_tensor(X[:, t, w], PS[:, 4 + o % 4, :], X[:, t, w], ALU.add).then_inc(S.residual_added, 1)

                def chunk(it, k, last=False):
                    c = 4 * it + k
                    g = 2 * it + k // 2
                    if not (last and k >= 2):
                        lo(it, J_U + k + 2)
                    dve.wait_ge(S.gelu_done, count(l, "gelu_done", c + 1))
                    dve.wait_ge(sems[f"routing_loaded{k // 2}"], 16 * (l * 32 + it + 1))
                    dve.tensor_tensor(WF[:, k % 2, :].rearrange("p (b t) -> p b t", b=NTB),
                                      GEL[:, k % 2, :].rearrange("p (b t) -> p b t", b=NTB),
                                      GC[:, k // 2, :, k % 2, :], ALU.mult).then_inc(S.weighted, 1)
                    dve.wait_ge(S.v_high, count(l, "v_high", c + 1))
                    dve.tensor_tensor(VLO[:, k, :], VRAW[:, k % 2, :], VHI[:, k, :].bitcast(F32),
                                      ALU.subtract).then_inc(S.v_low, 1)
                    dve.wait_ge(S.weighted_high, count(l, "weighted_high", c + 1))
                    dve.tensor_tensor(WLO[:, k, :], WF[:, k % 2, :], WHI[:, k, :].bitcast(F32),
                                      ALU.subtract).then_inc(S.weighted_low, 1)
                    if not isinstance(g, int) or g >= 1:
                        add_outputs(g - 1, 4 * (k % 2))
                    dve.drain()

                for k in range(4):
                    chunk(0, k)
                with dve.Fori(1, 31) as it:
                    for k in range(4):
                        chunk(it, k)
                for k in range(4):
                    chunk(31, k, last=True)
                add_outputs(63, 0)
                add_outputs(63, 4)
                dve.drain()

        @block.gpsimd
        def _(pool):
            for name in FROM_ONE:
                pool.sem_inc(sems[name], 1)
            pool.iota(IOTA[:], [[1, P]], base=0, channel_multiplier=0,
                      allow_small_or_imprecise_dtypes=True).then_inc(iota_made, 1)


def laid_out(x, positions, norm1_g, w_in, q_lora_g, kv_lora_g, w_uq, w_ukv, q_head_g, k_head_g,
             w_o_mla, pool_w, pool_scale, w_pool_out, gate_bias, w_out, norm2_g,
             peer_wq, peer_keys, peer_u, peer_v):
    f = np.float32
    L = LAYERS
    stream = np.zeros((L, J_U, P, 1024), f)
    cols = lambda w, a, b: w[:, :, a:b].reshape(L, KD, P, (b - a) // P, P).transpose(0, 3, 2, 1, 4).reshape(L, -1, P, D)
    p0 = Q_LORA + KV_LORA + ROPE
    stream[:, J_C:J_P] = cols(w_in, 0, Q_LORA + KV_LORA)
    stream[:, J_P:J_KPE] = cols(w_in, p0, p0 + 512)
    stream[:, J_KPE, :, :KD * ROPE] = w_in[:, :, Q_LORA + KV_LORA:p0].reshape(L, KD, P, ROPE).transpose(0, 2, 1, 3).reshape(L, P, -1)
    stream[:, J_POOL, :, :512] = pool_w.transpose(0, 2, 1, 3).reshape(L, P, 512)
    stream[:, J_GATE:J_WPO] = cols(w_in, p0 + 512, p0 + 512 + 2 * D)
    tiles = lambda w: w.reshape(L, 4, P, 4, 2, P).transpose(0, 3, 2, 4, 1, 5).reshape(L, 4, P, D)
    stream[:, J_WPO:J_UQ] = tiles(w_pool_out)
    stream[:, J_UQ:J_UKV, :, :768] = w_uq.reshape(L, QT_, P, 768)
    stream[:, J_UKV:J_WO] = w_ukv.reshape(L, KVT, P, D)
    stream[:, J_WO:J_WOUT] = tiles(w_o_mla)
    stream[:, J_WOUT:J_WQ] = w_out.reshape(L, 4, 2, P, 2, 512).transpose(0, 4, 1, 3, 2, 5).reshape(L, 8, P, D)
    stream[:, J_WQ:J_U] = cols(peer_wq, 0, 2048)
    vecs = np.zeros((L, P, V_ALL), f)
    for at, a in ((V_N1, norm1_g), (V_N2, norm2_g), (V_QG, q_lora_g), (V_KVG, kv_lora_g), (V_PS, pool_scale),
                  (V_GB, gate_bias.reshape(L, -1))):
        a = a.reshape(L, -1, P).transpose(0, 2, 1)
        vecs[:, :, at:at + a.shape[2]] = a
    vecs[:, :QK, V_QH] = q_head_g
    vecs[:, :QK, V_KH] = k_head_g
    edge = np.ones((GROUPS, 2, PAD), f)
    for g in range(GROUPS):
        h = 2 ** g
        for c in range(PAD):
            edge[g, 0, c] = 2 * h / min(c + h, 2 * h)
            edge[g, 1, c] = 2 * h / min(PAD - c + h, 2 * h)
    inv = (10000.0 ** (-np.arange(0, ROPE, 2, dtype=np.float64) / ROPE)).astype(f)
    return {
        "x": x,
        "pos": np.ascontiguousarray(positions.reshape(TT, P).T),
        "inv_freq": np.tile(inv, (P, 1)),
        "ident": np.eye(P, dtype=f),
        "edge": np.tile(edge.reshape(1, -1), (P, 1)),
        "vecs": vecs,
        "stream": stream,
        "peer_keys": np.ascontiguousarray(peer_keys.transpose(0, 4, 1, 2, 3).reshape(L, P, -1)),
        "peer_u": np.ascontiguousarray(peer_u.reshape(L, NK, NK, KD, P).transpose(0, 2, 4, 3, 1).reshape(L, NK, P, D)),
        "peer_v": peer_v.reshape(L, NK, NK, D),
    }


def kernel(**inputs):
    import concourse.bacc as bacc
    from concourse.bass_utils import run_bass_kernel_spmd

    arrays = laid_out(**{n: np.asarray(a) for n, a in inputs.items()})
    nc = bacc.Bacc("TRN2", target_bir_lowering=False, num_devices=1)
    aps = {n: nc.dram_tensor(f"in_{n}", a.shape, mybir.dt.from_np(a.dtype), kind="ExternalInput").ap()
           for n, a in arrays.items()}
    out = nc.dram_tensor("out", (1, SEQ, D), F32, kind="ExternalOutput").ap()
    program(nc, out=out, **aps)
    r = run_bass_kernel_spmd(nc, [{f"in_{n}": a for n, a in arrays.items()}], core_ids=[0])
    return r.results[0]["out"]
```

```python
from contextlib import ExitStack

import numpy as np

import concourse.bass as bass
from concourse import mybir

ACT = mybir.ActivationFunctionType
ALU = mybir.AluOpType
AX = mybir.AxisListType.X
F32 = mybir.dt.float32
F32R = mybir.dt.float32r
U32 = mybir.dt.uint32
I32 = mybir.dt.int32

P = 128
LAYERS = 2
SEQ = 512
D = 1024
TT = SEQ // P
KD = D // P
HEADS, NOPE, ROPE, VH = 8, 64, 32, 64
QK = NOPE + ROPE
HALF = ROPE // 2
Q_LORA, KV_LORA = 384, 256
QT_, KVT = Q_LORA // P, KV_LORA // P
GROUPS = 4
PAD = 8
NK = 128
TOPK = 16
PH = 8
EPS = 1e-6

J_C, J_P, J_KPE, J_POOL, J_GATE = 0, 5, 9, 10, 11
J_WPO, J_UQ, J_UKV, J_WO, J_WOUT, J_WQ, J_U = 27, 31, 34, 36, 40, 48, 64
JOBS = J_U + NK
FILLED = 64

V_N1, V_N2, V_QG, V_KVG, V_PS, V_GB, V_QH, V_KH, V_ALL = 0, 8, 16, 19, 21, 25, 41, 42, 43

TB = 64
NTB = SEQ // TB

PER = dict(
    vectors_loaded=16, keys_loaded=16, block_loaded0=16 * JOBS // 2, block_loaded1=16 * JOBS // 2,
    high_part=JOBS, low_part=JOBS, block_used=JOBS, squares_summed=2, variance_inverted=2, rms_ready=2,
    rows_normed=2, norm_transposed=2 * KD, norm_high=2 * KD, norm_low=2 * KD, taken_by_act=36,
    taken_by_dve=14, latent_squared=5, latent_summed=1, latent_variance=1, latent_rms=1, window_means=1,
    pool_high=4, pool_low=4, qkv_product=8, qkv_taken=8, heads_variance=1, heads_rms=1, head_sliced=8,
    head_transposed=8, head_ready=8, head_scores=32, head_max=32, head_exp=32, probs_transposed=32,
    probs_taken=32, head_output=8, head_stored=8, attn_transposed=4, attn_high=4, attn_low=4, mix_full=8,
    mix_high=8, key_scores=16, key_scores_taken=16, best_shifted=1, best_exp=1, choice_ready=1,
    choice_transposed=3, onehots_ready=128, routed=128, routing_taken=128, routing_stored0=64,
    routing_stored1=64, v_loaded0=1024, v_loaded1=1024, v_high=128, v_low=128, gelu_done=128, weighted=128,
    weighted_high=128, weighted_low=128, routing_loaded0=512, routing_loaded1=512, output_product=512,
    residual_added=8 + 512,
    gelu_stored0=256, gelu_stored1=256, gelu_stored2=256, gelu_stored3=256, gelu_loaded0=256, gelu_loaded1=256,
)

STARTS = dict(low_part=2, block_used=4, residual_added=1, weighted=4, v_low=2, head_stored=1, key_scores=2,
              key_scores_taken=2, routing_stored0=1, routing_stored1=1, output_product=9, gelu_done=2,
              routed=2, routing_taken=2)


def program(nc, x, pos, inv_freq, ident, edge, vecs, stream, peer_keys, peer_u, peer_v, out):
    route = nc.dram_tensor("route_dram", [NTB, P, NK, TB], F32, kind="Internal").ap()
    gelus = nc.dram_tensor("gelu_dram", [FILLED, P, SEQ], F32, kind="Internal").ap()
    ctx = ExitStack()
    with ctx:
        def sb(name, shape, dt=F32):
            return ctx.enter_context(nc.sbuf_tensor(name, shape, dt))

        X = sb("X", [P, TT, D])
        XH = sb("XH", [P, KD, SEQ], F32R)
        XL = sb("XL", [P, KD, SEQ], F32R)
        RAW = sb("RAW", [P, 2, 1024])
        RH = sb("RH", [P, 4, 1024], F32R)
        RL = sb("RL", [P, 4, 1024], F32R)
        IDN = sb("IDN", [P, P])
        IOTA = sb("IOTA", [P, P])
        ONES = sb("ONES", [P, 1])
        EDGE = sb("EDGE", [P, GROUPS, 2, PAD])
        VEC = sb("VEC", [P, V_ALL])
        COS = sb("COS", [P, TT, HALF])
        SIN = sb("SIN", [P, TT, HALF])
        NRM = sb("NRM", [P, 3, TT])
        CN = sb("CN", [P, 3, 8])
        GQS = sb("GQS", [P, 1])

        size = 117 * 1024
        sb("arena", [P, size // 4])
        start = nc.sbuf_base - size

        def at(name, offset, shape, dt=F32):
            n = 4
            for s in shape[1:]:
                n *= s
            assert offset + n <= size, name
            return nc.alloc_sbuf_tensor_at(name, shape, dt, offset=start + offset)

        K = 1024
        CH = at("CH", 0, [P, 5, SEQ], F32R)
        CL = at("CL", 10 * K, [P, 5, SEQ], F32R)
        SQT = at("SQT", 0, [P, TT * HEADS, QK])
        ROT = at("ROT", 12 * K, [P, 4, TT * HEADS * HALF])
        PR = at("PR", 0, [P, TT, SEQ])
        PT = at("PT", 8 * K, [P, TT, SEQ])
        XS = at("XS", 20 * K, [P, TT, D])
        MIXH = at("MIXH", 20 * K, [P, GROUPS, SEQ], F32R)
        MIXL = at("MIXL", 28 * K, [P, GROUPS, SEQ], F32R)
        O = at("O", 20 * K, [P, TT, SEQ])
        QTR = at("QTR", 28 * K, [P, SEQ])
        KTR = at("KTR", 30 * K, [P, SEQ])
        QSL = at("QSL", 32 * K, [P, TT, QK])
        KSL = at("KSL", 32 * K + 1536, [P, TT, QK])
        SMALL = at("SMALL", 35 * K, [P, 256])
        RQ = SMALL[:, 0:32].rearrange("p (t h) -> p t h", t=TT)
        RK = SMALL[:, 32:64].rearrange("p (t h) -> p t h", t=TT)
        NMX = SMALL[:, 64:68]
        RSM = SMALL[:, 68:72]
        RIN = SMALL[:, 72:76]
        KPS = SMALL[:, 76:80]
        ROTC = at("ROTC", 52 * K, [P, 4, TT, HALF])
        PADDED = at("PADDED", 36 * K, [P, GROUPS, SEQ + 2 * PAD])
        WA = at("WA", 36 * K + 8448, [P, SEQ + 2 * PAD])
        WB = at("WB", 36 * K + 10560, [P, SEQ + 2 * PAD])
        KV = at("KV", 36 * K, [P, TT, D])
        YH = at("YH", 52 * K, [P, GROUPS, SEQ], F32R)
        YL = at("YL", 60 * K, [P, GROUPS, SEQ], F32R)
        OH = at("OH", 52 * K, [P, GROUPS, SEQ], F32R)
        OL = at("OL", 60 * K, [P, GROUPS, SEQ], F32R)
        SQC = at("SQC", 68 * K, [P, 5, SEQ])
        GAB = at("GAB", 68 * K, [P, 2 * KD, SEQ])
        Q = at("Q", 100 * K, [P, TT, HEADS, QK])
        T2 = at("T2", 100 * K, [P, 2, SEQ])
        KPE = at("KPE", 112 * K, [P, TT, ROPE])
        KEYS = at("KEYS", 0, [P, 2 * PH * NK])
        QF = at("QF", 8 * K, [P, 2, SEQ])
        SW = at("SW", 12 * K, [P, TT, NK])
        CAND = at("CAND", 14 * K, [P, TT, 256])
        CW = at("CW", 18 * K, [P, TT, 256])
        EQ = at("EQ", 22 * K, [P, TT, TOPK, TOPK])
        EQ2 = at("EQ2", 26 * K, [P, TT, TOPK, TOPK])
        V16 = at("V16", 30 * K, [P, TT, 2, TOPK])
        I16 = at("I16", 30 * K + 512, [P, TT, 2, TOPK], U32)
        F16 = at("F16", 31 * K, [P, TT, 2, TOPK])
        B16 = at("B16", 31 * K + 512, [P, TT, TOPK])
        J16 = at("J16", 31 * K + 768, [P, TT, TOPK], U32)
        JHL = at("JHL", 32 * K, [P, 2, TT, TOPK], U32)
        JF = at("JF", 32 * K + 512, [P, 2, TT, TOPK])
        BV = at("BV", 33 * K, [P, TT, P])
        GW = at("GW", 35 * K, [P, TT, P])
        BS = at("BS", 37 * K, [P, 2, TT * PH])
        I1 = at("I1", 38 * K, [P, TT, P])
        I2 = at("I2", 40 * K, [P, TT, P])
        STAGE = [at(f"STAGE{s}", 32 * K * s, [P, NK, TB]) for s in range(2)]
        IT = at("IT", 64 * K, [P, 3, SEQ])
        OA = at("OA", 70 * K, [P, 2, 4, P])
        OB = at("OB", 74 * K, [P, 2, 4, P])
        VRAW = at("VRAW", 0, [P, 2, D])
        VHI = at("VHI", 8 * K, [P, 4, D], F32R)
        VLO = at("VLO", 24 * K, [P, 4, D], F32R)
        GC = at("GC", 40 * K, [P, 2, NTB, 2, TB])
        GEL = at("GEL", 48 * K, [P, 2, SEQ])
        GS = at("GS", 80 * K, [P, 4, SEQ])
        GB = at("GB", 88 * K, [P, 2, 2, SEQ])
        WF = at("WF", 52 * K, [P, 2, SEQ])
        WHI = at("WHI", 56 * K, [P, 4, SEQ], F32R)
        WLO = at("WLO", 64 * K, [P, 4, SEQ], F32R)

        PS = ctx.enter_context(nc.psum_tensor("PS", [P, 8, 512], F32))

        sems = {n: ctx.enter_context(nc.semaphore(n)) for n in PER}
        passed = ctx.enter_context(nc.semaphore("passed"))
        mix_low = ctx.enter_context(nc.semaphore("mix_low"))
        const_in = ctx.enter_context(nc.semaphore("const_in"))
        iota_made = ctx.enter_context(nc.semaphore("iota_made"))
        trig_arg = ctx.enter_context(nc.semaphore("trig_arg"))
        trig_made = ctx.enter_context(nc.semaphore("trig_made"))
        stored = ctx.enter_context(nc.semaphore("stored"))
        S = type("Sems", (), sems)

        def count(layer, name, n):
            return layer * PER[name] + n + STARTS.get(name, 0)

        def apart(engine):
            engine.sem_inc(passed, 1)

        block = ctx.enter_context(nc.Block())

        @block.sync
        def _(sp):
            sp.dma_start(X[:], x.rearrange("b (t p) d -> p (b t) d", p=P)).then_inc(const_in, 16)
            sp.dma_start(PADDED[:, 0, 0:TT].bitcast(I32), pos).then_inc(const_in, 16)
            sp.dma_start(COS[:, 0, :], inv_freq).then_inc(const_in, 16)
            sp.dma_start(IDN[:], ident).then_inc(const_in, 16)
            sp.dma_start(EDGE[:].rearrange("p g e c -> p (g e c)"), edge).then_inc(const_in, 16)
            with sp.Fori(0, LAYERS) as l:

                def load_block(src, slot):
                    sp.dma_start(RAW[:, slot, :], src).then_inc(sems[f"block_loaded{slot}"], 16)

                sp.wait_ge(S.residual_added, count(l, "residual_added", 0))
                sp.dma_start(VEC[:], vecs[l]).then_inc(S.vectors_loaded, 16)
                with sp.Fori(0, J_WQ // 4) as i:
                    for k in range(4):
                        sp.wait_ge(S.low_part, count(l, "low_part", 4 * i + k - 1))
                        load_block(stream[l, 4 * i + k], k % 2)

                def load_query(n, q, slot):
                    sp.wait_ge(S.low_part, count(l, "low_part", n - 1))
                    load_block(stream[l, J_WQ + q], slot)

                def load_experts(n, c, slot):
                    sp.wait_ge(S.low_part, count(l, "low_part", n - 1))
                    load_block(peer_u[l, c], slot)

                def store_gelu(f, slot):
                    sp.wait_ge(S.gelu_done, count(l, "gelu_done", f + 1))
                    sp.dma_start(gelus[f], GS[:, slot, :]).then_inc(sems[f"gelu_stored{slot}"], 16)

                load_query(J_WQ, 0, 0)
                load_query(J_WQ + 1, 1, 1)
                sp.wait_ge(S.residual_added, count(l, "residual_added", 8))
                sp.dma_start(KEYS[:], peer_keys[l]).then_inc(S.keys_loaded, 16)
                for q in (2, 3):
                    n = 44 + 3 * q
                    load_query(n, q, n % 2)
                    for m in range(2):
                        load_experts(n + 1 + m, 2 * q - 4 + m, (n + 1 + m) % 2)
                with sp.Fori(1, 4) as i:
                    for k in range(4):
                        n = 44 + 12 * i + 3 * k
                        load_query(n, 4 * i + k, 3 * k % 2)
                        for m in range(2):
                            f = 8 * i + 2 * k + m - 4
                            load_experts(n + 1 + m, f, (3 * k + 1 + m) % 2)
                            store_gelu(f - 4, (2 * k + m) % 4)
                for f in range(28, 32):
                    load_experts(J_U + f, f, f % 2)
                    store_gelu(f - 4, f % 4)

                def store_routing(b, s):
                    sp.wait_ge(S.routing_taken, count(l, "routing_taken", 16 * b + 16))
                    sp.dma_start(route[b], STAGE[s][:]).then_inc(sems[f"routing_stored{s}"], 16)

                for k in range(4):
                    load_experts(J_U + 32 + k, 32 + k, k % 2)
                    store_gelu(28 + k, k)
                with sp.Fori(0, 3) as i:
                    for k in range(8):
                        f = 36 + 8 * i + k
                        load_experts(J_U + f, f, k % 2)
                        store_gelu(f - 4, k % 4)
                        if k % 4 == 3:
                            store_routing(2 * i + k // 4, k // 4)
                for k in range(4):
                    load_experts(J_U + 60 + k, 60 + k, k % 2)
                    store_gelu(56 + k, k)
                store_routing(6, 0)
                for k in range(4):
                    load_experts(J_U + FILLED + k, FILLED + k, k % 2)
                for k in range(4):
                    store_gelu(60 + k, k)
                store_routing(7, 1)
                for s in range(2):
                    sp.wait_ge(sems[f"routing_stored{s}"], count(l, f"routing_stored{s}", 64))
                for s in range(4):
                    sp.wait_ge(sems[f"gelu_stored{s}"], count(l, f"gelu_stored{s}", 256))
                    apart(sp)

                def position(it, q, last=False):
                    pair, new = q // 2, q // 2 % 2
                    g = 2 * it + pair // 2
                    if q % 2 == 0:
                        sp.wait_ge(S.weighted, count(l, "weighted", 8 * it + q - 2))
                        sp.dma_start(
                            GC[:, new, :, :, :].rearrange("p b i t -> p b (i t)"),
                            route.rearrange("b p (g i) t -> p g b (i t)", i=2)[:, g + new * FILLED // 2],
                        ).then_inc(sems[f"routing_loaded{new}"], 16)
                        if not new:
                            sp.dma_start(GB[:, pair // 2, :, :],
                                         gelus.rearrange("(g i) p t -> p g i t", i=2)[:, g]).then_inc(
                                             sems[f"gelu_loaded{pair // 2}"], 16)
                    sp.wait_ge(S.v_low, count(l, "v_low", 8 * it + q - 1))
                    sp.dma_start(VRAW[:, q % 2, :],
                                 peer_v[l, :, 2 * g + new * FILLED + q % 2, :]).then_inc(sems[f"v_loaded{q % 2}"], 16)
                    if not new and not last:
                        c = FILLED + 4 * it + q // 2 + q % 2 + 4
                        load_experts(J_U + c, c, q % 2)

                with sp.Fori(0, 15) as it:
                    for q in range(8):
                        position(it, q)
                for q in range(8):
                    position(15, q, last=True)
            sp.wait_ge(S.residual_added, count(LAYERS, "residual_added", 0))
            sp.dma_start(out.rearrange("b (t p) d -> p (b t) d", p=P), X[:]).then_inc(stored, 16)
            sp.wait_ge(stored, 16)

        @block.tensor
        def _(pe):
            pe.wait_ge(iota_made, 1)
            pe.wait_ge(const_in, 80)
            with pe.Fori(0, LAYERS) as l:

                def passes(acc, sh, sl, mh, ml, first, last):
                    pe.matmul(acc, sh, mh, start=first, stop=False)
                    pe.matmul(acc, sh, ml, start=False, stop=False)
                    return pe.matmul(acc, sl, mh, start=False, stop=last)

                def by_columns(bank, slot, ks=range(KD)):
                    for k in ks:
                        w = slice(k * P, (k + 1) * P)
                        m = passes(PS[:, bank, :], RH[:, slot, w], RL[:, slot, w], XH[:, k, :], XL[:, k, :],
                                   k == 0, k == KD - 1)
                    return m

                def transpose_norm(n):
                    pe.wait_ge(S.rows_normed, count(l, "rows_normed", n + 1))
                    for k in range(KD):
                        if k >= 2:
                            pe.wait_ge(S.norm_low, count(l, "norm_low", KD * n + k - 1))
                        for t in range(TT):
                            m = pe.transpose(PS[:, k % 2, t * P:(t + 1) * P], XS[:, t, k * P:(k + 1) * P], IDN[:])
                        m.then_inc(S.norm_transposed, 1)
                    pe.wait_ge(S.norm_low, count(l, "norm_low", KD * (n + 1)))

                transpose_norm(0)
                for j in range(J_C, J_P):
                    if j >= 2:
                        pe.wait_ge(S.taken_by_dve, count(l, "taken_by_dve", j - 1))
                    pe.wait_ge(S.low_part, count(l, "low_part", j + 1))
                    by_columns(2 * (j % 2), j % 4).then_inc(S.block_used, 1)
                for j in range(J_P, J_KPE):
                    pe.wait_ge(S.taken_by_dve, count(l, "taken_by_dve", min(j - 1, 5)))
                    if j >= 7:
                        pe.wait_ge(S.taken_by_act, count(l, "taken_by_act", j - 6))
                    pe.wait_ge(S.low_part, count(l, "low_part", j + 1))
                    by_columns(2 * (j % 2), j % 4).then_inc(S.block_used, 1)
                pe.wait_ge(S.taken_by_act, count(l, "taken_by_act", 3))
                pe.wait_ge(S.low_part, count(l, "low_part", J_KPE + 1))
                for t in range(TT):
                    for k in range(KD):
                        s, tok, w = J_KPE % 4, slice(t * P, (t + 1) * P), slice(k * ROPE, (k + 1) * ROPE)
                        m = passes(PS[:, 2, t * ROPE:(t + 1) * ROPE], XH[:, k, tok], XL[:, k, tok],
                                   RH[:, s, w], RL[:, s, w], k == 0, k == KD - 1)
                m.then_inc(S.block_used, 1)
                pe.wait_ge(S.latent_squared, count(l, "latent_squared", 5))
                for t in range(TT):
                    for col, js in ((t, range(QT_)), (4 + t, range(QT_, QT_ + KVT))):
                        for j in js:
                            m = pe.matmul(PS[:, 7, col:col + 1], SQC[:, j, t * P:(t + 1) * P], ONES[:],
                                          start=j == js[0], stop=j == js[-1])
                m.then_inc(S.latent_summed, 1)
                pe.wait_ge(S.latent_summed, count(l, "latent_summed", 1))
                pe.wait_ge(S.latent_variance, count(l, "latent_variance", 1))
                pe.wait_ge(S.window_means, count(l, "window_means", 1))
                pe.wait_ge(S.low_part, count(l, "low_part", J_POOL + 1))
                for g in range(GROUPS):
                    w = slice(g * P, (g + 1) * P)
                    m = passes(PS[:, 4 + g, :], RH[:, J_POOL % 4, w], RL[:, J_POOL % 4, w],
                               MIXH[:, g, :], MIXL[:, g, :], True, True)
                m.then_inc(S.block_used, 1)
                pe.wait_ge(S.taken_by_dve, count(l, "taken_by_dve", 6))
                pe.wait_ge(S.low_part, count(l, "low_part", J_GATE + 1))
                by_columns(2, J_GATE % 4).then_inc(S.block_used, 1)
                pe.wait_ge(S.taken_by_act, count(l, "taken_by_act", 4))
                pe.wait_ge(S.low_part, count(l, "low_part", J_GATE + 2))
                by_columns(0, (J_GATE + 1) % 4).then_inc(S.block_used, 1)
                for j in range(J_GATE + 2, J_GATE + 4):
                    pe.wait_ge(S.taken_by_act, count(l, "taken_by_act", j - 8))
                    pe.wait_ge(S.low_part, count(l, "low_part", j + 1))
                    by_columns(2 * (j % 2), j % 4).then_inc(S.block_used, 1)
                with pe.Fori(0, 3) as i:
                    for k in range(4):
                        j = J_GATE + 4 + k
                        pe.wait_ge(S.taken_by_act, count(l, "taken_by_act", 4 * i + j - 8))
                        pe.wait_ge(S.low_part, count(l, "low_part", 4 * i + j + 1))
                        by_columns(2 * (j % 2), j % 4).then_inc(S.block_used, 1)
                pe.wait_ge(S.pool_low, count(l, "pool_low", 4))

                def two_tiles(j, mh, ml):
                    for h in range(2):
                        for k in range(4):
                            w = slice((h * 4 + k) * P, (h * 4 + k + 1) * P)
                            m = passes(PS[:, 2 * (j % 2) + h, :], RH[:, j % 4, w], RL[:, j % 4, w],
                                       mh[:, k, :], ml[:, k, :], k == 0, k == 3)
                    m.then_inc(S.block_used, 1)

                for j in range(J_WPO, J_UQ):
                    if j < J_WPO + 2:
                        pe.wait_ge(S.taken_by_act, count(l, "taken_by_act", 4 + 15 + j - J_WPO))
                    else:
                        pe.wait_ge(S.taken_by_dve, count(l, "taken_by_dve", j - 22))
                    pe.wait_ge(S.low_part, count(l, "low_part", j + 1))
                    two_tiles(j, YH, YL)
                pe.wait_ge(S.taken_by_dve, count(l, "taken_by_dve", 10))
                pe.wait_ge(S.low_part, count(l, "low_part", J_UKV))
                for t in range(TT):
                    if t >= 2:
                        pe.wait_ge(S.qkv_taken, count(l, "qkv_taken", t - 1))
                    tok = slice(t * P, (t + 1) * P)
                    for h in range(2):
                        for k in range(QT_):
                            w = slice(h * 384, (h + 1) * 384)
                            m = passes(PS[:, 2 * (t % 2) + h, 0:384], CH[:, k, tok], CL[:, k, tok],
                                       RH[:, (J_UQ + k) % 4, w], RL[:, (J_UQ + k) % 4, w], k == 0, k == QT_ - 1)
                    m.then_inc(S.qkv_product, 1)
                pe.wait_ge(S.qkv_product, count(l, "qkv_product", 4))
                pe.sem_inc(S.block_used, 3)
                pe.wait_ge(S.low_part, count(l, "low_part", J_UKV + 2))
                for t in range(TT):
                    pe.wait_ge(S.qkv_taken, count(l, "qkv_taken", t + 3))
                    tok = slice(t * P, (t + 1) * P)
                    for h in range(2):
                        for k in range(KVT):
                            w = slice(h * 512, (h + 1) * 512)
                            m = passes(PS[:, 2 * (t % 2) + h, :], CH[:, QT_ + k, tok], CL[:, QT_ + k, tok],
                                       RH[:, (J_UKV + k) % 4, w], RL[:, (J_UKV + k) % 4, w], k == 0, k == KVT - 1)
                    m.then_inc(S.qkv_product, 1)
                pe.wait_ge(S.qkv_product, count(l, "qkv_product", 8))
                pe.sem_inc(S.block_used, 2)
                pe.wait_ge(S.qkv_taken, count(l, "qkv_taken", 8))
                apart(pe)

                with pe.Fori(0, HEADS) as h:
                    pe.wait_ge(S.head_sliced, count(l, "head_sliced", h + 1))
                    pe.wait_ge(S.head_stored, count(l, "head_stored", h))
                    for t in range(TT):
                        pe.transpose(PS[0:QK, 0, t * P:(t + 1) * P], QSL[:, t, :], IDN[:])
                    for t in range(TT):
                        m = pe.transpose(PS[0:QK, 1, t * P:(t + 1) * P], KSL[:, t, :], IDN[:])
                    m.then_inc(S.head_transposed, 1)
                    pe.wait_ge(S.head_ready, count(l, "head_ready", h + 1))
                    for t in range(TT):
                        pe.matmul(PS[:, 2 + t, :], QTR[0:QK, t * P:(t + 1) * P], KTR[0:QK, :],
                                  start=True, stop=True).then_inc(S.head_scores, 1)
                    for t in range(TT):
                        pe.wait_ge(S.head_exp, count(l, "head_exp", 4 * h + t + 1))
                        if t >= 2:
                            pe.wait_ge(S.probs_taken, count(l, "probs_taken", 4 * h + t - 1))
                        for k in range(TT):
                            m = pe.transpose(PS[:, 6 + t % 2, k * P:(k + 1) * P], PR[:, t, k * P:(k + 1) * P], IDN[:])
                        m.then_inc(S.probs_transposed, 1)
                    pe.wait_ge(S.probs_taken, count(l, "probs_taken", 4 * h + 4))
                    for t in range(TT):
                        for k in range(TT):
                            m = pe.matmul(PS[:, 0, t * VH:(t + 1) * VH], PT[:, k, t * P:(t + 1) * P],
                                          KV[:, k, bass.ds(h * P + NOPE, VH)], start=k == 0, stop=k == TT - 1)
                    m.then_inc(S.head_output, 1)
                pe.wait_ge(S.head_stored, count(l, "head_stored", HEADS))
                for w in range(4):
                    for t in range(TT):
                        m = pe.transpose(PS[:, 4 + w, t * P:(t + 1) * P], O[:, t, w * P:(w + 1) * P], IDN[:])
                    m.then_inc(S.attn_transposed, 1)
                pe.wait_ge(S.attn_low, count(l, "attn_low", 4))
                for j in range(J_WO, J_WOUT):
                    if j >= J_WO + 2:
                        pe.wait_ge(S.taken_by_dve, count(l, "taken_by_dve", 11 + j - J_WO - 2))
                    pe.wait_ge(S.low_part, count(l, "low_part", j + 1))
                    two_tiles(j, OH, OL)
                pe.wait_ge(S.taken_by_dve, count(l, "taken_by_dve", 14))
                pe.wait_ge(S.norm_low, count(l, "norm_low", KD + 0))
                pe.wait_ge(S.mix_high, count(l, "mix_high", 8))
                pe.wait_ge(S.mix_full, count(l, "mix_full", 8))
                pe.wait_ge(mix_low, l * 8 + 8)
                for j in range(J_WOUT, J_WQ):
                    pe.wait_ge(S.low_part, count(l, "low_part", j + 1))
                    h, kk = divmod(j - J_WOUT, 4)
                    for t in range(TT):
                        for i in range(2):
                            k, w, tok = 2 * kk + i, slice(i * 512, (i + 1) * 512), slice(t * P, (t + 1) * P)
                            m = passes(PS[:, 4 * h + t, :], XH[:, k, tok], XL[:, k, tok],
                                       RH[:, j % 4, w], RL[:, j % 4, w], k == 0, k == KD - 1)
                    m.then_inc(S.block_used, 1)

                pe.wait_ge(S.residual_added, count(l, "residual_added", 8))
                transpose_norm(1)
                pe.wait_ge(S.keys_loaded, count(l, "keys_loaded", 16))

                def fill(f, n, slot, bank, ks=range(KD)):
                    if ks[0] == 0:
                        pe.wait_ge(S.gelu_done, count(l, "gelu_done", f - 1))
                        pe.wait_ge(S.low_part, count(l, "low_part", n + 1))
                    m = by_columns(bank, slot, ks)
                    if ks[-1] == KD - 1:
                        m.then_inc(S.block_used, 1)

                def query(n, k, block, slot, fills):
                    pe.wait_ge(S.low_part, count(l, "low_part", block + 1))
                    by_columns(2 * (k % 2), slot).then_inc(S.block_used, 1)
                    for a in fills[:1]:
                        fill(*a)
                    pe.wait_ge(S.taken_by_act, count(l, "taken_by_act", 20 + n + 1))
                    pe.wait_ge(S.key_scores_taken, count(l, "key_scores_taken", n - 1))
                    for t in range(TT):
                        m = pe.matmul(PS[:, 4 + k % 2, t * P:(t + 1) * P], QF[:, k % 2, t * P:(t + 1) * P],
                                      KEYS[:, bass.ds(n * NK, NK)], start=True, stop=True)
                    m.then_inc(S.key_scores, 1)
                    for a in fills[1:]:
                        fill(*a)

                for q in range(4):
                    n = J_WQ + q if q < 2 else 44 + 3 * q
                    query(q, q, n, n % 4,
                          [(2 * q - 4 + m, n + 1 + m, (n + 1 + m) % 4, 6 + m) for m in range(2)] if q >= 2 else [])
                with pe.Fori(1, 4) as i:
                    for k in range(4):
                        n = 44 + 12 * i + 3 * k
                        query(4 * i + k, k, n, 3 * k % 4,
                              [(8 * i + 2 * k + m - 4, n + 1 + m, (3 * k + 1 + m) % 4, 6 + m) for m in range(2)])
                for f in range(28, 32):
                    fill(f, J_U + f, f % 4, 6 + f % 2)
                pe.wait_ge(S.choice_ready, count(l, "choice_ready", 1))
                for n, src in enumerate((I1, I2, GW)):
                    for t in range(TT):
                        m = pe.transpose(PS[:, n, t * P:(t + 1) * P], src[:, t, :], IDN[:])
                    m.then_inc(S.choice_transposed, 1)
                with pe.Fori(0, 8) as i:
                    for k in range(4):
                        f = 32 + 4 * i + k
                        for s in range(4):
                            n = 16 * i + 4 * k + s
                            pe.wait_ge(S.onehots_ready, count(l, "onehots_ready", n + 1))
                            pe.wait_ge(S.routing_taken, count(l, "routing_taken", n - 1))
                            for t in range(4):
                                m = pe.matmul(PS[:, 4 + s % 2, t * P:(t + 1) * P], OA[:, s % 2, t, :], OB[:, s % 2, t, :],
                                              start=True, stop=True)
                            m.then_inc(S.routed, 1)
                            fill(f, J_U + f, k, 6 + k % 2, range(2 * s, 2 * s + 2))

                def hidden(it, m):
                    c = FILLED + 4 * it + m
                    pe.wait_ge(S.gelu_done, count(l, "gelu_done", c - 3))
                    pe.wait_ge(S.low_part, count(l, "low_part", J_U + c + 1))
                    by_columns(m, m).then_inc(S.block_used, 1)

                def output(it, pair):
                    g = 4 * it + pair
                    pe.wait_ge(S.weighted_low, count(l, "weighted_low", 2 * g + 2))
                    pe.wait_ge(S.v_low, count(l, "v_low", 2 * g + 2))
                    for o in range(8):
                        t, h = divmod(o, 2)
                        pe.wait_ge(S.residual_added, count(l, "residual_added", 8 + 8 * g + o - 3))
                        for i in range(2):
                            s, tok, w = 2 * (pair % 2) + i, slice(t * P, (t + 1) * P), slice(h * 512, (h + 1) * 512)
                            m = passes(PS[:, 4 + o % 4, :], WHI[:, s, tok], WLO[:, s, tok],
                                       VHI[:, s, w], VLO[:, s, w], i == 0, i == 1)
                        m.then_inc(S.output_product, 1)

                pe.wait_ge(S.routing_taken, count(l, "routing_taken", 128))
                pe.wait_ge(S.gelu_done, count(l, "gelu_done", FILLED))
                apart(pe)
                with pe.Fori(0, 16) as it:
                    for half in range(2):
                        hidden(it, 2 * half)
                        hidden(it, 2 * half + 1)
                        output(it, 2 * half)
                        output(it, 2 * half + 1)

        @block.scalar
        def _(act):
            act.wait_ge(const_in, 80)
            act.wait_ge(trig_arg, 1)
            act.activation(SIN[:], ROTC[:, 0], ACT.Sin)
            act.activation(COS[:], ROTC[:, 1], ACT.Sin).then_inc(trig_made, 1)
            with act.Fori(0, LAYERS) as l:

                def hi(i, j):
                    n = 4 * i + j
                    act.wait_ge(sems[f"block_loaded{j % 2}"], 16 * (l * (JOBS // 2) + 2 * i + j // 2 + 1))
                    act.wait_ge(S.block_used, count(l, "block_used", n - 3))
                    act.activation(RH[:, j % 4, :], RAW[:, j % 2, :], ACT.Copy).then_inc(S.high_part, 1)

                def norm(n):
                    for t in range(TT):
                        m = act.activation(XS[:, t, :], X[:, t, :], ACT.Square, accum_out=NRM[:, 0, t:t + 1])
                    m.then_inc(S.squares_summed, 1)
                    act.wait_ge(S.variance_inverted, count(l, "variance_inverted", n + 1))
                    act.activation(NRM[:, 2, :], NRM[:, 1, :], ACT.Sqrt).then_inc(S.rms_ready, 1)

                def split_norm(n, gain):
                    for k in range(KD):
                        act.wait_ge(S.norm_transposed, count(l, "norm_transposed", KD * n + k + 1))
                        act.activation(XH[:, k, :], PS[:, k % 2, :], ACT.Copy,
                                       scale=VEC[:, gain + k:gain + k + 1]).then_inc(S.norm_high, 1)

                act.wait_ge(S.vectors_loaded, count(l, "vectors_loaded", 16))
                act.wait_ge(S.residual_added, count(l, "residual_added", 0))
                norm(0)
                hi(0, 0)
                hi(0, 1)
                split_norm(0, V_N1)
                for j in range(J_C, J_P):
                    hi(0, j + 2)
                    act.wait_ge(S.block_used, count(l, "block_used", j + 1))
                    act.activation(CH[:, j, :], PS[:, 2 * (j % 2), :], ACT.Copy,
                                   scale=VEC[:, V_QG + j:V_QG + j + 1])
                    act.activation(SQC[:, j, :], PS[:, 2 * (j % 2), :], ACT.Square).then_inc(S.latent_squared, 1)
                for j in range(J_P, J_KPE):
                    hi(0, j + 2)
                    act.wait_ge(S.block_used, count(l, "block_used", j + 1))
                    act.activation(PADDED[:, j - J_P, PAD:PAD + SEQ], PS[:, 2 * (j % 2), :],
                                   ACT.Copy).then_inc(S.taken_by_act, 1)
                hi(0, J_KPE + 2)
                act.wait_ge(S.latent_variance, count(l, "latent_variance", 1))
                act.activation(CN[:, 2, :], CN[:, 1, :], ACT.Sqrt).then_inc(S.latent_rms, 1)
                hi(0, J_POOL + 2)
                act.wait_ge(S.block_used, count(l, "block_used", J_POOL + 1))
                for g in range(GROUPS):
                    act.activation(YH[:, g, :], PS[:, 4 + g, :], ACT.Copy,
                                   scale=VEC[:, V_PS + g:V_PS + g + 1]).then_inc(S.pool_high, 1)
                with act.Fori(0, 4) as i:
                    for k in range(4):
                        j = J_GATE + k
                        hi(i, j + 2)
                        act.wait_ge(S.block_used, count(l, "block_used", 4 * i + j + 1))
                        act.activation(GAB[:, 4 * i + k, :], PS[:, 2 * (j % 2), :], ACT.Sigmoid,
                                       bias=VEC[:, bass.ds(V_GB + 4 * i + k, 1)]).then_inc(S.taken_by_act, 1)
                for j in range(J_WPO, J_UQ):
                    hi(0, j + 2)
                hi(0, J_UQ + 2)
                hi(0, J_UQ + 3)
                for t in range(TT):
                    act.wait_ge(S.qkv_product, count(l, "qkv_product", t + 1))
                    act.activation(Q[:, t].rearrange("p (x h) e -> p x (h e)", x=2),
                                   PS[:, 2 * (t % 2):2 * (t % 2) + 2, 0:384], ACT.Copy,
                                   scale=CN[:, 2, t:t + 1]).then_inc(S.qkv_taken, 1)
                hi(0, J_UQ + 4)
                for t in range(TT):
                    act.wait_ge(S.qkv_product, count(l, "qkv_product", t + 5))
                    act.activation(KV[:, t, :].rearrange("p (x e) -> p x e", x=2),
                                   PS[:, 2 * (t % 2):2 * (t % 2) + 2, :], ACT.Copy,
                                   scale=CN[:, 2, 4 + t:5 + t]).then_inc(S.qkv_taken, 1)
                hi(0, J_WO)
                hi(0, J_WO + 1)
                act.wait_ge(S.heads_variance, count(l, "heads_variance", 1))
                act.activation(SMALL[:, 0:64], SMALL[:, 128:192], ACT.Sqrt).then_inc(S.heads_rms, 1)
                with act.Fori(0, HEADS) as h:
                    act.wait_ge(S.head_transposed, count(l, "head_transposed", h + 1))
                    act.activation(QTR[0:QK, :], PS[0:QK, 0, :], ACT.Copy, scale=GQS[0:QK, :])
                    act.activation(KTR[0:QK, :], PS[0:QK, 1, :], ACT.Copy,
                                   scale=VEC[0:QK, V_KH:V_KH + 1]).then_inc(S.head_ready, 1)
                    for t in range(TT):
                        act.wait_ge(S.head_max, count(l, "head_max", 4 * h + t + 1))
                        act.activation(PR[:, t, :], PS[:, 2 + t, :], ACT.Exp, bias=NMX[:, t:t + 1],
                                       accum_out=RSM[:, t:t + 1]).then_inc(S.head_exp, 1)
                for w in range(4):
                    act.wait_ge(S.attn_transposed, count(l, "attn_transposed", w + 1))
                    act.activation(OH[:, w, :], PS[:, 4 + w, :], ACT.Copy).then_inc(S.attn_high, 1)
                for j in range(J_WO, J_WOUT):
                    hi(0, j + 2)
                    for m in range(2):
                        n = 2 * (j - J_WO) + m
                        act.wait_ge(S.mix_full, count(l, "mix_full", n + 1))
                        act.activation(XH[:, n, :], T2[:, n % 2, :], ACT.Copy).then_inc(S.mix_high, 1)
                for j in range(J_WOUT, J_WQ):
                    hi(0, j + 2)
                act.wait_ge(S.residual_added, count(l, "residual_added", 8))
                norm(1)
                split_norm(1, V_N2)

                def take_query(n, k, block):
                    act.wait_ge(S.block_used, count(l, "block_used", block + 1))
                    act.wait_ge(S.key_scores, count(l, "key_scores", n - 1))
                    act.activation(QF[:, k % 2, :], PS[:, 2 * (k % 2), :], ACT.Copy).then_inc(S.taken_by_act, 1)

                def fill_gelu(f, n, turn, slot):
                    act.wait_ge(S.block_used, count(l, "block_used", n + 1))
                    if not isinstance(f, int) or f >= 4:
                        act.wait_ge(sems[f"gelu_stored{slot}"], count(l, f"gelu_stored{slot}", 16 * turn))
                    act.activation(GS[:, slot, :], PS[:, 6 + slot % 2, :], ACT.Gelu_apprx_tanh).then_inc(S.gelu_done, 1)

                for q in range(4):
                    n = J_WQ + q if q < 2 else 44 + 3 * q
                    hi(0, n + 2)
                    take_query(q, q, n)
                    if q >= 2:
                        for m in range(2):
                            hi(0, n + 3 + m)
                            f = 2 * q - 4 + m
                            fill_gelu(f, n + 1 + m, 0, f)
                with act.Fori(1, 4) as i:
                    for k in range(4):
                        j = 44 + 3 * k
                        hi(3 * i, j + 2)
                        take_query(4 * i + k, k, 12 * i + j)
                        for m in range(2):
                            hi(3 * i, j + 3 + m)
                            fill_gelu(8 * i + 2 * k + m - 4, 12 * i + j + 1 + m, 2 * i - 1 + (2 * k + m) // 4, (2 * k + m) % 4)
                for f in range(28, 32):
                    hi(0, J_U + f + 2)
                    fill_gelu(f, J_U + f, f // 4, f % 4)
                act.wait_ge(S.best_shifted, count(l, "best_shifted", 1))
                act.activation(GW[:], BV[:], ACT.Exp).then_inc(S.best_exp, 1)
                with act.Fori(0, NTB // 2) as b:
                    for k in range(8):
                        hi(2 * b, J_U + 32 + k + 2)
                        if k % 4 == 0:
                            s = k // 4
                            act.wait_ge(sems[f"routing_stored{s}"], count(l, f"routing_stored{s}", 16 * b))
                        for n in range(4):
                            act.wait_ge(S.routed, count(l, "routed", 32 * b + 4 * k + n + 1))
                            tok = 16 * (k % 4) + 4 * n
                            act.activation(STAGE[s][:, :, tok:tok + 4], PS[:, 4 + n % 2, :].rearrange("p (t i) -> p i t", t=4),
                                           ACT.Copy).then_inc(S.routing_taken, 1)
                        f = 32 + 8 * b + k
                        fill_gelu(f, J_U + f, 8 + 2 * b + k // 4, k % 4)

                def position(it, q, last=False):
                    n, new, m = 8 * it + q, q // 2 % 2, 2 * (q // 4) + q % 2
                    if not new and not (last and q >= 4):
                        hi(it, J_U + FILLED + m + 2)
                    act.wait_ge(sems[f"v_loaded{q % 2}"], 16 * (l * 64 + 4 * it + q // 2 + 1))
                    act.wait_ge(S.output_product, count(l, "output_product", 8 * (4 * it + q // 2) - 8))
                    act.activation(VHI[:, q % 4, :], VRAW[:, q % 2, :], ACT.Copy).then_inc(S.v_high, 1)
                    if new:
                        act.wait_ge(S.block_used, count(l, "block_used", J_U + FILLED + 4 * it + m + 1))
                        act.wait_ge(S.weighted, count(l, "weighted", n - 3))
                        act.activation(GEL[:, q % 2, :], PS[:, m, :], ACT.Gelu_apprx_tanh).then_inc(S.gelu_done, 1)
                    act.wait_ge(S.weighted, count(l, "weighted", n + 1))
                    act.activation(WHI[:, q % 4, :], WF[:, q % 2, :], ACT.Copy).then_inc(S.weighted_high, 1)

                with act.Fori(0, 15) as it:
                    for q in range(8):
                        position(it, q)
                for q in range(8):
                    position(15, q, last=True)

        @block.vector
        def _(dve):
            dve.memset(ONES[:], 1.0)
            dve.wait_ge(iota_made, 1)
            dve.wait_ge(const_in, 80)
            POSF, ANG, TURN = WA[:, 0:TT], ROTC[:, 2], ROTC[:, 3]
            dve.tensor_copy(POSF, PADDED[:, 0, 0:TT].bitcast(I32))
            dve.drain()
            dve.tensor_tensor(ANG, COS[:, 0, :].unsqueeze(1).to_broadcast([P, TT, HALF]),
                              POSF.unsqueeze(2).to_broadcast([P, TT, HALF]), ALU.mult)
            dve.drain()
            magic = 1.5 * 2.0 ** 23
            dve.tensor_scalar(TURN, ANG, 1 / (2 * np.pi), magic, ALU.mult, ALU.add)
            dve.drain()
            dve.tensor_scalar(TURN, TURN, -magic, None, ALU.add)
            dve.drain()
            c1 = 6.28125
            c2 = float(np.float32(np.round((2 * np.pi - c1) * 2.0 ** 21) / 2.0 ** 21))
            c3 = 2 * np.pi - c1 - c2
            for c in (c1, c2, c3):
                dve.scalar_tensor_tensor(ANG, TURN, -c, ANG, ALU.mult, ALU.add)
                dve.drain()
            top = float(np.float32(3.1415925))
            dve.tensor_scalar(ROTC[:, 0], ANG, top, -top, ALU.min, ALU.max)
            dve.tensor_scalar(ROTC[:, 1], ANG, np.pi / 2, None, ALU.add)
            dve.drain()
            dve.tensor_scalar(TURN, ROTC[:, 1], top, -2 * np.pi, ALU.is_gt, ALU.mult)
            dve.drain()
            dve.tensor_tensor(ROTC[:, 1], ROTC[:, 1], TURN, ALU.add)
            dve.drain()
            dve.tensor_scalar(ROTC[:, 1], ROTC[:, 1], top, -top, ALU.min, ALU.max).then_inc(trig_arg, 1)
            dve.wait_ge(trig_made, 1)
            dve.drain()
            with dve.Fori(0, LAYERS) as l:

                def norm(n):
                    dve.wait_ge(S.squares_summed, count(l, "squares_summed", n + 1))
                    dve.tensor_scalar(NRM[:, 0, :], NRM[:, 0, :], 1.0 / D, EPS, ALU.mult, ALU.add)
                    dve.drain()
                    dve.reciprocal(NRM[:, 1, :], NRM[:, 0, :]).then_inc(S.variance_inverted, 1)
                    dve.wait_ge(S.rms_ready, count(l, "rms_ready", n + 1))
                    for t in range(TT):
                        m = dve.tensor_scalar(XS[:, t, :], X[:, t, :], NRM[:, 2, t:t + 1], None, ALU.mult)
                    m.then_inc(S.rows_normed, 1)

                def split_norm(n, gain):
                    for k in range(KD):
                        dve.wait_ge(S.norm_high, count(l, "norm_high", KD * n + k + 1))
                        dve.scalar_tensor_tensor(XL[:, k, :], PS[:, k % 2, :], VEC[:, gain + k:gain + k + 1],
                                                 XH[:, k, :].bitcast(F32), ALU.mult, ALU.subtract).then_inc(S.norm_low, 1)

                dve.wait_ge(S.vectors_loaded, count(l, "vectors_loaded", 16))
                dve.tensor_scalar(GQS[:], VEC[:, V_QH:V_QH + 1], QK ** -0.5, None, ALU.mult)
                norm(0)
                split_norm(0, V_N1)
                for g in range(GROUPS):
                    dve.memset(PADDED[:, g, 0:PAD], 0.0)
                    m = dve.memset(PADDED[:, g, PAD + SEQ:], 0.0)
                dve.drain()
                for j in range(J_C, J_P):
                    dve.wait_ge(S.latent_squared, count(l, "latent_squared", j + 1))
                    dve.scalar_tensor_tensor(CL[:, j, :], PS[:, 2 * (j % 2), :], VEC[:, V_QG + j:V_QG + j + 1],
                                             CH[:, j, :].bitcast(F32), ALU.mult, ALU.subtract).then_inc(S.taken_by_dve, 1)
                dve.wait_ge(S.taken_by_act, count(l, "taken_by_act", 4))
                for g in range(GROUPS):
                    src = PADDED[:, g, :]
                    bufs = (WA, WB)
                    dve.tensor_tensor(WA[:, 1:528], src[:, 1:528], src[:, 0:527], ALU.add)
                    dve.drain()
                    have = 0
                    lo_i, hi_i = 1, 528
                    for step in range(g):
                        d = 2 ** step
                        lo_i, hi_i = lo_i + d, hi_i - d
                        a, b = bufs[have], bufs[1 - have]
                        dve.tensor_tensor(b[:, lo_i:hi_i], a[:, lo_i - d:hi_i - d], a[:, lo_i + d:hi_i + d], ALU.add)
                        dve.drain()
                        have = 1 - have
                    win = bufs[have]
                    dve.tensor_tensor(win[:, PAD:2 * PAD], win[:, PAD:2 * PAD], EDGE[:, g, 0, :], ALU.mult)
                    dve.tensor_tensor(win[:, SEQ:SEQ + PAD], win[:, SEQ:SEQ + PAD], EDGE[:, g, 1, :], ALU.mult)
                    dve.drain()
                    other = bufs[1 - have]
                    dve.scalar_tensor_tensor(other[:, 0:SEQ], win[:, PAD:PAD + SEQ], 0.5 ** (g + 1),
                                             src[:, PAD:PAD + SEQ], ALU.mult, ALU.subtract)
                    dve.drain()
                    dve.tensor_copy(MIXH[:, g, :], other[:, 0:SEQ])
                    dve.drain()
                    m = dve.tensor_tensor(MIXL[:, g, :], other[:, 0:SEQ], MIXH[:, g, :].bitcast(F32), ALU.subtract)
                    if g == GROUPS - 1:
                        m.then_inc(S.window_means, 1)
                    dve.drain()
                dve.wait_ge(S.block_used, count(l, "block_used", J_KPE + 1))
                dve.tensor_copy(KPE[:].rearrange("p t e -> p (t e)"), PS[:, 2, 0:TT * ROPE]).then_inc(S.taken_by_dve, 1)
                dve.wait_ge(S.latent_summed, count(l, "latent_summed", 1))
                dve.tensor_scalar(CN[:, 0, 0:4], PS[:, 7, 0:4], 1.0 / Q_LORA, EPS, ALU.mult, ALU.add)
                dve.tensor_scalar(CN[:, 0, 4:8], PS[:, 7, 4:8], 1.0 / KV_LORA, EPS, ALU.mult, ALU.add)
                dve.drain()
                dve.reciprocal(CN[:, 1, :], CN[:, 0, :]).then_inc(S.latent_variance, 1)
                for g in range(GROUPS):
                    dve.wait_ge(S.pool_high, count(l, "pool_high", g + 1))
                    dve.scalar_tensor_tensor(YL[:, g, :], PS[:, 4 + g, :], VEC[:, V_PS + g:V_PS + g + 1],
                                             YH[:, g, :].bitcast(F32), ALU.mult, ALU.subtract).then_inc(S.pool_low, 1)
                dve.wait_ge(S.taken_by_act, count(l, "taken_by_act", 20))
                for j in range(J_WPO, J_UQ):
                    dve.wait_ge(S.block_used, count(l, "block_used", j + 1))
                    for m in range(2):
                        n = KD + 2 * (j - J_WPO) + m
                        ins = dve.tensor_tensor(GAB[:, n, :], PS[:, 2 * (j % 2) + m, :], GAB[:, n, :], ALU.mult)
                    ins.then_inc(S.taken_by_dve, 1)
                dve.wait_ge(S.qkv_taken, count(l, "qkv_taken", 8))
                cosq = COS[:].unsqueeze(2).to_broadcast([P, TT, HEADS, HALF])
                sinq = SIN[:].unsqueeze(2).to_broadcast([P, TT, HEADS, HALF])

                def rotate(x1, x2, cos, sin, r):
                    dve.tensor_tensor(r[0], x1, cos, ALU.mult)
                    dve.tensor_tensor(r[1], x2, sin, ALU.mult)
                    dve.tensor_tensor(r[2], x1, sin, ALU.mult)
                    dve.tensor_tensor(r[3], x2, cos, ALU.mult)
                    dve.drain()
                    dve.tensor_tensor(x1, r[0], r[1], ALU.subtract)
                    dve.tensor_tensor(x2, r[2], r[3], ALU.add)
                    dve.drain()

                rotate(Q[:, :, :, NOPE:NOPE + HALF], Q[:, :, :, NOPE + HALF:QK], cosq, sinq,
                       [ROT[:, n, :].rearrange("p (t h e) -> p t h e", t=TT, h=HEADS) for n in range(4)])
                rotate(KPE[:, :, 0:HALF], KPE[:, :, HALF:ROPE], COS[:], SIN[:],
                       [ROT[:, n, 0:TT * HALF].rearrange("p (t e) -> p t e", t=TT) for n in range(4)])
                qv = Q[:].rearrange("p t h e -> p (t h) e")
                kn = KV[:].rearrange("p t (h e) -> p (t h) e", h=HEADS)[:, :, 0:NOPE]
                dve.tensor_tensor(SQT[:], qv, qv, ALU.mult)
                dve.drain()
                dve.tensor_reduce(SMALL[:, 128:160], SQT[:], AX, ALU.add)
                dve.drain()
                dve.tensor_tensor(SQT[:, :, 0:NOPE], kn, kn, ALU.mult)
                dve.tensor_tensor(ROT[:, 0, 0:TT * ROPE].rearrange("p (t e) -> p t e", t=TT), KPE[:], KPE[:], ALU.mult)
                dve.drain()
                dve.tensor_reduce(SMALL[:, 160:192], SQT[:, :, 0:NOPE], AX, ALU.add)
                dve.tensor_reduce(KPS, ROT[:, 0, 0:TT * ROPE].rearrange("p (t e) -> p t e", t=TT), AX, ALU.add)
                dve.drain()
                sk = SMALL[:, 160:192].rearrange("p (t h) -> p t h", t=TT)
                dve.tensor_tensor(sk, sk, KPS.unsqueeze(2).to_broadcast([P, TT, HEADS]), ALU.add)
                dve.drain()
                dve.tensor_scalar(SMALL[:, 128:192], SMALL[:, 128:192], 1.0 / QK, EPS, ALU.mult, ALU.add)
                dve.drain()
                dve.reciprocal(SMALL[:, 128:192], SMALL[:, 128:192]).then_inc(S.heads_variance, 1)
                dve.wait_ge(S.heads_rms, count(l, "heads_rms", 1))
                apart(dve)
                with dve.Fori(0, HEADS) as h:
                    def head_scale(r, n):
                        return r[:, :, bass.ds(h, 1)].to_broadcast([P, TT, n])

                    dve.tensor_tensor(QSL[:], Q[:, :, bass.ds(h, 1), :].rearrange("p t o e -> p (t o) e"),
                                      head_scale(RQ, QK), ALU.mult)
                    dve.tensor_tensor(KSL[:, :, 0:NOPE], KV[:, :, bass.ds(h * P, NOPE)], head_scale(RK, NOPE), ALU.mult)
                    dve.tensor_tensor(KSL[:, :, NOPE:QK], KPE[:], head_scale(RK, ROPE), ALU.mult).then_inc(S.head_sliced, 1)
                    for t in range(TT):
                        dve.wait_ge(S.head_scores, count(l, "head_scores", 4 * h + t + 1))
                        dve.tensor_reduce(NMX[:, t:t + 1], PS[:, 2 + t, :], AX, ALU.max, negate=True).then_inc(S.head_max, 1)
                    for t in range(TT):
                        dve.wait_ge(S.probs_transposed, count(l, "probs_transposed", 4 * h + t + 1))
                        dve.tensor_copy(PT[:, :, t * P:(t + 1) * P],
                                        PS[:, 6 + t % 2, :].rearrange("p (k q) -> p k q", k=TT)).then_inc(S.probs_taken, 1)
                    dve.wait_ge(S.head_exp, count(l, "head_exp", 4 * h + 4))
                    dve.reciprocal(RIN, RSM)
                    dve.drain()
                    dve.wait_ge(S.head_output, count(l, "head_output", h + 1))
                    dve.tensor_tensor(O[:, :, bass.ds(h * VH, VH)],
                                      PS[:, 0, 0:TT * VH].rearrange("p (t e) -> p t e", t=TT),
                                      RIN.unsqueeze(2).to_broadcast([P, TT, VH]), ALU.mult).then_inc(S.head_stored, 1)
                    dve.drain()
                for w in range(4):
                    dve.wait_ge(S.attn_high, count(l, "attn_high", w + 1))
                    dve.tensor_tensor(OL[:, w, :], PS[:, 4 + w, :], OH[:, w, :].bitcast(F32), ALU.subtract).then_inc(S.attn_low, 1)
                for j in range(J_WO, J_WOUT):
                    dve.wait_ge(S.block_used, count(l, "block_used", j + 1))
                    for m in range(2):
                        n = 2 * (j - J_WO) + m
                        dve.tensor_tensor(T2[:, m, :], PS[:, 2 * (j % 2) + m, :], GAB[:, n, :], ALU.mult)
                        dve.drain()
                        dve.tensor_tensor(T2[:, m, :], T2[:, m, :], GAB[:, KD + n, :], ALU.add).then_inc(S.mix_full, 1)
                        dve.wait_ge(S.mix_high, count(l, "mix_high", n + 1))
                        dve.tensor_tensor(XL[:, n, :], T2[:, m, :], XH[:, n, :].bitcast(F32), ALU.subtract).then_inc(mix_low, 1)
                    dve.drain()
                    dve.engine_nop().then_inc(S.taken_by_dve, 1)
                for j in range(J_WOUT, J_WQ):
                    h, kk = divmod(j - J_WOUT, 4)
                    if kk == 3:
                        dve.wait_ge(S.block_used, count(l, "block_used", j + 1))
                        for t in range(TT):
                            w = slice(h * 512, (h + 1) * 512)
                            dve.tensor_tensor(X[:, t, w], PS[:, 4 * h + t, :], X[:, t, w], ALU.add).then_inc(S.residual_added, 1)
                norm(1)
                split_norm(1, V_N2)

                def best16(n, vals, idx, src, work):
                    for t in range(TT):
                        dve.max(vals(t)[:, 0:8], src(t))
                    dve.drain()
                    for t in range(TT):
                        dve.max_index(idx(t)[:, 0:8], vals(t)[:, 0:8], src(t))
                        m = dve.match_replace(work(t), vals(t)[:, 0:8], src(t), -3.0e38)
                    dve.drain()
                    for t in range(TT):
                        dve.max(vals(t)[:, 8:16], work(t))
                    dve.drain()
                    for t in range(TT):
                        dve.max_index(idx(t)[:, 8:16], vals(t)[:, 8:16], work(t))
                    return m

                with dve.Fori(0, 4) as i:
                    for head in range(2):
                        for half in range(2):
                            k = 2 * head + half
                            dve.wait_ge(S.key_scores, count(l, "key_scores", 4 * i + k + 1))
                            apart(dve)
                            best16(0, lambda t: V16[:, t, half, :], lambda t: I16[:, t, half, :],
                                   lambda t: PS[:, 4 + k % 2, t * P:(t + 1) * P], lambda t: SW[:, t, :])
                            dve.drain()
                            dve.engine_nop().then_inc(S.key_scores_taken, 1)
                        dve.tensor_tensor(CAND[:].rearrange("p t (a b) -> p t a b", a=TOPK),
                                          V16[:, :, 0, :].unsqueeze(3).to_broadcast([P, TT, TOPK, TOPK]),
                                          V16[:, :, 1, :].unsqueeze(2).to_broadcast([P, TT, TOPK, TOPK]), ALU.add)
                        dve.tensor_copy(F16[:], I16[:])
                        dve.drain()
                        best16(0, lambda t: B16[:, t, :], lambda t: J16[:, t, :], lambda t: CAND[:, t, :],
                               lambda t: CW[:, t, :])
                        dve.drain()
                        dve.tensor_scalar(JHL[:, 0], J16[:], 4, None, ALU.logical_shift_right)
                        dve.tensor_scalar(JHL[:, 1], J16[:], 15, None, ALU.bitwise_and)
                        dve.drain()
                        dve.tensor_copy(JF[:], JHL[:])
                        dve.tensor_copy(BV[:, :, bass.ds((2 * i + head) * TOPK, TOPK)], B16[:])
                        dve.drain()
                        ramp = IOTA[:, 0:TOPK].unsqueeze(1).to_broadcast([P, TOPK, TOPK])
                        for half, (e, dst) in enumerate(((EQ, I1), (EQ2, I2))):
                            for t in range(TT):
                                dve.tensor_tensor(e[:, t], JF[:, half, t, :].unsqueeze(2).to_broadcast([P, TOPK, TOPK]),
                                                  ramp, ALU.is_equal)
                        dve.drain()
                        for half, e in enumerate((EQ, EQ2)):
                            dve.tensor_tensor(e[:], e[:], F16[:, :, half, :].unsqueeze(2).to_broadcast([P, TT, TOPK, TOPK]),
                                              ALU.mult)
                        dve.drain()
                        for e, dst in ((EQ, I1), (EQ2, I2)):
                            dve.tensor_reduce(dst[:, :, bass.ds((2 * i + head) * TOPK, TOPK)], e[:], AX, ALU.add)
                        dve.drain()
                bv = BV[:].rearrange("p t (h k) -> p (t h) k", k=TOPK)
                gw = GW[:].rearrange("p t (h k) -> p (t h) k", k=TOPK)
                dve.tensor_copy(BS[:, 0, :].unsqueeze(2), bv[:, :, 0:1])
                dve.drain()
                dve.tensor_tensor(bv, bv, BS[:, 0, :].unsqueeze(2).to_broadcast([P, TT * PH, TOPK]),
                                  ALU.subtract).then_inc(S.best_shifted, 1)
                dve.wait_ge(S.best_exp, count(l, "best_exp", 1))
                dve.tensor_reduce(BS[:, 1, :], gw, AX, ALU.add)
                dve.drain()
                dve.reciprocal(BS[:, 1, :], BS[:, 1, :])
                dve.drain()
                dve.tensor_tensor(gw, gw, BS[:, 1, :].unsqueeze(2).to_broadcast([P, TT * PH, TOPK]),
                                  ALU.mult).then_inc(S.choice_ready, 1)
                for n in range(3):
                    dve.wait_ge(S.choice_transposed, count(l, "choice_transposed", n + 1))
                    dve.tensor_copy(IT[:, n, :], PS[:, n, :])
                dve.drain()

                with dve.Fori(0, 64) as i:
                    for s in range(2):
                        dve.wait_ge(S.routed, count(l, "routed", 2 * i + s - 1))
                        for t in range(4):
                            tok = 8 * i + 4 * s + t
                            dve.tensor_scalar(OA[:, s, t, :], IOTA[:], IT[:, 0, bass.ds(tok, 1)], None, ALU.is_equal)
                            m = dve.tensor_scalar(OB[:, s, t, :], IOTA[:], IT[:, 1, bass.ds(tok, 1)],
                                                  IT[:, 2, bass.ds(tok, 1)], ALU.is_equal, ALU.mult)
                        m.then_inc(S.onehots_ready, 1)

                def add_outputs(g, first):
                    for o in range(first, first + 4):
                        t, h = divmod(o, 2)
                        w = slice(h * 512, (h + 1) * 512)
                        dve.wait_ge(S.output_product, count(l, "output_product", 8 * g + o + 1))
                        dve.tensor_tensor(X[:, t, w], PS[:, 4 + o % 4, :], X[:, t, w], ALU.add).then_inc(S.residual_added, 1)

                def position(it, q, first=False):
                    n, new = 8 * it + q, q // 2 % 2
                    if new:
                        gelu = GEL[:, q % 2, :]
                        dve.wait_ge(S.gelu_done, count(l, "gelu_done", FILLED + 4 * it + 2 * (q // 4) + q % 2 + 1))
                    else:
                        gelu = GB[:, q // 4, q % 2, :]
                        dve.wait_ge(sems[f"gelu_loaded{q // 4}"], count(l, f"gelu_loaded{q // 4}", 16 * it + 16))
                    dve.wait_ge(sems[f"routing_loaded{new}"], 16 * (l * 32 + 2 * it + q // 4 + 1))
                    dve.tensor_tensor(WF[:, q % 2, :].rearrange("p (b t) -> p b t", b=NTB),
                                      gelu.rearrange("p (b t) -> p b t", b=NTB),
                                      GC[:, new, :, q % 2, :], ALU.mult).then_inc(S.weighted, 1)
                    dve.wait_ge(S.v_high, count(l, "v_high", n + 1))
                    dve.tensor_tensor(VLO[:, q % 4, :], VRAW[:, q % 2, :], VHI[:, q % 4, :].bitcast(F32),
                                      ALU.subtract).then_inc(S.v_low, 1)
                    dve.wait_ge(S.weighted_high, count(l, "weighted_high", n + 1))
                    dve.tensor_tensor(WLO[:, q % 4, :], WF[:, q % 2, :], WHI[:, q % 4, :].bitcast(F32),
                                      ALU.subtract).then_inc(S.weighted_low, 1)
                    if not (first and q < 2):
                        add_outputs(4 * it + q // 2 - 1, 4 * (q % 2))
                    dve.drain()

                for q in range(8):
                    position(0, q, first=True)
                with dve.Fori(1, 16) as it:
                    for q in range(8):
                        position(it, q)
                add_outputs(63, 0)
                add_outputs(63, 4)
                dve.drain()

        @block.gpsimd
        def _(pool):
            for name, value in STARTS.items():
                pool.sem_inc(sems[name], value)
            pool.iota(IOTA[:], [[1, P]], base=0, channel_multiplier=0,
                      allow_small_or_imprecise_dtypes=True).then_inc(iota_made, 1)
            with pool.Fori(0, LAYERS) as l:
                with pool.Fori(0, JOBS // 4) as i:
                    for k in range(4):
                        pool.wait_ge(S.high_part, count(l, "high_part", 4 * i + k + 1))
                        pool.tensor_tensor(RL[:, k, :], RAW[:, k % 2, :], RH[:, k, :].bitcast(F32),
                                           ALU.subtract).then_inc(S.low_part, 1)


def laid_out(x, positions, norm1_g, w_in, q_lora_g, kv_lora_g, w_uq, w_ukv, q_head_g, k_head_g,
             w_o_mla, pool_w, pool_scale, w_pool_out, gate_bias, w_out, norm2_g,
             peer_wq, peer_keys, peer_u, peer_v):
    f = np.float32
    L = LAYERS
    stream = np.zeros((L, J_U, P, 1024), f)
    cols = lambda w, a, b: w[:, :, a:b].reshape(L, KD, P, (b - a) // P, P).transpose(0, 3, 2, 1, 4).reshape(L, -1, P, D)
    p0 = Q_LORA + KV_LORA + ROPE
    stream[:, J_C:J_P] = cols(w_in, 0, Q_LORA + KV_LORA)
    stream[:, J_P:J_KPE] = cols(w_in, p0, p0 + 512)
    stream[:, J_KPE, :, :KD * ROPE] = w_in[:, :, Q_LORA + KV_LORA:p0].reshape(L, KD, P, ROPE).transpose(0, 2, 1, 3).reshape(L, P, -1)
    stream[:, J_POOL, :, :512] = pool_w.transpose(0, 2, 1, 3).reshape(L, P, 512)
    stream[:, J_GATE:J_WPO] = cols(w_in, p0 + 512, p0 + 512 + 2 * D)
    tiles = lambda w: w.reshape(L, 4, P, 4, 2, P).transpose(0, 3, 2, 4, 1, 5).reshape(L, 4, P, D)
    stream[:, J_WPO:J_UQ] = tiles(w_pool_out)
    stream[:, J_UQ:J_UKV, :, :768] = w_uq.reshape(L, QT_, P, 768)
    stream[:, J_UKV:J_WO] = w_ukv.reshape(L, KVT, P, D)
    stream[:, J_WO:J_WOUT] = tiles(w_o_mla)
    stream[:, J_WOUT:J_WQ] = w_out.reshape(L, 4, 2, P, 2, 512).transpose(0, 4, 1, 3, 2, 5).reshape(L, 8, P, D)
    stream[:, J_WQ:J_U] = cols(peer_wq, 0, 2048)
    vecs = np.zeros((L, P, V_ALL), f)
    for at, a in ((V_N1, norm1_g), (V_N2, norm2_g), (V_QG, q_lora_g), (V_KVG, kv_lora_g), (V_PS, pool_scale),
                  (V_GB, gate_bias.reshape(L, -1))):
        a = a.reshape(L, -1, P).transpose(0, 2, 1)
        vecs[:, :, at:at + a.shape[2]] = a
    vecs[:, :QK, V_QH] = q_head_g
    vecs[:, :QK, V_KH] = k_head_g
    edge = np.ones((GROUPS, 2, PAD), f)
    for g in range(GROUPS):
        h = 2 ** g
        for c in range(PAD):
            edge[g, 0, c] = 2 * h / min(c + h, 2 * h)
            edge[g, 1, c] = 2 * h / min(PAD - c + h, 2 * h)
    inv = (10000.0 ** (-np.arange(0, ROPE, 2, dtype=np.float64) / ROPE)).astype(f)
    return {
        "x": x,
        "pos": np.ascontiguousarray(positions.reshape(TT, P).T),
        "inv_freq": np.tile(inv, (P, 1)),
        "ident": np.eye(P, dtype=f),
        "edge": np.tile(edge.reshape(1, -1), (P, 1)),
        "vecs": vecs,
        "stream": stream,
        "peer_keys": np.ascontiguousarray(peer_keys.transpose(0, 4, 1, 2, 3).reshape(L, P, -1)),
        "peer_u": np.ascontiguousarray(peer_u.reshape(L, NK, NK, KD, P).transpose(0, 2, 4, 3, 1).reshape(L, NK, P, D)),
        "peer_v": peer_v.reshape(L, NK, NK, D),
    }


def kernel(**inputs):
    import concourse.bacc as bacc
    from concourse.bass_utils import run_bass_kernel_spmd

    arrays = laid_out(**{n: np.asarray(a) for n, a in inputs.items()})
    nc = bacc.Bacc("TRN2", target_bir_lowering=False, num_devices=1)
    aps = {n: nc.dram_tensor(f"in_{n}", a.shape, mybir.dt.from_np(a.dtype), kind="ExternalInput").ap()
           for n, a in arrays.items()}
    out = nc.dram_tensor("out", (1, SEQ, D), F32, kind="ExternalOutput").ap()
    program(nc, out=out, **aps)
    r = run_bass_kernel_spmd(nc, [{f"in_{n}": a for n, a in arrays.items()}], core_ids=[0])
    return r.results[0]["out"]
```

```python
from contextlib import ExitStack

import numpy as np

import concourse.bass as bass
from concourse import mybir

ACT = mybir.ActivationFunctionType
ALU = mybir.AluOpType
AX = mybir.AxisListType.X
F32 = mybir.dt.float32
F32R = mybir.dt.float32r
U32 = mybir.dt.uint32
I32 = mybir.dt.int32
BF16 = mybir.dt.bfloat16

P = 128
LAYERS = 2
SEQ = 512
D = 1024
TT = SEQ // P
KD = D // P
HEADS, NOPE, ROPE, VH = 8, 64, 32, 64
QK = NOPE + ROPE
HALF = ROPE // 2
Q_LORA, KV_LORA = 384, 256
QT_, KVT = Q_LORA // P, KV_LORA // P
GROUPS = 4
PAD = 8
NK = 128
TOPK = 16
CANDS = TOPK + (TOPK - 1) * TOPK // 2
PH = 8
EPS = 1e-6

J_C, J_P, J_KPE, J_UQ, J_UKV, J_POOL, J_WPO = 0, 5, 9, 10, 13, 15, 16
J_GATE, J_WO, J_WOUT, J_WQ, J_U = 20, 36, 40, 48, 64
JOBS = J_U + NK
FILLED = 64
FIRST = 30

V_N1, V_N2, V_QG, V_KVG, V_PS, V_GB, V_QH, V_KH, V_ALL = 0, 8, 16, 19, 21, 25, 41, 42, 43

TB = 64
NTB = SEQ // TB

PER = dict(
    vectors_loaded=16, keys_loaded=16, block_loaded0=16 * JOBS // 2, block_loaded1=16 * JOBS // 2,
    high_part=JOBS, low_part=JOBS, block_used=JOBS, squares_summed=2, variance_inverted=2, rms_ready=2,
    rows_normed=4, norm_transposed=2 * KD, norm_high=2 * KD, norm_low=2 * KD, taken_by_act=40,
    taken_by_dve=10, latent_squared=5, latent_summed=1, latent_variance=1, latent_rms=1, kpe_taken=1,
    kpe_transposed=1, window_means=4, pool_product=4, pool_high=4, pool_low=4, qkv_product=8, qkv_taken=8,
    heads_variance=1, heads_rms=1, head_sliced=8, head_transposed=8, head_high=8, head_low=8,
    gate_applied=16, head_scores=32, head_max=32, head_exp=32, probs_transposed=32,
    probs_taken=32, head_output=8, head_stored=8, attn_transposed=4, attn_high=4, attn_low=4, mix_full=8,
    mix_high=8, key_scores=16, key_scores_taken=16, best_shifted=8, best_exp=1, choice_ready=1,
    choice_transposed=3, onehots_ready=64, routed=128, routing_taken=128, routing_stored0=64,
    routing_stored1=64, v_loaded0=1024, v_loaded1=1024, v_high=128, v_low=128, gelu_done=128, weighted=128,
    weighted_high=128, weighted_low=128, routing_loaded0=512, routing_loaded1=512, output_product=512,
    residual_added=8 + 512, projected=8,
    gelu_stored0=256, gelu_stored1=256, gelu_stored2=256, gelu_stored3=256, gelu_loaded0=256, gelu_loaded1=256,
)

STARTS = dict(low_part=2, block_used=4, residual_added=7, weighted=4, v_low=2, head_stored=1, key_scores=2,
              key_scores_taken=2, routing_stored0=1, routing_stored1=1, output_product=9, gelu_done=2,
              routed=3, routing_taken=2, gate_applied=2)


def program(nc, x, pos, inv_freq, ident, edge, vecs, stream, peer_keys, peer_u, peer_v, out):
    route = nc.dram_tensor("route_dram", [NTB, P, NK, TB], F32, kind="Internal").ap()
    gelus = nc.dram_tensor("gelu_dram", [FILLED, P, SEQ], F32, kind="Internal").ap()
    ctx = ExitStack()
    with ctx:
        def sb(name, shape, dt=F32):
            return ctx.enter_context(nc.sbuf_tensor(name, shape, dt))

        X = sb("X", [P, TT, D])
        XH = sb("XH", [P, KD, SEQ], F32R)
        XL = sb("XL", [P, KD, SEQ], F32R)
        RAW = sb("RAW", [P, 2, 1024])
        RH = sb("RH", [P, 4, 1024], F32R)
        RL = sb("RL", [P, 4, 1024], F32R)
        IDN = sb("IDN", [P, P])
        IOTA = sb("IOTA", [P, P])
        IOTA4 = sb("IOTA4", [P, P, 4], BF16)
        ONES = sb("ONES", [P, 1])
        ROOT = sb("ROOT", [P, 1])
        EDGE = sb("EDGE", [P, GROUPS, 2, PAD])
        VEC = sb("VEC", [P, V_ALL])
        COS = sb("COS", [P, TT, HALF])
        SIN = sb("SIN", [P, TT, HALF])
        NRM = sb("NRM", [P, 3, TT])
        CN = sb("CN", [P, 3, 8])
        HGB = sb("HGB", [P, 2 * KD])
        GQS = sb("GQS", [P, 1])

        size = 116 * 1024
        sb("arena", [P, size // 4])
        start = nc.sbuf_base - size

        def at(name, offset, shape, dt=F32):
            n = 4
            for s in shape[1:]:
                n *= s
            assert offset + n <= size, name
            return nc.alloc_sbuf_tensor_at(name, shape, dt, offset=start + offset)

        K = 1024
        CH = at("CH", 0, [P, 5, SEQ], F32R)
        CL = at("CL", 10 * K, [P, 5, SEQ], F32R)
        SQT = at("SQT", 0, [P, TT * HEADS, QK])
        ROT = at("ROT", 12 * K, [P, 4, TT * HEADS * HALF])
        PR = at("PR", 0, [P, TT, SEQ])
        PT = at("PT", 8 * K, [P, TT, SEQ])
        XS = at("XS", 20 * K, [P, TT, D])
        SQX = at("SQX", 96 * K, [P, TT, D])
        MIXH = at("MIXH", 20 * K, [P, GROUPS, SEQ], F32R)
        MIXL = at("MIXL", 28 * K, [P, GROUPS, SEQ], F32R)
        O = at("O", 20 * K, [P, TT, SEQ])
        QH = at("QH", 28 * K, [P, SEQ], F32R)
        KH = at("KH", 30 * K, [P, SEQ], F32R)
        QL = at("QL", 16 * K, [P, SEQ], F32R)
        KL = at("KL", 18 * K, [P, SEQ], F32R)
        GATE = at("GATE", 36 * K, [P, 2, SEQ])
        QSL = at("QSL", 32 * K, [P, TT, QK])
        KSL = at("KSL", 32 * K + 1536, [P, TT, QK])
        SMALL = at("SMALL", 35 * K, [P, 256])
        RQ = SMALL[:, 0:32].rearrange("p (t h) -> p t h", t=TT)
        RK = SMALL[:, 32:64].rearrange("p (t h) -> p t h", t=TT)
        NMX = SMALL[:, 64:68]
        RSM = SMALL[:, 68:72]
        RIN = SMALL[:, 72:76]
        KPS = SMALL[:, 76:80]
        ROTC = at("ROTC", 52 * K, [P, 4, TT, HALF])
        PADDED = at("PADDED", 36 * K, [P, GROUPS, SEQ + 2 * PAD])
        WA = at("WA", 36 * K + 8448, [P, SEQ + 2 * PAD])
        WB = at("WB", 36 * K + 10560, [P, SEQ + 2 * PAD])
        KV = at("KV", 52 * K, [P, TT, D])
        YH = at("YH", 36 * K, [P, GROUPS, SEQ], F32R)
        YL = at("YL", 44 * K, [P, GROUPS, SEQ], F32R)
        OH = at("OH", 52 * K, [P, GROUPS, SEQ], F32R)
        OL = at("OL", 60 * K, [P, GROUPS, SEQ], F32R)
        SQC = at("SQC", 68 * K, [P, 5, SEQ])
        GAB = at("GAB", 68 * K, [P, 2 * KD, SEQ])
        Q = at("Q", 100 * K, [P, TT, HEADS, QK])
        T2 = at("T2", 100 * K, [P, 2, SEQ])
        KPE = at("KPE", 112 * K, [P, TT, ROPE])
        KPT = at("KPT", 114 * K, [P, SEQ])
        KEYS = at("KEYS", 0, [P, 2 * PH * NK])
        QF = at("QF", 8 * K, [P, 2, SEQ])
        SW = at("SW", 12 * K, [P, TT, NK])
        CAND = at("CAND", 14 * K, [P, TT, CANDS])
        CW = at("CW", 18 * K, [P, TT, CANDS])
        EQ = at("EQ", 22 * K, [P, TT, TOPK, TOPK])
        EQ2 = at("EQ2", 26 * K, [P, TT, TOPK, TOPK])
        V16 = at("V16", 30 * K, [P, TT, 2, TOPK])
        I16 = at("I16", 30 * K + 512, [P, TT, 2, TOPK], U32)
        F16 = at("F16", 31 * K, [P, TT, 2, TOPK])
        B16 = at("B16", 31 * K + 512, [P, TT, TOPK])
        J16 = at("J16", 31 * K + 768, [P, TT, TOPK], U32)
        JHL = at("JHL", 32 * K, [P, 2, TT, TOPK], U32)
        JF = at("JF", 32 * K + 512, [P, 2, TT, TOPK])
        J8 = at("J8", 42 * K, [P, TT, TOPK])
        BV = at("BV", 33 * K, [P, TT, P])
        GW = at("GW", 35 * K, [P, TT, P])
        BS = at("BS", 37 * K, [P, TT * PH])
        I1 = at("I1", 38 * K, [P, TT, P])
        I2 = at("I2", 40 * K, [P, TT, P])
        STAGE = [at(f"STAGE{s}", 32 * K * s, [P, NK, TB]) for s in range(2)]
        IT = at("IT", 64 * K, [P, 5, SEQ], BF16)
        REST = at("REST", 69 * K, [P, 2, SEQ])
        OA = at("OA", 73 * K, [P, 2, 2, P, 4], BF16)
        OE = at("OE", 77 * K, [P, 2, P, 4], BF16)
        OB = at("OB", 88 * K, [P, 2, 3, 2, P, 4], BF16)
        VRAW = at("VRAW", 0, [P, 2, D])
        VHI = at("VHI", 8 * K, [P, 4, D], F32R)
        VLO = at("VLO", 24 * K, [P, 4, D], F32R)
        GC = at("GC", 40 * K, [P, 2, NTB, 2, TB])
        GEL = at("GEL", 48 * K, [P, 2, SEQ])
        GS = at("GS", 80 * K, [P, 4, SEQ])
        GB = at("GB", 88 * K, [P, 2, 2, SEQ])
        WF = at("WF", 52 * K, [P, 2, SEQ])
        WHI = at("WHI", 56 * K, [P, 4, SEQ], F32R)
        WLO = at("WLO", 64 * K, [P, 4, SEQ], F32R)

        PS = ctx.enter_context(nc.psum_tensor("PS", [P, 8, 512], F32))

        sems = {n: ctx.enter_context(nc.semaphore(n)) for n in PER}
        passed = ctx.enter_context(nc.semaphore("passed"))
        mix_low = ctx.enter_context(nc.semaphore("mix_low"))
        const_in = ctx.enter_context(nc.semaphore("const_in"))
        x_loaded = ctx.enter_context(nc.semaphore("x_loaded"))
        iota_made = ctx.enter_context(nc.semaphore("iota_made"))
        trig_arg = ctx.enter_context(nc.semaphore("trig_arg"))
        trig_made = ctx.enter_context(nc.semaphore("trig_made"))
        stored = ctx.enter_context(nc.semaphore("stored"))
        S = type("Sems", (), sems)

        def count(layer, name, n):
            return layer * PER[name] + n + STARTS.get(name, 0)

        def apart(engine):
            engine.sem_inc(passed, 1)

        block = ctx.enter_context(nc.Block())

        @block.sync
        def _(sp):
            sp.dma_start(PADDED[:, 0, 0:TT].bitcast(I32), pos).then_inc(const_in, 16)
            sp.dma_start(COS[:, 0, :], inv_freq).then_inc(const_in, 16)
            sp.dma_start(IDN[:], ident).then_inc(const_in, 16)
            sp.dma_start(EDGE[:].rearrange("p g e c -> p (g e c)"), edge).then_inc(const_in, 16)
            sp.dma_start(X[:], x.rearrange("b (t p) d -> p (b t) d", p=P)).then_inc(x_loaded, 16)
            with sp.Fori(0, LAYERS) as l:

                def load_block(src, slot):
                    sp.dma_start(RAW[:, slot, :], src).then_inc(sems[f"block_loaded{slot}"], 16)

                sp.wait_ge(S.residual_added, count(l, "residual_added", 0))
                sp.dma_start(VEC[:], vecs[l]).then_inc(S.vectors_loaded, 16)
                with sp.Fori(0, J_WQ // 4) as i:
                    for k in range(4):
                        sp.wait_ge(S.low_part, count(l, "low_part", 4 * i + k - 1))
                        load_block(stream[l, 4 * i + k], k % 2)

                def load_query(n, q, slot):
                    sp.wait_ge(S.low_part, count(l, "low_part", n - 1))
                    load_block(stream[l, J_WQ + q], slot)

                def load_experts(n, c, slot):
                    sp.wait_ge(S.low_part, count(l, "low_part", n - 1))
                    load_block(peer_u[l, c], slot)

                def store_gelu(f, slot):
                    sp.wait_ge(S.gelu_done, count(l, "gelu_done", f + 1))
                    sp.dma_start(gelus[f], GS[:, slot, :]).then_inc(sems[f"gelu_stored{slot}"], 16)

                load_query(J_WQ, 0, 0)
                load_query(J_WQ + 1, 1, 1)
                sp.wait_ge(S.residual_added, count(l, "residual_added", 8))
                sp.dma_start(KEYS[:], peer_keys[l]).then_inc(S.keys_loaded, 16)
                for q in (2, 3):
                    n = 44 + 3 * q
                    load_query(n, q, n % 2)
                    for m in range(2):
                        load_experts(n + 1 + m, 2 * q - 4 + m, (n + 1 + m) % 2)

                def query_and_experts(i, k):
                    n = 44 + 12 * i + 3 * k
                    load_query(n, 4 * i + k, 3 * k % 2)
                    for m in range(2):
                        f = 8 * i + 2 * k + m - 4
                        load_experts(n + 1 + m, f, (3 * k + 1 + m) % 2)
                        store_gelu(f - 4, (2 * k + m) % 4)

                with sp.Fori(1, 3) as i:
                    for k in range(4):
                        query_and_experts(i, k)
                for k in range(2):
                    query_and_experts(3, k)
                for k in range(2):
                    load_query(J_U + 22 + k, 14 + k, k)
                for f in range(24, FIRST):
                    load_experts(J_U + f, f, f % 2)
                    store_gelu(f - 4, f % 4)

                def store_routing(b, s):
                    sp.wait_ge(S.routing_taken, count(l, "routing_taken", 16 * b + 16))
                    sp.dma_start(route[b], STAGE[s][:]).then_inc(sems[f"routing_stored{s}"], 16)

                for k in range(4):
                    load_experts(J_U + FIRST + k, FIRST + k, k % 2)
                    store_gelu(FIRST + k - 4, (FIRST + k) % 4)
                with sp.Fori(0, 3) as i:
                    for k in range(8):
                        f = FIRST + 4 + 8 * i + k
                        load_experts(J_U + f, f, k % 2)
                        store_gelu(f - 4, (FIRST + k) % 4)
                        if k % 4 == 3:
                            store_routing(2 * i + k // 4, k // 4)
                for f in range(FIRST + 28, FILLED):
                    load_experts(J_U + f, f, f % 2)
                    store_gelu(f - 4, f % 4)
                    if f == FIRST + 31:
                        store_routing(6, 0)
                for k in range(2):
                    load_experts(J_U + FILLED + k, FILLED + k, k)
                store_routing(7, 1)
                for k in range(2):
                    load_experts(J_U + FILLED + 2 + k, FILLED + 2 + k, k)
                for k in range(4):
                    store_gelu(60 + k, k)
                for s in range(2):
                    sp.wait_ge(sems[f"routing_stored{s}"], count(l, f"routing_stored{s}", 64))
                for s in range(4):
                    sp.wait_ge(sems[f"gelu_stored{s}"], count(l, f"gelu_stored{s}", 256))
                    apart(sp)

                def position(it, q, last=False):
                    pair, new = q // 2, q // 2 % 2
                    g = 2 * it + pair // 2
                    if q % 2 == 0:
                        sp.wait_ge(S.weighted, count(l, "weighted", 8 * it + q - 2))
                        sp.dma_start(
                            GC[:, new, :, :, :].rearrange("p b i t -> p b (i t)"),
                            route.rearrange("b p (g i) t -> p g b (i t)", i=2)[:, g + new * FILLED // 2],
                        ).then_inc(sems[f"routing_loaded{new}"], 16)
                        if not new:
                            sp.dma_start(GB[:, pair // 2, :, :],
                                         gelus.rearrange("(g i) p t -> p g i t", i=2)[:, g]).then_inc(
                                             sems[f"gelu_loaded{pair // 2}"], 16)
                    sp.wait_ge(S.v_low, count(l, "v_low", 8 * it + q - 1))
                    sp.dma_start(VRAW[:, q % 2, :],
                                 peer_v[l, :, 2 * g + new * FILLED + q % 2, :]).then_inc(sems[f"v_loaded{q % 2}"], 16)
                    if not new and not last:
                        c = FILLED + 4 * it + q // 2 + q % 2 + 4
                        load_experts(J_U + c, c, q % 2)

                with sp.Fori(0, 15) as it:
                    for q in range(8):
                        position(it, q)
                for q in range(8):
                    position(15, q, last=True)
            for t in range(TT):
                sp.wait_ge(S.residual_added, count(LAYERS, "residual_added", 2 * t + 2 - 8))
                sp.dma_start(out.rearrange("b (t p) d -> p (b t) d", p=P)[:, t], X[:, t, :]).then_inc(stored, 16)
            sp.wait_ge(stored, 16 * TT)

        @block.tensor
        def _(pe):
            pe.wait_ge(iota_made, 1)
            pe.wait_ge(const_in, 64)
            with pe.Fori(0, LAYERS) as l:

                def passes(acc, sh, sl, mh, ml, first, last):
                    pe.matmul(acc, sh, mh, start=first, stop=False)
                    pe.matmul(acc, sh, ml, start=False, stop=False)
                    return pe.matmul(acc, sl, mh, start=False, stop=last)

                def by_columns(bank, slot, ks=range(KD), norm=None):
                    for k in ks:
                        if norm is not None:
                            pe.wait_ge(S.norm_low, count(l, "norm_low", KD * norm + k + 1))
                        w = slice(k * P, (k + 1) * P)
                        m = passes(PS[:, bank, :], RH[:, slot, w], RL[:, slot, w], XH[:, k, :], XL[:, k, :],
                                   k == 0, k == KD - 1)
                    return m

                def transpose_norm(n):
                    pe.wait_ge(S.rows_normed, count(l, "rows_normed", 2 * n + 2))
                    for k in range(KD):
                        if k >= 4:
                            pe.wait_ge(S.norm_low, count(l, "norm_low", KD * n + k - 3))
                        for t in range(TT):
                            m = pe.transpose(PS[:, k % 4, t * P:(t + 1) * P], XS[:, t, k * P:(k + 1) * P], IDN[:])
                        m.then_inc(S.norm_transposed, 1)

                transpose_norm(0)
                for j in range(J_C, J_P):
                    if j >= 2:
                        pe.wait_ge(S.taken_by_dve, count(l, "taken_by_dve", j - 1))
                    pe.wait_ge(S.low_part, count(l, "low_part", j + 1))
                    by_columns(4 if j == 0 else 2 * (j % 2), j % 4, norm=0 if j == 0 else None).then_inc(S.block_used, 1)
                for j in range(J_P, J_KPE):
                    pe.wait_ge(S.taken_by_dve, count(l, "taken_by_dve", min(j - 1, 5)))
                    if j >= 7:
                        pe.wait_ge(S.taken_by_act, count(l, "taken_by_act", j - 6))
                    pe.wait_ge(S.low_part, count(l, "low_part", j + 1))
                    by_columns(2 * (j % 2), j % 4).then_inc(S.block_used, 1)
                pe.wait_ge(S.low_part, count(l, "low_part", J_KPE + 1))
                for k in range(KD):
                    s, w = J_KPE % 4, slice(k * ROPE, (k + 1) * ROPE)
                    m = passes(PS[0:ROPE, 4, :], RH[:, s, w], RL[:, s, w], XH[:, k, :], XL[:, k, :], k == 0, k == KD - 1)
                m.then_inc(S.block_used, 1)
                pe.wait_ge(S.latent_squared, count(l, "latent_squared", 5))
                for t in range(TT):
                    for col, js in ((t, range(QT_)), (4 + t, range(QT_, QT_ + KVT))):
                        for j in js:
                            m = pe.matmul(PS[:, 7, col:col + 1], SQC[:, j, t * P:(t + 1) * P], ONES[:],
                                          start=j == js[0], stop=j == js[-1])
                m.then_inc(S.latent_summed, 1)
                pe.wait_ge(S.kpe_taken, count(l, "kpe_taken", 1))
                apart(pe)
                for t in range(TT):
                    m = pe.transpose(PS[:, 5, t * ROPE:(t + 1) * ROPE], KPT[0:ROPE, t * P:(t + 1) * P], IDN[0:ROPE, 0:ROPE])
                m.then_inc(S.kpe_transposed, 1)
                pe.wait_ge(S.taken_by_act, count(l, "taken_by_act", 4))
                for k in range(QT_):
                    pe.wait_ge(S.low_part, count(l, "low_part", J_UQ + k + 1))
                    for t in range(TT):
                        if k == 0 and t == 2:
                            pe.wait_ge(S.taken_by_dve, count(l, "taken_by_dve", 6))
                        if k == 0 and t == 3:
                            pe.wait_ge(S.latent_variance, count(l, "latent_variance", 1))
                        tok, s = slice(t * P, (t + 1) * P), (J_UQ + k) % 4
                        for h in range(2):
                            w = slice(h * 384, (h + 1) * 384)
                            m = passes(PS[:, 2 * t + h, 0:384], CH[:, k, tok], CL[:, k, tok],
                                       RH[:, s, w], RL[:, s, w], k == 0, k == QT_ - 1)
                        if k == QT_ - 1:
                            m.then_inc(S.qkv_product, 1)
                    if k < QT_ - 1:
                        m.then_inc(S.block_used, 1)
                pe.wait_ge(S.qkv_product, count(l, "qkv_product", 4))
                pe.sem_inc(S.block_used, 1)
                pe.wait_ge(S.low_part, count(l, "low_part", J_UKV + 2))
                for t in range(TT):
                    pe.wait_ge(S.qkv_taken, count(l, "qkv_taken", t + 1))
                    tok = slice(t * P, (t + 1) * P)
                    for h in range(2):
                        for k in range(KVT):
                            w = slice(h * 512, (h + 1) * 512)
                            m = passes(PS[:, 2 * t + h, :], CH[:, QT_ + k, tok], CL[:, QT_ + k, tok],
                                       RH[:, (J_UKV + k) % 4, w], RL[:, (J_UKV + k) % 4, w], k == 0, k == KVT - 1)
                    m.then_inc(S.qkv_product, 1)
                pe.wait_ge(S.qkv_product, count(l, "qkv_product", 8))
                pe.sem_inc(S.block_used, KVT)
                pe.wait_ge(S.qkv_taken, count(l, "qkv_taken", 6))
                pe.wait_ge(S.window_means, count(l, "window_means", GROUPS))
                pe.wait_ge(S.low_part, count(l, "low_part", J_POOL + 1))
                for g in range(GROUPS):
                    w = slice(g * P, (g + 1) * P)
                    m = passes(PS[:, g, :], RH[:, J_POOL % 4, w], RL[:, J_POOL % 4, w],
                               MIXH[:, g, :], MIXL[:, g, :], True, True)
                    m.then_inc(S.pool_product, 1)
                pe.wait_ge(S.pool_product, count(l, "pool_product", GROUPS))
                pe.sem_inc(S.block_used, 1)
                pe.wait_ge(S.qkv_taken, count(l, "qkv_taken", 8))

                def two_tiles(j, mh, ml, bank):
                    for h in range(2):
                        for k in range(4):
                            if j == J_WPO and h == 0:
                                pe.wait_ge(S.pool_low, count(l, "pool_low", k + 1))
                            if j == J_WO and h == 0:
                                pe.wait_ge(S.attn_low, count(l, "attn_low", k + 1))
                            w = slice((h * 4 + k) * P, (h * 4 + k + 1) * P)
                            m = passes(PS[:, bank + 2 * (j % 2) + h, :], RH[:, j % 4, w], RL[:, j % 4, w],
                                       mh[:, k, :], ml[:, k, :], k == 0, k == 3)
                    m.then_inc(S.block_used, 1)

                for j in range(J_WPO, J_GATE):
                    if j >= J_WPO + 2:
                        pe.wait_ge(S.taken_by_act, count(l, "taken_by_act", 4 + j - J_WPO - 1))
                    pe.wait_ge(S.low_part, count(l, "low_part", j + 1))
                    two_tiles(j, YH, YL, 4)
                pe.wait_ge(S.taken_by_act, count(l, "taken_by_act", 8))
                apart(pe)

                with pe.Fori(0, HEADS // 2) as pair:
                    for a in range(2):
                        h = 2 * pair + a
                        gate = J_GATE + 4 * pair + 2 * a
                        pe.wait_ge(S.head_sliced, count(l, "head_sliced", h + 1))
                        for t in range(TT):
                            pe.transpose(PS[0:QK, 0, t * P:(t + 1) * P], QSL[:, t, :], IDN[:])
                        pe.wait_ge(S.taken_by_act, count(l, "taken_by_act", 8 + 2 * h))
                        for t in range(TT):
                            m = pe.transpose(PS[0:QK, 1, t * P:(t + 1) * P], KSL[:, t, :], IDN[:])
                        m.then_inc(S.head_transposed, 1)
                        pe.wait_ge(S.low_part, count(l, "low_part", gate + 1))
                        by_columns(6, 2 * a).then_inc(S.block_used, 1)
                        pe.wait_ge(S.head_high, count(l, "head_high", h + 1))
                        pe.wait_ge(S.head_low, count(l, "head_low", h + 1))
                        for t in range(TT):
                            tok = slice(t * P, (t + 1) * P)
                            if t == 3:
                                pe.wait_ge(S.head_stored, count(l, "head_stored", h))
                            passes(PS[:, 2 + t, :], QH[0:QK, tok], QL[0:QK, tok], KH[0:QK, :], KL[0:QK, :],
                                   True, True).then_inc(S.head_scores, 1)
                        pe.wait_ge(S.low_part, count(l, "low_part", gate + 2))
                        by_columns(1, 2 * a + 1, range(0, 3))
                        for t in range(TT):
                            by_columns(1, 2 * a + 1, range(3 + t, 4 + t))
                            pe.wait_ge(S.head_exp, count(l, "head_exp", 4 * h + t + 1))
                            if t == 1:
                                pe.wait_ge(S.taken_by_act, count(l, "taken_by_act", 8 + 2 * h + 1))
                            if t >= 2:
                                pe.wait_ge(S.probs_taken, count(l, "probs_taken", 4 * h + t - 1))
                            for k in range(TT):
                                m = pe.transpose(PS[:, 7 - t % 2, k * P:(k + 1) * P], PR[:, t, k * P:(k + 1) * P], IDN[:])
                            m.then_inc(S.probs_transposed, 1)
                        by_columns(1, 2 * a + 1, range(7, 8)).then_inc(S.block_used, 1)
                        pe.wait_ge(S.probs_taken, count(l, "probs_taken", 4 * h + 4))
                        for t in range(TT):
                            for k in range(TT):
                                m = pe.matmul(PS[:, 5, t * VH:(t + 1) * VH], PT[:, k, t * P:(t + 1) * P],
                                              KV[:, k, bass.ds(h * P + NOPE, VH)], start=k == 0, stop=k == TT - 1)
                        m.then_inc(S.head_output, 1)
                pe.wait_ge(S.head_stored, count(l, "head_stored", HEADS))
                for w in range(4):
                    for t in range(TT):
                        m = pe.transpose(PS[:, 4 + w, t * P:(t + 1) * P], O[:, t, w * P:(w + 1) * P], IDN[:])
                    m.then_inc(S.attn_transposed, 1)
                pe.wait_ge(S.taken_by_act, count(l, "taken_by_act", 24))
                for j in range(J_WO, J_WOUT):
                    if j >= J_WO + 2:
                        pe.wait_ge(S.taken_by_dve, count(l, "taken_by_dve", 7 + j - J_WO - 2))
                    pe.wait_ge(S.low_part, count(l, "low_part", j + 1))
                    two_tiles(j, OH, OL, 0)
                for j in range(J_WOUT, J_WQ):
                    h, kk = divmod(j - J_WOUT, 4)
                    if h == 0:
                        pe.wait_ge(S.mix_high, count(l, "mix_high", 2 * kk + 2))
                        pe.wait_ge(mix_low, l * 8 + 2 * kk + 2)
                    if h == 1 and kk == 0:
                        pe.wait_ge(S.taken_by_dve, count(l, "taken_by_dve", 10))
                    pe.wait_ge(S.low_part, count(l, "low_part", j + 1))
                    for t in range(TT):
                        for i in range(2):
                            k, w, tok = 2 * kk + i, slice(i * 512, (i + 1) * 512), slice(t * P, (t + 1) * P)
                            m = passes(PS[:, 4 - 4 * h + t, :], XH[:, k, tok], XL[:, k, tok],
                                       RH[:, j % 4, w], RL[:, j % 4, w], k == 0, k == KD - 1)
                        if kk == 3:
                            m.then_inc(S.projected, 1)
                    if kk < 3:
                        m.then_inc(S.block_used, 1)
                    else:
                        pe.wait_ge(S.projected, count(l, "projected", 4 * h + 4))
                        pe.sem_inc(S.block_used, 1)

                pe.wait_ge(S.residual_added, count(l, "residual_added", 8))
                transpose_norm(1)
                pe.wait_ge(S.keys_loaded, count(l, "keys_loaded", 16))

                def fill(f, n, slot, bank, ks=range(KD)):
                    if ks[0] == 0:
                        pe.wait_ge(S.gelu_done, count(l, "gelu_done", f - 1))
                        pe.wait_ge(S.low_part, count(l, "low_part", n + 1))
                    m = by_columns(bank, slot, ks)
                    if ks[-1] == KD - 1:
                        m.then_inc(S.block_used, 1)

                def query(n, k, block, slot, fills, norm=None):
                    pe.wait_ge(S.low_part, count(l, "low_part", block + 1))
                    by_columns(2 * (k % 2) if norm is None else 6, slot, norm=norm).then_inc(S.block_used, 1)
                    for a in fills[:1]:
                        fill(*a)
                    pe.wait_ge(S.taken_by_act, count(l, "taken_by_act", 24 + n + 1))
                    pe.wait_ge(S.key_scores_taken, count(l, "key_scores_taken", n - 1))
                    for t in range(TT):
                        m = pe.matmul(PS[:, 4 + k % 2, t * P:(t + 1) * P], QF[:, k % 2, t * P:(t + 1) * P],
                                      KEYS[:, bass.ds(n * NK, NK)], start=True, stop=True)
                    m.then_inc(S.key_scores, 1)
                    for a in fills[1:]:
                        fill(*a)

                for q in range(4):
                    n = J_WQ + q if q < 2 else 44 + 3 * q
                    fills = [(2 * q - 4 + m, n + 1 + m, (n + 1 + m) % 4, 6 + m) for m in range(2)]
                    query(q, q, n, n % 4, fills if q >= 2 else [], norm=1 if q == 0 else None)

                def query_and_experts(i, k):
                    n = 44 + 12 * i + 3 * k
                    query(4 * i + k, k, n, 3 * k % 4,
                          [(8 * i + 2 * k + m - 4, n + 1 + m, (3 * k + 1 + m) % 4, 6 + m) for m in range(2)])

                with pe.Fori(1, 3) as i:
                    for k in range(4):
                        query_and_experts(i, k)
                for k in range(2):
                    query_and_experts(3, k)
                for k in range(2, 4):
                    query(12 + k, k, J_U + 20 + k, k, [])
                for f in range(24, FIRST - 1):
                    fill(f, J_U + f, f % 4, 6 + f % 2)
                pe.wait_ge(S.choice_ready, count(l, "choice_ready", 1))
                for n, src in enumerate((I1, I2, GW)):
                    for t in range(TT):
                        m = pe.transpose(PS[:, n, t * P:(t + 1) * P], src[:, t, :], IDN[:])
                    m.then_inc(S.choice_transposed, 1)
                fill(FIRST - 1, J_U + FIRST - 1, (FIRST - 1) % 4, 6 + (FIRST - 1) % 2)
                with pe.Fori(0, 8) as i:
                    for k in range(4):
                        f = FIRST + 4 * i + k
                        for s in range(4):
                            n = 16 * i + 4 * k + s
                            pe.wait_ge(S.onehots_ready, count(l, "onehots_ready", 8 * i + 2 * k + s // 2 + 1))
                            pe.wait_ge(S.routing_taken, count(l, "routing_taken", n - 1))
                            for t in range(4):
                                for p in range(3):
                                    m = pe.matmul(PS[:, 4 + s % 2, t * P:(t + 1) * P], OA[:, s // 2, s % 2, :, t],
                                                  OB[:, s // 2, p, s % 2, :, t], start=p == 0, stop=p == 2)
                            m.then_inc(S.routed, 1)
                            fill(f, J_U + f, (FIRST + k) % 4, 6 + k % 2, range(2 * s, 2 * s + 2))
                for f in range(FIRST + 32, FILLED):
                    fill(f, J_U + f, f % 4, 6 + f % 2)

                def hidden(it, m):
                    c = FILLED + 4 * it + m
                    pe.wait_ge(S.gelu_done, count(l, "gelu_done", c - 3))
                    pe.wait_ge(S.low_part, count(l, "low_part", J_U + c + 1))
                    by_columns(m, m).then_inc(S.block_used, 1)

                def output(it, pair):
                    g = 4 * it + pair
                    pe.wait_ge(S.weighted_low, count(l, "weighted_low", 2 * g + 2))
                    pe.wait_ge(S.v_low, count(l, "v_low", 2 * g + 2))
                    for o in range(8):
                        t, h = divmod(o, 2)
                        pe.wait_ge(S.residual_added, count(l, "residual_added", 8 + 8 * g + o - 3))
                        for i in range(2):
                            s, tok, w = 2 * (pair % 2) + i, slice(t * P, (t + 1) * P), slice(h * 512, (h + 1) * 512)
                            m = passes(PS[:, 4 + o % 4, :], WHI[:, s, tok], WLO[:, s, tok],
                                       VHI[:, s, w], VLO[:, s, w], i == 0, i == 1)
                        m.then_inc(S.output_product, 1)

                for m in range(4):
                    hidden(0, m)
                pe.wait_ge(S.routing_taken, count(l, "routing_taken", 128))
                pe.wait_ge(S.gelu_done, count(l, "gelu_done", FILLED))
                apart(pe)
                with pe.Fori(0, 15) as it:
                    for half in range(2):
                        output(it, 2 * half)
                        output(it, 2 * half + 1)
                        hidden(it + 1, 2 * half)
                        hidden(it + 1, 2 * half + 1)
                for pair in range(4):
                    output(15, pair)

        @block.scalar
        def _(act):
            act.wait_ge(const_in, 64)
            act.wait_ge(trig_arg, 1)
            act.activation(SIN[:], ROTC[:, 0], ACT.Sin)
            act.activation(COS[:], ROTC[:, 1], ACT.Sin).then_inc(trig_made, 1)
            act.wait_ge(x_loaded, 16)
            with act.Fori(0, LAYERS) as l:

                def hi(i, j):
                    n = 4 * i + j
                    act.wait_ge(sems[f"block_loaded{j % 2}"], 16 * (l * (JOBS // 2) + 2 * i + j // 2 + 1))
                    act.wait_ge(S.block_used, count(l, "block_used", n - 3))
                    act.activation(RH[:, j % 4, :], RAW[:, j % 2, :], ACT.Copy).then_inc(S.high_part, 1)

                def norm(n):
                    act.activation(ROOT[:], ONES[:], ACT.Sqrt)
                    for t in range(TT):
                        act.wait_ge(S.residual_added, count(l, "residual_added", 2 * t - 6 if n == 0 else t + 5))
                        m = act.activation(SQX[:, t, :], X[:, t, :], ACT.Square, accum_out=NRM[:, 0, t:t + 1])
                    m.then_inc(S.squares_summed, 1)
                    act.wait_ge(S.variance_inverted, count(l, "variance_inverted", n + 1))
                    act.activation(NRM[:, 2, :], NRM[:, 1, :], ACT.Sqrt).then_inc(S.rms_ready, 1)
                    act.wait_ge(S.rms_ready, count(l, "rms_ready", n + 1))
                    act.activation(XS[:, TT - 1, :], X[:, TT - 1, :], ACT.Copy,
                                   scale=NRM[:, 2, TT - 1:TT]).then_inc(S.rows_normed, 1)

                def split_norm(n, gain):
                    for k in range(KD):
                        act.wait_ge(S.norm_transposed, count(l, "norm_transposed", KD * n + k + 1))
                        act.activation(XH[:, k, :], PS[:, k % 4, :], ACT.Copy,
                                       scale=VEC[:, gain + k:gain + k + 1]).then_inc(S.norm_high, 1)

                norm(0)
                act.wait_ge(S.vectors_loaded, count(l, "vectors_loaded", 16))
                hi(0, 0)
                hi(0, 1)
                split_norm(0, V_N1)
                for j in range(J_C, J_P):
                    hi(0, j + 2)
                    act.wait_ge(S.block_used, count(l, "block_used", j + 1))
                    bank = 4 if j == 0 else 2 * (j % 2)
                    act.activation(CH[:, j, :], PS[:, bank, :], ACT.Copy,
                                   scale=VEC[:, V_QG + j:V_QG + j + 1])
                    act.activation(SQC[:, j, :], PS[:, bank, :], ACT.Square).then_inc(S.latent_squared, 1)
                for j in range(J_P, J_KPE):
                    hi(0, j + 2)
                    act.wait_ge(S.block_used, count(l, "block_used", j + 1))
                    act.activation(PADDED[:, j - J_P, PAD:PAD + SEQ], PS[:, 2 * (j % 2), :],
                                   ACT.Copy).then_inc(S.taken_by_act, 1)
                for j in (11, 12, 13):
                    hi(0, j)
                act.wait_ge(S.block_used, count(l, "block_used", J_KPE + 1))
                act.activation(KPT[0:ROPE, :], PS[0:ROPE, 4, :], ACT.Copy).then_inc(S.kpe_taken, 1)
                act.wait_ge(S.latent_variance, count(l, "latent_variance", 1))
                act.activation(CN[:, 2, :], CN[:, 1, :], ACT.Sqrt).then_inc(S.latent_rms, 1)
                act.wait_ge(S.latent_rms, count(l, "latent_rms", 1))
                hi(0, 14)
                for t in range(TT):
                    act.wait_ge(S.qkv_product, count(l, "qkv_product", t + 1))
                    act.activation(Q[:, t].rearrange("p (x h) e -> p x (h e)", x=2),
                                   PS[:, 2 * t:2 * t + 2, 0:384], ACT.Copy,
                                   scale=CN[:, 2, t:t + 1]).then_inc(S.qkv_taken, 1)
                for j in (15, 16):
                    hi(0, j)
                for t in range(TT):
                    act.wait_ge(S.qkv_product, count(l, "qkv_product", t + 5))
                    act.activation(KV[:, t, :].rearrange("p (x e) -> p x e", x=2),
                                   PS[:, 2 * t:2 * t + 2, :], ACT.Copy,
                                   scale=CN[:, 2, 4 + t:5 + t]).then_inc(S.qkv_taken, 1)
                hi(0, J_POOL + 2)
                for g in range(GROUPS):
                    act.wait_ge(S.pool_product, count(l, "pool_product", g + 1))
                    act.activation(YH[:, g, :], PS[:, g, :], ACT.Copy,
                                   scale=VEC[:, V_PS + g:V_PS + g + 1]).then_inc(S.pool_high, 1)
                for j in range(J_WPO, J_GATE):
                    hi(0, j + 2)
                    if j == J_GATE - 1:
                        act.wait_ge(S.heads_variance, count(l, "heads_variance", 1))
                        act.activation(SMALL[:, 0:64], SMALL[:, 128:192], ACT.Sqrt).then_inc(S.heads_rms, 1)
                    act.wait_ge(S.block_used, count(l, "block_used", j + 1))
                    n = KD + 2 * (j - J_WPO)
                    act.activation(GAB[:, n:n + 2, :], PS[:, 4 + 2 * (j % 2):6 + 2 * (j % 2), :],
                                   ACT.Copy).then_inc(S.taken_by_act, 1)
                with act.Fori(0, HEADS // 2) as pair:
                    for a in range(2):
                        h = 2 * pair + a

                        def gate(m):
                            hi(pair, J_GATE + 2 * a + m + 2)
                            act.wait_ge(S.block_used, count(l, "block_used", J_GATE + 2 * h + m + 1))
                            act.wait_ge(S.gate_applied, count(l, "gate_applied", 2 * h + m - 1))
                            act.activation(GATE[:, m, :], PS[:, 6 - 5 * m, :], ACT.Tanh, scale=0.5,
                                           bias=HGB[:, bass.ds(2 * h + m, 1)]).then_inc(S.taken_by_act, 1)

                        act.wait_ge(S.head_transposed, count(l, "head_transposed", h + 1))
                        act.activation(QH[0:QK, :], PS[0:QK, 0, :], ACT.Copy, scale=GQS[0:QK, :])
                        act.activation(KH[0:QK, :], PS[0:QK, 1, :], ACT.Copy,
                                       scale=VEC[0:QK, V_KH:V_KH + 1]).then_inc(S.head_high, 1)
                        gate(0)
                        for t in range(TT):
                            act.wait_ge(S.head_max, count(l, "head_max", 4 * h + t + 1))
                            act.activation(PR[:, t, :], PS[:, 2 + t, :], ACT.Exp, bias=NMX[:, t:t + 1],
                                           accum_out=RSM[:, t:t + 1]).then_inc(S.head_exp, 1)
                        gate(1)
                for w in range(4):
                    act.wait_ge(S.attn_transposed, count(l, "attn_transposed", w + 1))
                    act.activation(OH[:, w, :], PS[:, 4 + w, :], ACT.Copy).then_inc(S.attn_high, 1)
                for j in range(J_WO, J_WOUT):
                    hi(0, j + 2)
                    for m in range(2):
                        n = 2 * (j - J_WO) + m
                        act.wait_ge(S.mix_full, count(l, "mix_full", n + 1))
                        act.activation(XH[:, n, :], T2[:, n % 2, :], ACT.Copy).then_inc(S.mix_high, 1)
                for j in range(J_WOUT, J_WQ):
                    hi(0, j + 2)
                norm(1)
                split_norm(1, V_N2)

                def take_query(n, k, block, bank):
                    act.wait_ge(S.block_used, count(l, "block_used", block + 1))
                    act.wait_ge(S.key_scores, count(l, "key_scores", n - 1))
                    act.activation(QF[:, k % 2, :], PS[:, bank, :], ACT.Copy).then_inc(S.taken_by_act, 1)

                def fill_gelu(f, n, turn, slot):
                    act.wait_ge(S.block_used, count(l, "block_used", n + 1))
                    if not isinstance(f, int) or f >= 4:
                        act.wait_ge(sems[f"gelu_stored{slot}"], count(l, f"gelu_stored{slot}", 16 * turn))
                    act.activation(GS[:, slot, :], PS[:, 6 + slot % 2, :], ACT.Gelu_apprx_tanh).then_inc(S.gelu_done, 1)

                for q in range(4):
                    n = J_WQ + q if q < 2 else 44 + 3 * q
                    hi(0, n + 2)
                    take_query(q, q, n, 6 if q == 0 else 2 * (q % 2))
                    if q >= 2:
                        for m in range(2):
                            hi(0, n + 3 + m)
                            f = 2 * q - 4 + m
                            fill_gelu(f, n + 1 + m, 0, f)

                def query_and_experts(i, k):
                    j = 44 + 3 * k
                    hi(3 * i, j + 2)
                    take_query(4 * i + k, k, 12 * i + j, 2 * (k % 2))
                    for m in range(2):
                        hi(3 * i, j + 3 + m)
                        u = 2 * k + m
                        fill_gelu(8 * i + u - 4, 12 * i + j + 1 + m, 2 * i - 1 + u // 4, u % 4)

                with act.Fori(1, 3) as i:
                    for k in range(4):
                        query_and_experts(i, k)
                for k in range(2):
                    query_and_experts(3, k)
                for k in range(2, 4):
                    hi(0, J_U + 22 + k)
                    take_query(12 + k, k, J_U + 20 + k, 2 * (k % 2))
                for f in range(24, FIRST):
                    if f == FIRST - 2:
                        act.wait_ge(S.best_shifted, count(l, "best_shifted", PH))
                        act.activation(GW[:], BV[:], ACT.Exp).then_inc(S.best_exp, 1)
                    hi(0, J_U + f + 2)
                    fill_gelu(f, J_U + f, f // 4, f % 4)
                with act.Fori(0, NTB // 2) as b:
                    for k in range(8):
                        hi(2 * b, J_U + FIRST + k + 2)
                        if k % 4 == 0:
                            s = k // 4
                            act.wait_ge(sems[f"routing_stored{s}"], count(l, f"routing_stored{s}", 16 * b))
                        for n in range(4):
                            act.wait_ge(S.routed, count(l, "routed", 32 * b + 4 * k + n + 1))
                            tok = 16 * (k % 4) + 4 * n
                            act.activation(STAGE[s][:, :, tok:tok + 4], PS[:, 4 + n % 2, :].rearrange("p (t i) -> p i t", t=4),
                                           ACT.Copy).then_inc(S.routing_taken, 1)
                        f = FIRST + k
                        fill_gelu(8 * b + f, J_U + 8 * b + f, 2 * b + f // 4, f % 4)
                for f in range(FIRST + 32, FILLED):
                    hi(0, J_U + f + 2)
                    fill_gelu(f, J_U + f, f // 4, f % 4)

                def position(it, q, last=False):
                    n, new, m = 8 * it + q, q // 2 % 2, 2 * (q // 4) + q % 2
                    act.wait_ge(sems[f"v_loaded{q % 2}"], 16 * (l * 64 + 4 * it + q // 2 + 1))
                    act.wait_ge(S.output_product, count(l, "output_product", 8 * (4 * it + q // 2) - 8))
                    act.activation(VHI[:, q % 4, :], VRAW[:, q % 2, :], ACT.Copy).then_inc(S.v_high, 1)
                    if new:
                        act.wait_ge(S.block_used, count(l, "block_used", J_U + FILLED + 4 * it + m + 1))
                        act.wait_ge(S.weighted, count(l, "weighted", n - 3))
                        act.activation(GEL[:, q % 2, :], PS[:, m, :], ACT.Gelu_apprx_tanh).then_inc(S.gelu_done, 1)
                        if not last:
                            hi(it + 1, J_U + FILLED + m)
                    act.wait_ge(S.weighted, count(l, "weighted", n + 1))
                    act.activation(WHI[:, q % 4, :], WF[:, q % 2, :], ACT.Copy).then_inc(S.weighted_high, 1)

                hi(0, J_U + FILLED + 2)
                hi(0, J_U + FILLED + 3)
                with act.Fori(0, 15) as it:
                    for q in range(8):
                        position(it, q)
                for q in range(8):
                    position(15, q, last=True)

        @block.vector
        def _(dve):
            dve.memset(ONES[:], 1.0)
            dve.wait_ge(iota_made, 1)
            dve.tensor_copy(IOTA4[:], IOTA[:].unsqueeze(2).to_broadcast([P, P, 4]))
            dve.wait_ge(const_in, 64)
            POSF, ANG, TURN = WA[:, 0:TT], ROTC[:, 2], ROTC[:, 3]
            dve.tensor_copy(POSF, PADDED[:, 0, 0:TT].bitcast(I32))
            dve.drain()
            dve.tensor_tensor(ANG, COS[:, 0, :].unsqueeze(1).to_broadcast([P, TT, HALF]),
                              POSF.unsqueeze(2).to_broadcast([P, TT, HALF]), ALU.mult)
            dve.drain()
            magic = 1.5 * 2.0 ** 23
            dve.tensor_scalar(TURN, ANG, 1 / (2 * np.pi), magic, ALU.mult, ALU.add)
            dve.drain()
            dve.tensor_scalar(TURN, TURN, -magic, None, ALU.add)
            dve.drain()
            c1 = 6.28125
            c2 = float(np.float32(np.round((2 * np.pi - c1) * 2.0 ** 21) / 2.0 ** 21))
            c3 = 2 * np.pi - c1 - c2
            for c in (c1, c2, c3):
                dve.scalar_tensor_tensor(ANG, TURN, -c, ANG, ALU.mult, ALU.add)
                dve.drain()
            top = float(np.float32(3.1415925))
            dve.tensor_scalar(ROTC[:, 0], ANG, top, -top, ALU.min, ALU.max)
            dve.tensor_scalar(ROTC[:, 1], ANG, np.pi / 2, None, ALU.add)
            dve.drain()
            dve.tensor_scalar(TURN, ROTC[:, 1], top, -2 * np.pi, ALU.is_gt, ALU.mult)
            dve.drain()
            dve.tensor_tensor(ROTC[:, 1], ROTC[:, 1], TURN, ALU.add)
            dve.drain()
            dve.tensor_scalar(ROTC[:, 1], ROTC[:, 1], top, -top, ALU.min, ALU.max).then_inc(trig_arg, 1)
            dve.wait_ge(trig_made, 1)
            dve.wait_ge(x_loaded, 16)
            dve.drain()
            with dve.Fori(0, LAYERS) as l:

                def norm(n):
                    dve.wait_ge(S.squares_summed, count(l, "squares_summed", n + 1))
                    dve.tensor_scalar(NRM[:, 0, :], NRM[:, 0, :], 1.0 / D, EPS, ALU.mult, ALU.add)
                    dve.drain()
                    dve.reciprocal(NRM[:, 1, :], NRM[:, 0, :]).then_inc(S.variance_inverted, 1)
                    dve.wait_ge(S.rms_ready, count(l, "rms_ready", n + 1))
                    for t in range(TT - 1):
                        m = dve.tensor_scalar(XS[:, t, :], X[:, t, :], NRM[:, 2, t:t + 1], None, ALU.mult)
                    m.then_inc(S.rows_normed, 1)

                def split_norm(n, gain):
                    for k in range(KD):
                        dve.wait_ge(S.norm_high, count(l, "norm_high", KD * n + k + 1))
                        dve.scalar_tensor_tensor(XL[:, k, :], PS[:, k % 4, :], VEC[:, gain + k:gain + k + 1],
                                                 XH[:, k, :].bitcast(F32), ALU.mult, ALU.subtract).then_inc(S.norm_low, 1)

                norm(0)
                dve.wait_ge(S.vectors_loaded, count(l, "vectors_loaded", 16))
                apart(dve)
                dve.tensor_scalar(GQS[:], VEC[:, V_QH:V_QH + 1], QK ** -0.5, None, ALU.mult)
                dve.tensor_scalar(HGB[:], VEC[:, V_GB:V_GB + 2 * KD], 0.5, None, ALU.mult)
                split_norm(0, V_N1)
                for g in range(GROUPS):
                    dve.memset(PADDED[:, g, 0:PAD], 0.0)
                    m = dve.memset(PADDED[:, g, PAD + SEQ:], 0.0)
                dve.drain()
                for j in range(J_C, J_P):
                    dve.wait_ge(S.latent_squared, count(l, "latent_squared", j + 1))
                    dve.scalar_tensor_tensor(CL[:, j, :], PS[:, 4 if j == 0 else 2 * (j % 2), :], VEC[:, V_QG + j:V_QG + j + 1],
                                             CH[:, j, :].bitcast(F32), ALU.mult, ALU.subtract).then_inc(S.taken_by_dve, 1)
                def window_means(g):
                    src, now, other = PADDED[:, g, :], WA, WB
                    dve.wait_ge(S.taken_by_act, count(l, "taken_by_act", g + 1))
                    dve.tensor_tensor(now[:, 1:528], src[:, 1:528], src[:, 0:527], ALU.add)
                    dve.drain()
                    first, end = 1, 528
                    for step in range(g):
                        d = 2 ** step
                        first, end = first + d, end - d
                        dve.tensor_tensor(other[:, first:end], now[:, first - d:end - d], now[:, first + d:end + d], ALU.add)
                        dve.drain()
                        now, other = other, now
                    dve.tensor_tensor(now[:, PAD:2 * PAD], now[:, PAD:2 * PAD], EDGE[:, g, 0, :], ALU.mult)
                    dve.tensor_tensor(now[:, SEQ:SEQ + PAD], now[:, SEQ:SEQ + PAD], EDGE[:, g, 1, :], ALU.mult)
                    dve.drain()
                    dve.scalar_tensor_tensor(other[:, 0:SEQ], now[:, PAD:PAD + SEQ], 0.5 ** (g + 1),
                                             src[:, PAD:PAD + SEQ], ALU.mult, ALU.subtract)
                    dve.drain()
                    dve.tensor_copy(MIXH[:, g, :], other[:, 0:SEQ])
                    dve.drain()
                    dve.tensor_tensor(MIXL[:, g, :], other[:, 0:SEQ], MIXH[:, g, :].bitcast(F32),
                                      ALU.subtract).then_inc(S.window_means, 1)
                    dve.drain()

                for g in range(GROUPS - 1):
                    window_means(g)
                dve.wait_ge(S.latent_summed, count(l, "latent_summed", 1))
                dve.tensor_scalar(CN[:, 0, 0:4], PS[:, 7, 0:4], 1.0 / Q_LORA, EPS, ALU.mult, ALU.add)
                dve.tensor_scalar(CN[:, 0, 4:8], PS[:, 7, 4:8], 1.0 / KV_LORA, EPS, ALU.mult, ALU.add)
                dve.drain()
                dve.reciprocal(CN[:, 1, :], CN[:, 0, :]).then_inc(S.latent_variance, 1)
                dve.wait_ge(S.kpe_transposed, count(l, "kpe_transposed", 1))
                dve.tensor_copy(KPE[:].rearrange("p t e -> p (t e)"), PS[:, 5, 0:TT * ROPE]).then_inc(S.taken_by_dve, 1)
                window_means(GROUPS - 1)
                for g in range(GROUPS):
                    dve.wait_ge(S.pool_high, count(l, "pool_high", g + 1))
                    dve.scalar_tensor_tensor(YL[:, g, :], PS[:, g, :], VEC[:, V_PS + g:V_PS + g + 1],
                                             YH[:, g, :].bitcast(F32), ALU.mult, ALU.subtract).then_inc(S.pool_low, 1)
                dve.wait_ge(S.qkv_taken, count(l, "qkv_taken", 8))
                cosq = COS[:].unsqueeze(2).to_broadcast([P, TT, HEADS, HALF])
                sinq = SIN[:].unsqueeze(2).to_broadcast([P, TT, HEADS, HALF])

                def rotate(x1, x2, cos, sin, r):
                    dve.tensor_tensor(r[0], x1, cos, ALU.mult)
                    dve.tensor_tensor(r[1], x2, sin, ALU.mult)
                    dve.tensor_tensor(r[2], x1, sin, ALU.mult)
                    dve.tensor_tensor(r[3], x2, cos, ALU.mult)
                    dve.drain()
                    dve.tensor_tensor(x1, r[0], r[1], ALU.subtract)
                    dve.tensor_tensor(x2, r[2], r[3], ALU.add)
                    dve.drain()

                rotate(Q[:, :, :, NOPE:NOPE + HALF], Q[:, :, :, NOPE + HALF:QK], cosq, sinq,
                       [ROT[:, n, :].rearrange("p (t h e) -> p t h e", t=TT, h=HEADS) for n in range(4)])
                rotate(KPE[:, :, 0:HALF], KPE[:, :, HALF:ROPE], COS[:], SIN[:],
                       [ROT[:, n, 0:TT * HALF].rearrange("p (t e) -> p t e", t=TT) for n in range(4)])
                qv = Q[:].rearrange("p t h e -> p (t h) e")
                kn = KV[:].rearrange("p t (h e) -> p (t h) e", h=HEADS)[:, :, 0:NOPE]
                dve.tensor_tensor(SQT[:], qv, qv, ALU.mult)
                dve.drain()
                dve.tensor_reduce(SMALL[:, 128:160], SQT[:], AX, ALU.add)
                dve.drain()
                dve.tensor_tensor(SQT[:, :, 0:NOPE], kn, kn, ALU.mult)
                dve.tensor_tensor(ROT[:, 0, 0:TT * ROPE].rearrange("p (t e) -> p t e", t=TT), KPE[:], KPE[:], ALU.mult)
                dve.drain()
                dve.tensor_reduce(SMALL[:, 160:192], SQT[:, :, 0:NOPE], AX, ALU.add)
                dve.tensor_reduce(KPS, ROT[:, 0, 0:TT * ROPE].rearrange("p (t e) -> p t e", t=TT), AX, ALU.add)
                dve.drain()
                sk = SMALL[:, 160:192].rearrange("p (t h) -> p t h", t=TT)
                dve.tensor_tensor(sk, sk, KPS.unsqueeze(2).to_broadcast([P, TT, HEADS]), ALU.add)
                dve.drain()
                dve.tensor_scalar(SMALL[:, 128:192], SMALL[:, 128:192], 1.0 / QK, EPS, ALU.mult, ALU.add)
                dve.drain()
                dve.reciprocal(SMALL[:, 128:192], SMALL[:, 128:192]).then_inc(S.heads_variance, 1)
                dve.wait_ge(S.heads_rms, count(l, "heads_rms", 1))
                apart(dve)

                def slice_head(h):
                    def head_scale(r, n):
                        return r[:, :, bass.ds(h, 1)].to_broadcast([P, TT, n])

                    dve.tensor_tensor(QSL[:], Q[:, :, bass.ds(h, 1), :].rearrange("p t o e -> p (t o) e"),
                                      head_scale(RQ, QK), ALU.mult)
                    dve.tensor_tensor(KSL[:, :, 0:NOPE], KV[:, :, bass.ds(h * P, NOPE)], head_scale(RK, NOPE), ALU.mult)
                    dve.tensor_tensor(KSL[:, :, NOPE:QK], KPE[:], head_scale(RK, ROPE), ALU.mult).then_inc(S.head_sliced, 1)

                def head(h, last=False):
                    dve.wait_ge(S.head_high, count(l, "head_high", h + 1))
                    dve.scalar_tensor_tensor(QL[0:QK, :], PS[0:QK, 0, :], GQS[0:QK, :], QH[0:QK, :].bitcast(F32),
                                             ALU.mult, ALU.subtract)
                    dve.scalar_tensor_tensor(KL[0:QK, :], PS[0:QK, 1, :], VEC[0:QK, V_KH:V_KH + 1],
                                             KH[0:QK, :].bitcast(F32), ALU.mult, ALU.subtract).then_inc(S.head_low, 1)
                    if not last:
                        slice_head(h + 1)
                    for t in range(TT):
                        dve.wait_ge(S.head_scores, count(l, "head_scores", 4 * h + t + 1))
                        dve.tensor_reduce(NMX[:, t:t + 1], PS[:, 2 + t, :], AX, ALU.max, negate=True).then_inc(S.head_max, 1)
                    for t in range(TT):
                        dve.wait_ge(S.probs_transposed, count(l, "probs_transposed", 4 * h + t + 1))
                        dve.tensor_copy(PT[:, :, t * P:(t + 1) * P],
                                        PS[:, 7 - t % 2, :].rearrange("p (k q) -> p k q", k=TT)).then_inc(S.probs_taken, 1)
                    dve.wait_ge(S.head_exp, count(l, "head_exp", 4 * h + 4))
                    dve.reciprocal(RIN, RSM)
                    dve.drain()
                    dve.wait_ge(S.head_output, count(l, "head_output", h + 1))
                    dve.tensor_tensor(O[:, :, bass.ds(h * VH, VH)],
                                      PS[:, 5, 0:TT * VH].rearrange("p (t e) -> p t e", t=TT),
                                      RIN.unsqueeze(2).to_broadcast([P, TT, VH]), ALU.mult).then_inc(S.head_stored, 1)
                    dve.drain()

                slice_head(0)
                with dve.Fori(0, HEADS // 2 - 1) as pair:
                    head(2 * pair)
                    head(2 * pair + 1)
                head(HEADS - 2)
                head(HEADS - 1, last=True)
                for w in range(4):
                    dve.wait_ge(S.attn_high, count(l, "attn_high", w + 1))
                    dve.tensor_tensor(OL[:, w, :], PS[:, 4 + w, :], OH[:, w, :].bitcast(F32), ALU.subtract).then_inc(S.attn_low, 1)
                dve.wait_ge(S.gate_applied, count(l, "gate_applied", 2 * KD))
                for j in range(J_WO, J_WOUT):
                    dve.wait_ge(S.block_used, count(l, "block_used", j + 1))
                    for m in range(2):
                        n = 2 * (j - J_WO) + m
                        dve.tensor_tensor(T2[:, m, :], PS[:, 2 * (j % 2) + m, :], GAB[:, n, :], ALU.mult)
                        dve.drain()
                        dve.tensor_tensor(T2[:, m, :], T2[:, m, :], GAB[:, KD + n, :], ALU.add).then_inc(S.mix_full, 1)
                        dve.wait_ge(S.mix_high, count(l, "mix_high", n + 1))
                        dve.tensor_tensor(XL[:, n, :], T2[:, m, :], XH[:, n, :].bitcast(F32), ALU.subtract).then_inc(mix_low, 1)
                    dve.drain()
                    dve.engine_nop().then_inc(S.taken_by_dve, 1)
                for j in range(J_WOUT, J_WQ):
                    h, kk = divmod(j - J_WOUT, 4)
                    if kk == 3:
                        for t in range(TT):
                            w = slice(h * 512, (h + 1) * 512)
                            dve.wait_ge(S.projected, count(l, "projected", 4 * h + t + 1))
                            dve.tensor_tensor(X[:, t, w], PS[:, 4 - 4 * h + t, :], X[:, t, w], ALU.add).then_inc(S.residual_added, 1)
                norm(1)
                split_norm(1, V_N2)

                def best16(n, vals, idx, src, work):
                    for t in range(TT):
                        dve.max(vals(t)[:, 0:8], src(t))
                    dve.drain()
                    for t in range(TT):
                        dve.max_index(idx(t)[:, 0:8], vals(t)[:, 0:8], src(t))
                        m = dve.match_replace(work(t), vals(t)[:, 0:8], src(t), -3.0e38)
                    dve.drain()
                    for t in range(TT):
                        dve.max(vals(t)[:, 8:16], work(t))
                    dve.drain()
                    for t in range(TT):
                        dve.max_index(idx(t)[:, 8:16], vals(t)[:, 8:16], work(t))
                    return m

                with dve.Fori(0, 4) as i:
                    for head in range(2):
                        for half in range(2):
                            k = 2 * head + half
                            dve.wait_ge(S.key_scores, count(l, "key_scores", 4 * i + k + 1))
                            apart(dve)
                            best16(0, lambda t: V16[:, t, half, :], lambda t: I16[:, t, half, :],
                                   lambda t: PS[:, 4 + k % 2, t * P:(t + 1) * P], lambda t: SW[:, t, :])
                            dve.drain()
                            dve.engine_nop().then_inc(S.key_scores_taken, 1)
                        dve.tensor_tensor(CAND[:, :, 0:TOPK], V16[:, :, 1, :],
                                          V16[:, :, 0, 0:1].to_broadcast([P, TT, TOPK]), ALU.add)
                        dve.tensor_tensor(CAND[:, :, TOPK:].rearrange("p t (a b) -> p t a b", b=8),
                                          V16[:, :, 0, 1:].unsqueeze(3).to_broadcast([P, TT, TOPK - 1, 8]),
                                          V16[:, :, 1, 0:8].unsqueeze(2).to_broadcast([P, TT, TOPK - 1, 8]), ALU.add)
                        dve.tensor_copy(F16[:], I16[:])
                        dve.drain()
                        best16(0, lambda t: B16[:, t, :], lambda t: J16[:, t, :], lambda t: CAND[:, t, :],
                               lambda t: CW[:, t, :])
                        dve.drain()
                        dve.tensor_scalar(JHL[:, 0], J16[:], 3, None, ALU.logical_shift_right)
                        dve.tensor_scalar(JHL[:, 1], J16[:], 7, None, ALU.bitwise_and)
                        dve.drain()
                        dve.tensor_copy(JF[:], JHL[:])
                        dve.tensor_tensor(BV[:, :, bass.ds((2 * i + head) * TOPK, TOPK)], B16[:],
                                          B16[:, :, 0:1].to_broadcast([P, TT, TOPK]), ALU.subtract).then_inc(S.best_shifted, 1)
                        dve.drain()
                        dve.tensor_scalar(J8[:], JF[:, 0], 1.0, 8.0, ALU.is_equal, ALU.mult)
                        dve.drain()
                        dve.tensor_tensor(JF[:, 1], JF[:, 1], J8[:], ALU.add)
                        dve.tensor_scalar(JF[:, 0], JF[:, 0], -1.0, 0.0, ALU.add, ALU.max)
                        dve.drain()
                        ramp = IOTA[:, 0:TOPK].unsqueeze(1).to_broadcast([P, TOPK, TOPK])
                        for half, (e, dst) in enumerate(((EQ, I1), (EQ2, I2))):
                            for t in range(TT):
                                dve.tensor_tensor(e[:, t], JF[:, half, t, :].unsqueeze(2).to_broadcast([P, TOPK, TOPK]),
                                                  ramp, ALU.is_equal)
                        dve.drain()
                        for half, e in enumerate((EQ, EQ2)):
                            dve.tensor_tensor(e[:], e[:], F16[:, :, half, :].unsqueeze(2).to_broadcast([P, TT, TOPK, TOPK]),
                                              ALU.mult)
                        dve.drain()
                        for e, dst in ((EQ, I1), (EQ2, I2)):
                            dve.tensor_reduce(dst[:, :, bass.ds((2 * i + head) * TOPK, TOPK)], e[:], AX, ALU.add)
                        dve.drain()
                gw = GW[:].rearrange("p t (h k) -> p (t h) k", k=TOPK)
                dve.wait_ge(S.best_exp, count(l, "best_exp", 1))
                dve.tensor_reduce(BS[:], gw, AX, ALU.add)
                dve.drain()
                dve.reciprocal(BS[:], BS[:])
                dve.drain()
                dve.tensor_tensor(gw, gw, BS[:].unsqueeze(2).to_broadcast([P, TT * PH, TOPK]),
                                  ALU.mult).then_inc(S.choice_ready, 1)
                for n in range(3):
                    dve.wait_ge(S.choice_transposed, count(l, "choice_transposed", n + 1))
                    dve.tensor_copy(IT[:, n, :] if n < 2 else REST[:, 0, :], PS[:, n, :])
                dve.drain()
                for p in range(3):
                    dve.tensor_copy(IT[:, 2 + p, :], REST[:, p % 2, :])
                    dve.drain()
                    if p < 2:
                        dve.tensor_tensor(REST[:, (p + 1) % 2, :], REST[:, p % 2, :], IT[:, 2 + p, :], ALU.subtract)
                        dve.drain()

                with dve.Fori(0, SEQ // 16) as i:
                    for slot in range(2):
                        n = 2 * i + slot

                        def of_tokens(row):
                            return IT[:, row, bass.ds(8 * n, 8)].rearrange("p (g t) -> p g t", g=2).unsqueeze(
                                2).to_broadcast([P, 2, P, 4])

                        numbers = IOTA4[:].unsqueeze(1).to_broadcast([P, 2, P, 4])
                        dve.wait_ge(S.routed, count(l, "routed", 2 * n - 2))
                        dve.tensor_tensor(OA[:, slot], numbers, of_tokens(0), ALU.is_equal)
                        dve.tensor_tensor(OE[:], numbers, of_tokens(1), ALU.is_equal)
                        dve.drain()
                        for p in range(3):
                            m = dve.tensor_tensor(OB[:, slot, p], OE[:], of_tokens(2 + p), ALU.mult)
                        m.then_inc(S.onehots_ready, 1)
                        dve.drain()

                def add_outputs(g, first):
                    for o in range(first, first + 4):
                        t, h = divmod(o, 2)
                        w = slice(h * 512, (h + 1) * 512)
                        dve.wait_ge(S.output_product, count(l, "output_product", 8 * g + o + 1))
                        dve.tensor_tensor(X[:, t, w], PS[:, 4 + o % 4, :], X[:, t, w], ALU.add).then_inc(S.residual_added, 1)

                def position(it, q, first=False):
                    n, new = 8 * it + q, q // 2 % 2
                    if new:
                        gelu = GEL[:, q % 2, :]
                        dve.wait_ge(S.gelu_done, count(l, "gelu_done", FILLED + 4 * it + 2 * (q // 4) + q % 2 + 1))
                    else:
                        gelu = GB[:, q // 4, q % 2, :]
                        dve.wait_ge(sems[f"gelu_loaded{q // 4}"], count(l, f"gelu_loaded{q // 4}", 16 * it + 16))
                    dve.wait_ge(sems[f"routing_loaded{new}"], 16 * (l * 32 + 2 * it + q // 4 + 1))
                    dve.tensor_tensor(WF[:, q % 2, :].rearrange("p (b t) -> p b t", b=NTB),
                                      gelu.rearrange("p (b t) -> p b t", b=NTB),
                                      GC[:, new, :, q % 2, :], ALU.mult).then_inc(S.weighted, 1)
                    dve.wait_ge(S.v_high, count(l, "v_high", n + 1))
                    dve.tensor_tensor(VLO[:, q % 4, :], VRAW[:, q % 2, :], VHI[:, q % 4, :].bitcast(F32),
                                      ALU.subtract).then_inc(S.v_low, 1)
                    dve.wait_ge(S.weighted_high, count(l, "weighted_high", n + 1))
                    dve.tensor_tensor(WLO[:, q % 4, :], WF[:, q % 2, :], WHI[:, q % 4, :].bitcast(F32),
                                      ALU.subtract).then_inc(S.weighted_low, 1)
                    if not (first and q < 2):
                        add_outputs(4 * it + q // 2 - 1, 4 * (q % 2))
                    dve.drain()

                for q in range(8):
                    position(0, q, first=True)
                with dve.Fori(1, 16) as it:
                    for q in range(8):
                        position(it, q)
                add_outputs(63, 0)
                add_outputs(63, 4)
                dve.drain()

        @block.gpsimd
        def _(pool):
            for name, value in STARTS.items():
                pool.sem_inc(sems[name], value)
            pool.iota(IOTA[:], [[1, P]], base=0, channel_multiplier=0,
                      allow_small_or_imprecise_dtypes=True).then_inc(iota_made, 1)
            with pool.Fori(0, LAYERS) as l:
                def low(i, k):
                    pool.wait_ge(S.high_part, count(l, "high_part", 4 * i + k + 1))
                    pool.tensor_tensor(RL[:, k % 4, :], RAW[:, k % 2, :], RH[:, k % 4, :].bitcast(F32),
                                       ALU.subtract).then_inc(S.low_part, 1)

                with pool.Fori(0, J_GATE // 4) as i:
                    for k in range(4):
                        low(i, k)
                low(0, J_GATE)
                low(0, J_GATE + 1)
                pool.wait_ge(S.latent_summed, count(l, "latent_summed", 1))
                apart(pool)
                pool.memset(GAB[:, 0:KD, :], 1.0)
                pool.drain()
                with pool.Fori(0, 4) as i:
                    for k in range(4):
                        low(i, J_GATE + k + 2)
                        n = 4 * i + k
                        pool.wait_ge(S.taken_by_act, count(l, "taken_by_act", 8 + n + 1))
                        gab = GAB[:, bass.ds(n, 1), :].rearrange("p o t -> p (o t)")
                        apart(pool)
                        pool.tensor_scalar(GATE[:, k % 2, :], GATE[:, k % 2, :], 0.5, 0.5, ALU.mult, ALU.add)
                        pool.drain()
                        pool.tensor_tensor(gab, gab, GATE[:, k % 2, :], ALU.mult).then_inc(S.gate_applied, 1)
                low(0, J_WO + 2)
                low(0, J_WO + 3)
                with pool.Fori(J_WO // 4 + 1, JOBS // 4) as i:
                    for k in range(4):
                        low(i, k)


def laid_out(x, positions, norm1_g, w_in, q_lora_g, kv_lora_g, w_uq, w_ukv, q_head_g, k_head_g,
             w_o_mla, pool_w, pool_scale, w_pool_out, gate_bias, w_out, norm2_g,
             peer_wq, peer_keys, peer_u, peer_v):
    f = np.float32
    L = LAYERS
    stream = np.zeros((L, J_U, P, 1024), f)

    def cols(w, a, b):
        return w[:, :, a:b].reshape(L, KD, P, (b - a) // P, P).transpose(0, 3, 2, 1, 4).reshape(L, -1, P, D)

    p0 = Q_LORA + KV_LORA + ROPE
    stream[:, J_C:J_P] = cols(w_in, 0, Q_LORA + KV_LORA)
    stream[:, J_P:J_KPE] = cols(w_in, p0, p0 + 512)
    kpe = w_in[:, :, Q_LORA + KV_LORA:p0].reshape(L, KD, P, ROPE)
    stream[:, J_KPE, :, :KD * ROPE] = kpe.transpose(0, 2, 1, 3).reshape(L, P, -1)
    stream[:, J_POOL, :, :512] = pool_w.transpose(0, 2, 1, 3).reshape(L, P, 512)
    stream[:, J_GATE:J_WO] = cols(w_in, p0 + 512, p0 + 512 + 2 * D)
    tiles = lambda w: w.reshape(L, 4, P, 4, 2, P).transpose(0, 3, 2, 4, 1, 5).reshape(L, 4, P, D)
    stream[:, J_WPO:J_GATE] = tiles(w_pool_out)
    stream[:, J_UQ:J_UKV, :, :768] = w_uq.reshape(L, QT_, P, 768)
    stream[:, J_UKV:J_POOL] = w_ukv.reshape(L, KVT, P, D)
    stream[:, J_WO:J_WOUT] = tiles(w_o_mla)
    stream[:, J_WOUT:J_WQ] = w_out.reshape(L, 4, 2, P, 2, 512).transpose(0, 4, 1, 3, 2, 5).reshape(L, 8, P, D)
    stream[:, J_WQ:J_U] = cols(peer_wq, 0, 2048)
    vecs = np.zeros((L, P, V_ALL), f)
    for at, a in ((V_N1, norm1_g), (V_N2, norm2_g), (V_QG, q_lora_g), (V_KVG, kv_lora_g), (V_PS, pool_scale),
                  (V_GB, gate_bias.reshape(L, -1))):
        a = a.reshape(L, -1, P).transpose(0, 2, 1)
        vecs[:, :, at:at + a.shape[2]] = a
    vecs[:, :QK, V_QH] = q_head_g
    vecs[:, :QK, V_KH] = k_head_g
    edge = np.ones((GROUPS, 2, PAD), f)
    for g in range(GROUPS):
        h = 2 ** g
        for c in range(PAD):
            edge[g, 0, c] = 2 * h / min(c + h, 2 * h)
            edge[g, 1, c] = 2 * h / min(PAD - c + h, 2 * h)
    inv = (10000.0 ** (-np.arange(0, ROPE, 2, dtype=np.float64) / ROPE)).astype(f)
    return {
        "x": x,
        "pos": np.ascontiguousarray(positions.reshape(TT, P).T),
        "inv_freq": np.tile(inv, (P, 1)),
        "ident": np.eye(P, dtype=f),
        "edge": np.tile(edge.reshape(1, -1), (P, 1)),
        "vecs": vecs,
        "stream": stream,
        "peer_keys": np.ascontiguousarray(peer_keys.transpose(0, 4, 1, 2, 3).reshape(L, P, -1)),
        "peer_u": peer_u.reshape(L, NK, NK, KD, P).transpose(0, 2, 4, 3, 1).reshape(L, NK, P, D),
        "peer_v": peer_v.reshape(L, NK, NK, D),
    }


def kernel(**inputs):
    import concourse.bacc as bacc
    from concourse.bass_utils import run_bass_kernel_spmd

    arrays = laid_out(**{n: np.asarray(a) for n, a in inputs.items()})
    nc = bacc.Bacc("TRN2", target_bir_lowering=False, num_devices=1)
    aps = {n: nc.dram_tensor(f"in_{n}", a.shape, mybir.dt.from_np(a.dtype), kind="ExternalInput").ap()
           for n, a in arrays.items()}
    out = nc.dram_tensor("out", (1, SEQ, D), F32, kind="ExternalOutput").ap()
    program(nc, out=out, **aps)
    r = run_bass_kernel_spmd(nc, [{f"in_{n}": a for n, a in arrays.items()}], core_ids=[0])
    return r.results[0]["out"]
```
